# Optimizing a Trainium2 kernel written in Bass

```python
import math
import jax
import jax.numpy as jnp
from jax import lax
import numpy as np
import jax, jax.numpy as jnp

D_MODEL = 1024
BATCH = 1
SEQ = 512
DEPTH = 1

N_MIXERS = 2
HEAD_DIM = 64
MIX_WIDTH = 3 * D_MODEL // 4
MEM_WIDTH = D_MODEL - MIX_WIDTH
MEM_HEADS = 4
MEM_HEAD_DIM = MEM_WIDTH // MEM_HEADS
MEM_TOKENS = 256
RWKV_HEADS = MIX_WIDTH // HEAD_DIM
DECAY_LORA = 64
ICLR_LORA = 64
GATE_LORA = 128
RWKV_COLS = 3 * MIX_WIDTH + DECAY_LORA + ICLR_LORA + GATE_LORA
RWKV_IN = RWKV_COLS + MEM_WIDTH
DIFF_HEADS = MIX_WIDTH // (2 * HEAD_DIM)
DIFF_IN = 3 * MIX_WIDTH + MEM_WIDTH
D_FF = 4 * D_MODEL
N_RWKV_LAYERS = (DEPTH + N_MIXERS - 1) // N_MIXERS
N_DIFF_LAYERS = DEPTH // N_MIXERS
Q_BLOCK = 128
RMS_EPS = 1e-6
GN_EPS = 64e-5


def rms_norm(x, g=None):
    xf = x.astype(jnp.float32)
    y = xf * lax.rsqrt(jnp.mean(jnp.square(xf), axis=-1, keepdims=True) + RMS_EPS)
    if g is not None:
        y = y * g.astype(jnp.float32)
    return y.astype(x.dtype)

def token_shift(z, mu):
    z_prev = jnp.pad(z[:, :-1], ((0, 0), (1, 0), (0, 0)))
    return z + (z_prev - z) * mu

def delta_rule_scan(r, w, k, v, a, b):
    B, T, H, N = r.shape
    xs = tuple(jnp.moveaxis(z.astype(jnp.float32), 1, 0) for z in (r, w, k, v, a, b))

    def step(S, inp):
        r_t, w_t, k_t, v_t, a_t, b_t = inp
        sa = jnp.einsum('bhvk,bhk->bhv', S, a_t)
        S = (S * w_t[:, :, None, :] + sa[..., None] * b_t[:, :, None, :]
             + v_t[..., None] * k_t[:, :, None, :])
        return S, jnp.einsum('bhvk,bhk->bhv', S, r_t)

    S0 = jnp.zeros((B, H, N, N), jnp.float32)
    _, y = lax.scan(step, S0, xs)
    return jnp.moveaxis(y, 0, 1)

def rwkv7_time_mix(h, w_in, mu, w0, w2, a0, a2, g2, k_k, k_a, r_k, lnx_g, lnx_b):
    B, T, _ = h.shape
    H, N = RWKV_HEADS, HEAD_DIM
    proj = h @ w_in
    slab = token_shift(proj[..., :RWKV_COLS], mu)
    q_mem = proj[..., RWKV_COLS:]
    c3 = 3 * MIX_WIDTH
    r, k, v, wd, ad, gd = jnp.split(
        slab, [MIX_WIDTH, 2 * MIX_WIDTH, c3, c3 + DECAY_LORA, c3 + DECAY_LORA + ICLR_LORA], axis=-1)
    log_w = -jax.nn.softplus(-(w0 + jnp.tanh(wd) @ w2)) - 0.5
    decay = jnp.exp(-jnp.exp(log_w.astype(jnp.float32)))
    a = jax.nn.sigmoid(a0 + ad @ a2)
    g = jax.nn.sigmoid(gd) @ g2

    def heads(z):
        return z.reshape(B, T, H, N)

    kk = heads(k * k_k).astype(jnp.float32)
    kk = kk / jnp.maximum(jnp.sqrt(jnp.sum(jnp.square(kk), axis=-1, keepdims=True)), 1e-12)
    k = k * (1.0 + (a - 1.0) * k_a)
    a_h = heads(a).astype(jnp.float32)
    r_h, k_h, v_h = heads(r), heads(k), heads(v)
    y = delta_rule_scan(r_h, heads(decay), k_h, v_h, -kk, kk * a_h)
    mean = jnp.mean(y, axis=-1, keepdims=True)
    var = jnp.mean(jnp.square(y - mean), axis=-1, keepdims=True)
    y = ((y - mean) * lax.rsqrt(var + GN_EPS)).reshape(B, T, MIX_WIDTH)
    y = (y * lnx_g.astype(jnp.float32) + lnx_b.astype(jnp.float32)).astype(h.dtype)
    bonus = (jnp.sum(r_h * k_h * r_k, axis=-1, keepdims=True) * v_h).reshape(B, T, MIX_WIDTH)
    return (y + bonus) * g, q_mem

def alibi_slopes(n):
    return jnp.exp2(-8.0 * jnp.arange(1, n + 1, dtype=jnp.float32) / n)

def causal_diff_attention(q, k, v, lam, slopes):
    B, T, H, _, d = q.shape
    nb = T // Q_BLOCK
    qb = jnp.moveaxis(q.reshape(B, nb, Q_BLOCK, H, 2, d), 1, 0)
    starts = jnp.arange(nb, dtype=jnp.int32) * Q_BLOCK
    k_pos = jnp.arange(T, dtype=jnp.int32)
    scale = d ** -0.5

    def block(args):
        q_blk, start = args
        q_pos = start + jnp.arange(Q_BLOCK, dtype=jnp.int32)
        dist = q_pos[:, None] - k_pos[None, :]
        bias = -slopes[:, None, None] * dist.astype(jnp.float32)[None]
        s = jnp.einsum('bqhcd,bkhcd->bhcqk', q_blk, k).astype(jnp.float32) * scale
        s = jnp.where(dist >= 0, s + bias[None, :, None], -jnp.inf)
        p = jax.nn.softmax(s, axis=-1)
        p = p[:, :, 0] - lam * p[:, :, 1]
        return jnp.einsum('bhqk,bkhe->bqhe', p.astype(v.dtype), v)

    out = lax.map(block, (qb, starts))
    return jnp.moveaxis(out, 0, 1).reshape(B, T, H, 2 * d)

def diff_lambda_init(layer):
    return 0.8 - 0.6 * math.exp(-0.3 * layer)

def diff_attention_mixer(h, w_in, q_g, k_g, lq1, lk1, lq2, lk2, subln_g, lambda_init):
    B, T, _ = h.shape
    H, d = DIFF_HEADS, HEAD_DIM
    proj = h @ w_in
    q = rms_norm(proj[..., :MIX_WIDTH].reshape(B, T, H, 2, d), q_g)
    k = rms_norm(proj[..., MIX_WIDTH:2 * MIX_WIDTH].reshape(B, T, H, 2, d), k_g)
    v = proj[..., 2 * MIX_WIDTH:3 * MIX_WIDTH].reshape(B, T, H, 2 * d)
    q_mem = proj[..., 3 * MIX_WIDTH:]
    lam = (jnp.exp(jnp.sum(lq1 * lk1).astype(jnp.float32))
           - jnp.exp(jnp.sum(lq2 * lk2).astype(jnp.float32)) + lambda_init)
    o = causal_diff_attention(q, k, v, lam, alibi_slopes(H))
    o = rms_norm(o, subln_g) * (1.0 - lambda_init)
    return o.reshape(B, T, MIX_WIDTH), q_mem

def memory_cross_attention(q_mem, k_mem, v_mem, q_g, k_g):
    B, T, _ = q_mem.shape
    q = rms_norm(q_mem.reshape(B, T, MEM_HEADS, MEM_HEAD_DIM), q_g)
    k = k_mem * k_g
    s = jnp.einsum('bthd,bmhd->bhtm', q, k).astype(jnp.float32) * MEM_HEAD_DIM ** -0.5
    p = jax.nn.softmax(s, axis=-1).astype(v_mem.dtype)
    return jnp.einsum('bhtm,bmhd->bthd', p, v_mem).reshape(B, T, MEM_WIDTH)

def first_inputs(seed: int = 0) -> dict:
    key = jax.random.key(seed)
    keys = jax.random.split(key, 40)
    counter = [0]

    def next_key():
        counter[0] += 1
        return keys[counter[0] - 1]

    def nrm(shape, scale):
        return jax.random.normal(next_key(), shape, jnp.float32) * scale

    def gain(shape):
        return 1.0 + nrm(shape, 0.05)

    def unif(shape, lo, hi):
        return jax.random.uniform(next_key(), shape, jnp.float32, lo, hi)

    NR, ND = N_RWKV_LAYERS, N_DIFF_LAYERS
    return {
        "x": nrm((BATCH, SEQ, D_MODEL), 1.0),
        "mem": nrm((BATCH, MEM_TOKENS, D_MODEL), 1.0),
        "norm_mix_g": gain((DEPTH, D_MODEL)),
        "norm_ffn_g": gain((DEPTH, D_MODEL)),
        "w_out": nrm((DEPTH, D_MODEL, D_MODEL), D_MODEL ** -0.5),
        "w_ff1": nrm((DEPTH, D_MODEL, D_FF), D_MODEL ** -0.5),
        "w_ff2": nrm((DEPTH, D_FF, D_MODEL), D_FF ** -0.5),
        "mem_norm_g": gain((D_MODEL,)),
        "w_mem_kv": nrm((D_MODEL, 2 * MEM_WIDTH), D_MODEL ** -0.5),
        "mem_q_norm_g": gain((DEPTH, MEM_HEAD_DIM)),
        "mem_k_norm_g": gain((DEPTH, MEM_HEAD_DIM)),
        "rw_in": nrm((NR, D_MODEL, RWKV_IN), D_MODEL ** -0.5),
        "rw_mu": unif((NR, RWKV_COLS), 0.0, 1.0),
        "rw_w0": unif((NR, MIX_WIDTH), -6.0, -1.0),
        "rw_w2": nrm((NR, DECAY_LORA, MIX_WIDTH), 0.5 * DECAY_LORA ** -0.5),
        "rw_a0": nrm((NR, MIX_WIDTH), 0.1),
        "rw_a2": nrm((NR, ICLR_LORA, MIX_WIDTH), ICLR_LORA ** -0.5),
        "rw_g2": nrm((NR, GATE_LORA, MIX_WIDTH), GATE_LORA ** -0.5),
        "rw_k_k": 0.85 + nrm((NR, MIX_WIDTH), 0.05),
        "rw_k_a": gain((NR, MIX_WIDTH)),
        "rw_r_k": nrm((NR, RWKV_HEADS, HEAD_DIM), 0.1),
        "rw_lnx_g": gain((NR, MIX_WIDTH)),
        "rw_lnx_b": nrm((NR, MIX_WIDTH), 0.01),
        "df_in": nrm((ND, D_MODEL, DIFF_IN), D_MODEL ** -0.5),
        "df_q_norm_g": gain((ND, 2, HEAD_DIM)),
        "df_k_norm_g": gain((ND, 2, HEAD_DIM)),
        "df_lq1": nrm((ND, HEAD_DIM), 0.1),
        "df_lk1": nrm((ND, HEAD_DIM), 0.1),
        "df_lq2": nrm((ND, HEAD_DIM), 0.1),
        "df_lk2": nrm((ND, HEAD_DIM), 0.1),
        "df_subln_g": gain((ND, 2 * HEAD_DIM)),
    }

def first_block(x, mem, norm_mix_g, norm_ffn_g, w_out, w_ff1, w_ff2, mem_norm_g, w_mem_kv,
              mem_q_norm_g, mem_k_norm_g, rw_in, rw_mu, rw_w0, rw_w2, rw_a0, rw_a2, rw_g2,
              rw_k_k, rw_k_a, rw_r_k, rw_lnx_g, rw_lnx_b, df_in, df_q_norm_g, df_k_norm_g,
              df_lq1, df_lk1, df_lq2, df_lk2, df_subln_g):
    B, M, _ = mem.shape
    kv = rms_norm(mem, mem_norm_g) @ w_mem_kv
    k_mem = rms_norm(kv[..., :MEM_WIDTH].reshape(B, M, MEM_HEADS, MEM_HEAD_DIM))
    v_mem = kv[..., MEM_WIDTH:].reshape(B, M, MEM_HEADS, MEM_HEAD_DIM)

    for layer in range(DEPTH):
        j = layer // N_MIXERS
        h = rms_norm(x, norm_mix_g[layer])
        if layer % N_MIXERS == 0:
            mix, q_mem = rwkv7_time_mix(h, rw_in[j], rw_mu[j], rw_w0[j], rw_w2[j], rw_a0[j],
                                        rw_a2[j], rw_g2[j], rw_k_k[j], rw_k_a[j], rw_r_k[j],
                                        rw_lnx_g[j], rw_lnx_b[j])
        else:
            mix, q_mem = diff_attention_mixer(h, df_in[j], df_q_norm_g[j], df_k_norm_g[j],
                                              df_lq1[j], df_lk1[j], df_lq2[j], df_lk2[j],
                                              df_subln_g[j], diff_lambda_init(layer))
        mem_out = memory_cross_attention(q_mem, k_mem, v_mem, mem_q_norm_g[layer],
                                         mem_k_norm_g[layer])
        x = x + jnp.concatenate([mix, mem_out], axis=-1) @ w_out[layer]
        u = rms_norm(x, norm_ffn_g[layer]) @ w_ff1[layer]
        x = x + jnp.square(jax.nn.relu(u)) @ w_ff2[layer]
    return x


DEPTH_2 = 2

FOX_HEADS = 8
NSA_HEADS = 8
NSA_KV_GROUPS = 2
NSA_GROUP_SIZE = NSA_HEADS // NSA_KV_GROUPS
CMP_BLOCK = 32
CMP_STRIDE = 16
SLC_BLOCK = 64
N_SELECT = 16
WINDOW = 512
POOL_WINDOWS = (2, 4, 8, 16)
POOL_GROUP = D_MODEL // len(POOL_WINDOWS)
FFN_HIDDEN = -(-8 * D_MODEL // (3 * 256)) * 256
NEG_INF = -1e30
BIG = 1e30
N_EVEN = (DEPTH_2 + 1) // 2
N_ODD = DEPTH_2 // 2
MIX_WIDTH_2 = (FOX_HEADS + NSA_HEADS) * HEAD_DIM
KV_DIM = NSA_KV_GROUPS * HEAD_DIM
IN_SIZES = (FOX_HEADS * HEAD_DIM, FOX_HEADS * HEAD_DIM, FOX_HEADS * HEAD_DIM, FOX_HEADS,
            NSA_HEADS * HEAD_DIM, KV_DIM, KV_DIM, KV_DIM, KV_DIM, KV_DIM, KV_DIM, 3 * NSA_HEADS)
IN_COLS = sum(IN_SIZES)


def rmsnorm(x, g):
    xf = x.astype(jnp.float32)
    y = xf * lax.rsqrt(jnp.mean(xf * xf, axis=-1, keepdims=True) + RMS_EPS)
    return (y * g.astype(jnp.float32)).astype(x.dtype)

def masked_softmax(s, mask):
    s = jnp.where(mask, s, NEG_INF)
    m = jnp.max(s, axis=-1, keepdims=True)
    e = jnp.where(mask, jnp.exp(s - m), 0.0)
    return e / jnp.maximum(jnp.sum(e, axis=-1, keepdims=True), 1e-30)

def alibi_slopes_2(n):
    return jnp.asarray(2.0 ** (-8.0 * (np.arange(n, dtype=np.float32) + 1.0) / n), dtype=jnp.float32)

def fox_attention(q, k, v, log_f):
    B, S, H, dh = q.shape
    c = jnp.transpose(jnp.cumsum(log_f, axis=1), (0, 2, 1))
    kpos = jnp.arange(S)
    scale = dh ** -0.5

    def block(qb):
        start = qb * Q_BLOCK
        t = start + jnp.arange(Q_BLOCK)
        qi = lax.dynamic_slice_in_dim(q, start, Q_BLOCK, axis=1)
        ci = lax.dynamic_slice_in_dim(c, start, Q_BLOCK, axis=2)
        s = jnp.einsum('bqhd,bkhd->bhqk', qi, k).astype(jnp.float32) * scale
        s = s + ci[..., None] - c[:, :, None, :]
        mask = kpos[None, :] <= t[:, None]
        p = masked_softmax(s, mask)
        return jnp.einsum('bhqk,bkhd->bqhd', p.astype(v.dtype), v)

    out = lax.map(block, jnp.arange(S // Q_BLOCK))
    return jnp.transpose(out, (1, 0, 2, 3, 4)).reshape(B, S, H * dh)

def nsa_compress(tok, pe, w1, w2):
    B, S, G, dh = tok.shape
    r = CMP_BLOCK // CMP_STRIDE
    n_chunks = S // CMP_STRIDE
    n_c = n_chunks - r + 1
    chunks = tok.reshape(B, n_chunks, CMP_STRIDE, G, dh)
    blocks = jnp.concatenate([chunks[:, j:j + n_c] for j in range(r)], axis=2)
    blocks = blocks + pe[None, None, :, None, :]
    flat = jnp.transpose(blocks, (0, 1, 3, 2, 4)).reshape(B, n_c, G, CMP_BLOCK * dh)
    return jax.nn.gelu(flat @ w1) @ w2

def nsa_attention(q, k_c, v_c, k_s, v_s, k_w, v_w, gates, pe, w1, w2):
    B, S, H, dh = q.shape
    G = k_c.shape[2]
    R = H // G
    scale = dh ** -0.5
    slopes = alibi_slopes_2(H).reshape(G, R)
    dt = q.dtype
    r = CMP_BLOCK // CMP_STRIDE
    ratio = SLC_BLOCK // CMP_STRIDE
    n_s = S // SLC_BLOCK
    n_sel = min(N_SELECT, n_s)

    kc = nsa_compress(k_c, pe[0], w1[0], w2[0])
    vc = nsa_compress(v_c, pe[1], w1[1], w2[1])
    n_c = kc.shape[1]
    cmp_end = jnp.arange(n_c) * CMP_STRIDE + CMP_BLOCK - 1

    q_g = q.reshape(B, S, G, R, dh)
    k_blocks = jnp.transpose(k_s.reshape(B, n_s, SLC_BLOCK, G, dh), (0, 3, 1, 2, 4)).reshape(B, G, n_s, SLC_BLOCK * dh)
    v_blocks = jnp.transpose(v_s.reshape(B, n_s, SLC_BLOCK, G, dh), (0, 3, 1, 2, 4)).reshape(B, G, n_s, SLC_BLOCK * dh)
    k_w_pad = jnp.pad(k_w, ((0, 0), (WINDOW, 0), (0, 0), (0, 0)))
    v_w_pad = jnp.pad(v_w, ((0, 0), (WINDOW, 0), (0, 0), (0, 0)))
    blk = jnp.arange(n_s)

    def block(qb):
        start = qb * Q_BLOCK
        t = start + jnp.arange(Q_BLOCK)
        tf = t.astype(jnp.float32)
        qi = lax.dynamic_slice_in_dim(q_g, start, Q_BLOCK, axis=1)
        gi = lax.dynamic_slice_in_dim(gates, start, Q_BLOCK, axis=1)

        d_c = tf[:, None] - cmp_end[None, :].astype(jnp.float32)
        s_c = jnp.einsum('bqgrd,bngd->bgrqn', qi, kc).astype(jnp.float32) * scale
        s_c = s_c - slopes[None, :, :, None, None] * d_c
        p_c = masked_softmax(s_c, d_c >= 0)
        o_c = jnp.einsum('bgrqn,bngd->bqgrd', p_c.astype(dt), vc)

        imp = jnp.sum(p_c, axis=2)
        imp = jnp.pad(imp, ((0, 0), (0, 0), (0, 0), (r - 1, ratio * n_s + r - 1 - n_c - (r - 1))))
        p_slc = imp[..., 0:ratio * n_s:ratio]
        for o in range(1, ratio + r - 1):
            p_slc = p_slc + imp[..., o:o + ratio * n_s:ratio]
        cur = t // SLC_BLOCK
        forced = (blk[None, :] == 0) | (blk[None, :] == cur[:, None]) | (blk[None, :] == cur[:, None] - 1)
        future = blk[None, :] > cur[:, None]
        p_slc = jnp.where(forced, BIG, jnp.where(future, NEG_INF, p_slc))
        _, idx = lax.top_k(p_slc, n_sel)

        flat_idx = idx.reshape(B, G, Q_BLOCK * n_sel)[..., None]
        kg = jnp.take_along_axis(k_blocks, flat_idx, axis=2).reshape(B, G, Q_BLOCK, n_sel * SLC_BLOCK, dh)
        vg = jnp.take_along_axis(v_blocks, flat_idx, axis=2).reshape(B, G, Q_BLOCK, n_sel * SLC_BLOCK, dh)
        kpos = (idx[..., None] * SLC_BLOCK + jnp.arange(SLC_BLOCK)).reshape(B, G, Q_BLOCK, n_sel * SLC_BLOCK)
        d_s = (t[None, None, :, None] - kpos).astype(jnp.float32)
        s_s = jnp.einsum('bqgrd,bgqkd->bgrqk', qi, kg).astype(jnp.float32) * scale
        s_s = s_s - slopes[None, :, :, None, None] * d_s[:, :, None]
        p_s = masked_softmax(s_s, (d_s >= 0)[:, :, None])
        o_s = jnp.einsum('bgrqk,bgqkd->bqgrd', p_s.astype(dt), vg)

        kw = lax.dynamic_slice_in_dim(k_w_pad, start, WINDOW + Q_BLOCK, axis=1)
        vw = lax.dynamic_slice_in_dim(v_w_pad, start, WINDOW + Q_BLOCK, axis=1)
        wpos = start - WINDOW + jnp.arange(WINDOW + Q_BLOCK)
        d_w = t[:, None] - wpos[None, :]
        m_w = (d_w >= 0) & (d_w < WINDOW) & (wpos[None, :] >= 0)
        s_w = jnp.einsum('bqgrd,bkgd->bgrqk', qi, kw).astype(jnp.float32) * scale
        s_w = s_w - slopes[None, :, :, None, None] * d_w.astype(jnp.float32)
        p_w = masked_softmax(s_w, m_w)
        o_w = jnp.einsum('bgrqk,bkgd->bqgrd', p_w.astype(dt), vw)

        return gi[..., 0:1] * o_c + gi[..., 1:2] * o_s + gi[..., 2:3] * o_w

    out = lax.map(block, jnp.arange(S // Q_BLOCK))
    return jnp.transpose(out, (1, 0, 2, 3, 4, 5)).reshape(B, S, H * dh)

def mixer_fox_nsa(h, w_in, b_f, cmp_pe, cmp_w1, cmp_w2, w_out):
    B, S, _ = h.shape
    proj = h @ w_in
    offs = [0]
    for n in IN_SIZES:
        offs.append(offs[-1] + n)
    fq, fk, fv, ff, nq, kc, vc, ks, vs, kw, vw, ng = [proj[..., offs[i]:offs[i + 1]] for i in range(len(IN_SIZES))]
    hd = (B, S, FOX_HEADS, HEAD_DIM)
    log_f = jax.nn.log_sigmoid((ff + b_f).astype(jnp.float32))
    o_fox = fox_attention(fq.reshape(hd), fk.reshape(hd), fv.reshape(hd), log_f)
    kvd = (B, S, NSA_KV_GROUPS, HEAD_DIM)
    gates = jax.nn.sigmoid(ng.astype(jnp.float32)).astype(h.dtype).reshape(B, S, NSA_KV_GROUPS, NSA_GROUP_SIZE, 3)
    o_nsa = nsa_attention(nq.reshape(B, S, NSA_HEADS, HEAD_DIM), kc.reshape(kvd), vc.reshape(kvd),
                          ks.reshape(kvd), vs.reshape(kvd), kw.reshape(kvd), vw.reshape(kvd),
                          gates, cmp_pe, cmp_w1, cmp_w2)
    return jnp.concatenate([o_fox, o_nsa], axis=-1) @ w_out

def mixer_pool(h, w_groups, scale):
    B, S, D = h.shape
    hf = h.astype(jnp.float32)
    c = jnp.cumsum(hf, axis=1)
    count = jnp.arange(1, S + 1, dtype=jnp.float32)
    outs = []
    for gi, w in enumerate(POOL_WINDOWS):
        sl = slice(gi * POOL_GROUP, (gi + 1) * POOL_GROUP)
        cg = c[..., sl]
        lag = jnp.pad(cg, ((0, 0), (w, 0), (0, 0)))[:, :S]
        mean = (cg - lag) / jnp.minimum(count, float(w))[None, :, None]
        outs.append(mean - hf[..., sl])
    pooled = jnp.stack(outs, axis=2).astype(h.dtype)
    y = jnp.einsum('bsgc,gcd->bsgd', pooled, w_groups).reshape(B, S, D)
    return y * scale

def swiglu(h, w_gate, w_up, w_down):
    return (jax.nn.silu(h @ w_gate) * (h @ w_up)) @ w_down

def second_inputs(seed: int = 0) -> dict:
    key = jax.random.key(seed)
    ks = jax.random.split(key, 13)
    f32 = jnp.float32
    dh = HEAD_DIM
    x = jax.random.normal(ks[0], (BATCH, SEQ, D_MODEL), f32)
    norm_g = 1.0 + 0.05 * jax.random.normal(ks[1], (DEPTH_2, 4, D_MODEL), f32)
    attn_w_in = jax.random.normal(ks[2], (N_EVEN, D_MODEL, IN_COLS), f32) * D_MODEL ** -0.5
    fox_b_f = jax.random.uniform(ks[3], (N_EVEN, FOX_HEADS), f32, 1.0, 4.0)
    nsa_cmp_pe = 0.1 * jax.random.normal(ks[4], (N_EVEN, 2, CMP_BLOCK, dh), f32)
    nsa_cmp_w1 = jax.random.normal(ks[5], (N_EVEN, 2, CMP_BLOCK * dh, dh), f32) * (CMP_BLOCK * dh) ** -0.5
    nsa_cmp_w2 = jax.random.normal(ks[6], (N_EVEN, 2, dh, dh), f32) * dh ** -0.5
    attn_w_out = jax.random.normal(ks[7], (N_EVEN, MIX_WIDTH_2, D_MODEL), f32) * MIX_WIDTH_2 ** -0.5
    pool_w = jax.random.normal(ks[8], (N_ODD, len(POOL_WINDOWS), POOL_GROUP, POOL_GROUP), f32) * POOL_GROUP ** -0.5
    pool_scale = 1.0 + 0.1 * jax.random.normal(ks[9], (N_ODD, D_MODEL), f32)
    ffn_w_gate = jax.random.normal(ks[10], (DEPTH_2, D_MODEL, FFN_HIDDEN), f32) * D_MODEL ** -0.5
    ffn_w_up = jax.random.normal(ks[11], (DEPTH_2, D_MODEL, FFN_HIDDEN), f32) * D_MODEL ** -0.5
    ffn_w_down = jax.random.normal(ks[12], (DEPTH_2, FFN_HIDDEN, D_MODEL), f32) * FFN_HIDDEN ** -0.5
    return {"x": x, "norm_g": norm_g, "attn_w_in": attn_w_in, "fox_b_f": fox_b_f,
            "nsa_cmp_pe": nsa_cmp_pe, "nsa_cmp_w1": nsa_cmp_w1, "nsa_cmp_w2": nsa_cmp_w2,
            "attn_w_out": attn_w_out, "pool_w": pool_w, "pool_scale": pool_scale,
            "ffn_w_gate": ffn_w_gate, "ffn_w_up": ffn_w_up, "ffn_w_down": ffn_w_down}

def second_block(x, norm_g, attn_w_in, fox_b_f, nsa_cmp_pe, nsa_cmp_w1, nsa_cmp_w2, attn_w_out,
              pool_w, pool_scale, ffn_w_gate, ffn_w_up, ffn_w_down):
    h = x
    for layer in range(DEPTH_2):
        g = norm_g[layer]
        i = layer // 2
        u = rmsnorm(h, g[0])
        if layer % 2 == 0:
            m = mixer_fox_nsa(u, attn_w_in[i], fox_b_f[i], nsa_cmp_pe[i], nsa_cmp_w1[i], nsa_cmp_w2[i], attn_w_out[i])
        else:
            m = mixer_pool(u, pool_w[i], pool_scale[i])
        h = h + rmsnorm(m, g[1])
        u = rmsnorm(h, g[2])
        h = h + rmsnorm(swiglu(u, ffn_w_gate[layer], ffn_w_up[layer], ffn_w_down[layer]), g[3])
    return h


def setup_inputs(seed=0):
    out = dict(first_inputs(seed))
    for name, value in second_inputs(seed + 1).items():
        if name != "x":
            out[name + "_2"] = value
    return out


def reference(
    x, mem, norm_mix_g, norm_ffn_g, w_out, w_ff1, w_ff2, mem_norm_g, w_mem_kv, mem_q_norm_g,
    mem_k_norm_g, rw_in, rw_mu, rw_w0, rw_w2, rw_a0, rw_a2, rw_g2, rw_k_k, rw_k_a, rw_r_k,
    rw_lnx_g, rw_lnx_b, df_in, df_q_norm_g, df_k_norm_g, df_lq1, df_lk1, df_lq2, df_lk2,
    df_subln_g, norm_g_2, attn_w_in_2, fox_b_f_2, nsa_cmp_pe_2, nsa_cmp_w1_2, nsa_cmp_w2_2,
    attn_w_out_2, pool_w_2, pool_scale_2, ffn_w_gate_2, ffn_w_up_2, ffn_w_down_2,
):
    x = first_block(
        x, mem, norm_mix_g, norm_ffn_g, w_out, w_ff1, w_ff2, mem_norm_g, w_mem_kv, mem_q_norm_g,
        mem_k_norm_g, rw_in, rw_mu, rw_w0, rw_w2, rw_a0, rw_a2, rw_g2, rw_k_k, rw_k_a, rw_r_k,
        rw_lnx_g, rw_lnx_b, df_in, df_q_norm_g, df_k_norm_g, df_lq1, df_lk1, df_lq2, df_lk2,
        df_subln_g,
    )
    return second_block(
        x, norm_g_2, attn_w_in_2, fox_b_f_2, nsa_cmp_pe_2, nsa_cmp_w1_2, nsa_cmp_w2_2,
        attn_w_out_2, pool_w_2, pool_scale_2, ffn_w_gate_2, ffn_w_up_2, ffn_w_down_2,
    )


_drawn_inputs = setup_inputs


def setup_inputs(seed=0):
    import zlib

    import numpy as np

    out = dict(_drawn_inputs(seed))
    spreads = {}
    factors = {'mem_norm_g': 8.0,
     'mem_q_norm_g': 8.0,
     'mem_k_norm_g': 8.0,
     'rw_w2': 16.469,
     'rw_a0': 12.544,
     'rw_lnx_b': 44.094,
     'norm_ffn_g': 3.296,
     'rw_k_k': 37.716,
     'rw_k_a': 8.0,
     'rw_lnx_g': 8.0,
     'nsa_cmp_pe_2': 17.749,
     'norm_g_2': 4.953,
     'fox_b_f_2': 4.501,
     'pool_scale_2': 7.909}
    for name, (base, spread) in spreads.items():
        noise = np.random.default_rng([zlib.crc32(name.encode()), seed]).standard_normal(out[name].shape)
        drawn = base * np.exp(spread * noise) if base else spread * noise
        out[name] = jnp.asarray(drawn.astype(out[name].dtype))
    for name, factor in factors.items():
        out[name] = (out[name] * factor).astype(out[name].dtype)
    return out
```

```python
from contextlib import ExitStack

import concourse.bass as bass
from concourse import mybir

F32 = mybir.dt.float32
ALU = mybir.AluOpType
ACT = mybir.ActivationFunctionType
AX = mybir.AxisListType

P = 128
T = 512
D = 1024
KT = D // P
TT = T // P
M = 256
HD = 64
MIX = 768
PAIRS = MIX // P
LOG_DECAY = 0.6065306597126334
CH = 64
NCH = T // CH
RING = 4
PW = 256
HID = 2816
HK = HID // P
DOWN_CHUNKS = (6, 6, 5, 5)
BANK = 512
BIG = 1e30
RMS_EPS = 1e-6
GN_EPS = 64e-5
KK_SCALE = 2.0 ** 24
KK_BIAS = 12.0 * 0.6931471805599453

VEC_A = (("norm_mix_g", 8), ("norm_ffn_g", 8), ("mem_norm_g", 8), ("rw_mu", 20), ("rw_w0", 6), ("rw_a0", 6),
         ("rw_k_k", 6), ("rw_k_a", 6), ("rw_r_k", 6), ("rw_lnx_g", 6), ("rw_lnx_b", 6),
         ("mem_q_norm_g", 1), ("mem_k_norm_g", 1))
VEC_B = (("norm_g_2", 64), ("pool_scale_2", 8))


def rows_of(table):
    at, out = 0, {}
    for name, n in table:
        out[name] = at
        at += n
    return out, at


ROW_A, N_A = rows_of(VEC_A)
ROW_B, N_B = rows_of(VEC_B)

FQ, FK, FV, FF, NQ, KC, VC, KS, VS, KW, VW, NG = 0, 512, 1024, 1536, 1544, 2056, 2184, 2312, 2440, 2568, 2696, 2824


class Kernel:

    def __init__(self, nc, ctx, ins, out):
        self.nc, self.ins, self.out = nc, ins, out
        self.n_blocks = 0

        def sb(name, shape):
            return ctx.enter_context(nc.sbuf_tensor(name, shape, F32))

        self.ring = sb("weight_ring", [P, RING, KT * PW])
        self.xT = sb("residual_T", [P, KT, T])
        self.hT = sb("normed_T", [P, KT, T])
        self.ident = sb("identity", [P, P])
        self.ones = sb("ones", [P, P])
        self.head_ones = sb("head_ones", [P, P])
        self.eye64 = sb("eye64", [P, HD])
        self.level = sb("level_masks", [P, 6, P])
        self.level0_T = sb("level0_mask_T", [P, P])
        self.upto_T = sb("upto_mask_T", [P, P])
        self.before_T = sb("before_mask_T", [P, P])
        self.restart = sb("restart", [P, T])
        self.eps = sb("eps_columns", [P, 4])
        self.col_a = sb("columns_a", [P, N_A])
        self.col_b = sb("columns_b", [P, N_B])
        self.pe_T = sb("position_T", [P, 2, 32])
        self.k_mem = sb("k_mem_T", [P, 2, M])
        self.v_mem = sb("v_mem", [P, 2, M])
        self.ps = ctx.enter_context(nc.psum_tensor("psum", [P, 8, BANK], F32))
        self.panel_landed = [ctx.enter_context(nc.semaphore(f"panel_landed_{s}")) for s in range(RING)]
        self.panel_used = ctx.enter_context(nc.semaphore("panel_used"))
        self.norm_sems = [ctx.enter_context(nc.semaphore(f"norm_{s}")) for s in ("squared", "summed", "logged", "rooted", "scaled")]
        self.norms = 0
        self.plan_panels()
        self.loaded = 0

    def plan_panels(self):
        ins, self.phases, self.first_panel = self.ins, [], {}

        def tall(w):
            return w.rearrange("(k p) m -> p k m", p=P)

        def columns(w, c0=0):
            view = tall(w)
            return lambda i: (view[:, :, bass.ds(c0 + PW * i, PW)], view.shape[1], PW)

        def listed(parts):
            return lambda i: parts[i]

        def chunked(w, chunks):
            view, parts, k0 = tall(w), [], 0
            for n in chunks:
                parts.append((k0, n))
                k0 += n
            return lambda i, j: (view[:, parts[j][0]:parts[j][0] + parts[j][1], bass.ds(PW * i, PW)], parts[j][1], PW)

        def add(name, n, view, kind="columns"):
            self.first_panel[name] = sum(x[1] for x in self.phases)
            self.phases.append((name, n, view, kind))

        add("mem_kv", 2, columns(ins["w_mem_kv"]))
        add("rw_in", 11, columns(ins["rw_in"][0]))
        add("w_out", 4, columns(ins["w_out"][0]))
        add("ff1", 16, columns(ins["w_ff1"][0]))
        add("ff2", 16, chunked(ins["w_ff2"][0], (8, 8, 8, 8)), "chunks")
        w = tall(ins["attn_w_in_2"][0])
        cuts = [(FQ, 256), (FQ + 256, 256), (FK, 256), (FK + 256, 256), (FV, 256), (FV + 256, 256), (NQ, 256),
                (NQ + 256, 256), (KC, 256), (KS, 256), (KW, 256), (FF, 8), (NG, 24)]
        add("attn_in", len(cuts), listed([(w[:, :, c:c + n], KT, n) for c, n in cuts]), "listed")
        add("attn_out", 4, columns(ins["attn_w_out_2"][0]))
        for layer in range(2):
            gate, up = tall(ins["ffn_w_gate_2"][layer]), tall(ins["ffn_w_up_2"][layer])

            def gate_up(i, j, gate=gate, up=up):
                return ((gate, up)[j % 2][:, :, bass.ds(2 * PW * i + PW * (j // 2), PW)], KT, PW)

            add(f"gate_up{layer}", 2 * HID // PW, gate_up, "chunks")
            add(f"down{layer}", 16, chunked(ins["ffn_w_down_2"][layer], DOWN_CHUNKS), "chunks")
            if layer == 0:
                pool = [(ins["pool_w_2"][0, g].rearrange("(k p) m -> p k m", p=P), 2, PW) for g in range(4)]
                add("pool", 4, listed(pool), "listed")
        self.n_panels = sum(x[1] for x in self.phases)

    def load_panels(self, sp, until):
        until = min(until, self.n_panels)
        start = 0
        for name, n, view, kind in self.phases:
            lo, hi = max(self.loaded, start), min(until, start + n)
            g0, start = start, start + n

            def load(i, j, g0=g0, view=view, kind=kind):
                slot, g = (g0 + j) % RING, g0 + j
                src, kt, width = view(i, j) if kind == "chunks" else view(4 * i + j)
                if not isinstance(i, int) or g + 4 * i >= RING:
                    sp.wait_ge(self.panel_used, 4 * i + (g - RING + 1))
                dst = self.ring[:, slot, 0:kt * width].rearrange("p (k m) -> p k m", k=kt)
                sp.dma_start(dst, src).then_inc(self.panel_landed[slot], 16)

            at = lo - g0
            while at < hi - g0:
                fours = (hi - g0 - at) // 4
                if at % 4 == 0 and fours >= 2 and kind != "listed" and g0 + at >= RING:
                    with sp.Fori(at // 4, at // 4 + fours) as i:
                        for j in range(4):
                            load(i, j)
                    at += 4 * fours
                else:
                    load(at // 4, at % 4)
                    at += 1
        self.loaded = max(self.loaded, until)

    def panel(self, g0, i, j, kt, width):
        slot = (g0 + j) % RING
        tile = self.ring[:, slot, 0:kt * width].rearrange("p (k m) -> p k m", k=kt)
        return tile, self.panel_landed[slot], 16 * i + 16 * ((g0 + j) // RING + 1)

    def lookahead(self, name):
        n = next(x[1] for x in self.phases if x[0] == name)
        return self.first_panel[name] + n + RING


class Phase:

    def __init__(self, k, name):
        self.k, self.name, self.ctx = k, name, ExitStack()

    def __enter__(self):
        self.ctx.__enter__()
        return self

    def __exit__(self, *a):
        return self.ctx.__exit__(*a)

    def sem(self, name):
        return self.ctx.enter_context(self.k.nc.semaphore(f"{self.name}_{name}"))

    def sb(self, name, shape):
        return self.ctx.enter_context(self.k.nc.sbuf_tensor(f"{self.name}_{name}", shape, F32))


def in_fours(eng, n, body):
    if n >= 8:
        with eng.Fori(0, n // 4) as i:
            for j in range(4):
                body(i, j)
    else:
        for at in range(4 * (n // 4)):
            body(at // 4, at % 4)
    for j in range(n % 4):
        body(n // 4, j)



def setup(k):
    nc, ps, ins = k.nc, k.ps, k.ins
    with Phase(k, "setup") as f:
        x_in, mem_in = f.sb("x", [P, TT, D]), f.sb("mem", [P, 2, D])
        vec_a, vec_b, pe_in = f.sb("vec_a", [N_A, P]), f.sb("vec_b", [N_B, P]), f.sb("pe", [32, 2, P])
        k.memT = k.hT
        x_landed, vec_landed, mem_landed = f.sem("x_landed"), f.sem("vec_landed"), f.sem("mem_landed")
        filled, cut = f.sem("filled"), f.sem("cut")
        x_turned, x_copied, mem_turned, mem_copied = (f.sem(n) for n in ("x_turned", "x_copied", "mem_turned", "mem_copied"))
        vec_turned = f.sem("vec_turned")
        with nc.Block() as block:

            @block.sync
            def _(sp):
                for t in range(TT):
                    sp.dma_start(x_in[:, t, :], ins["x"][0, t * P:(t + 1) * P, :]).then_inc(x_landed, 16)
                for t in range(2):
                    sp.dma_start(mem_in[:, t, :], ins["mem"][0, t * P:(t + 1) * P, :]).then_inc(mem_landed, 16)
                k.load_panels(sp, RING)

            @block.gpsimd
            def _(pool):
                for n, (tile, value) in enumerate(((k.ident, 0.0), (k.head_ones, 1.0), (k.eye64, 0.0), (k.level, 1.0),
                                                   (k.level0_T, 0.0), (k.upto_T, 1.0), (k.before_T, 1.0),
                                                   (k.restart, 1.0), (k.ones, 1.0))):
                    pool.memset(tile[:], value).then_inc(filled, 1)
                pool.wait_ge(filled, 9)

                def select(n, view, pattern, base, channel, op, fill):
                    if n:
                        pool.wait_ge(cut, n)
                    pool.affine_select(out=view, in_=view, pattern=pattern, compare_op=op, fill=fill, base=base,
                                       channel_multiplier=channel).then_inc(cut, 1)

                cuts = [(k.ident[:], [[-1, P]], 0, 1, ALU.not_equal, 1.0),
                        (k.eye64[:], [[-1, HD]], 0, 1, ALU.not_equal, 1.0),
                        (k.eye64[:], [[-1, HD]], -HD, 1, ALU.not_equal, 1.0)]
                halves = k.head_ones[:].rearrange("p (h c) -> p h c", h=2)
                cuts += [(halves, [[-HD, 2], [0, HD]], 0, 1, ALU.is_ge, 0.0),
                         (halves, [[HD, 2], [0, HD]], HD - 1, -1, ALU.is_ge, 0.0)]
                for lv in range(6):
                    s = 1 << lv
                    cells = k.level[:, lv, :].rearrange("p (b h s) -> p b h s", h=2, s=s)
                    cuts += [(cells, [[-2 * s, P // (2 * s)], [-P * 2, 2], [0, s]], -s, 1, ALU.is_ge, 0.0),
                             (cells, [[2 * s, P // (2 * s)], [0, 2], [0, s]], 2 * s - 1, -1, ALU.is_ge, 0.0)]
                cells = k.level0_T[:].rearrange("p (b h) -> p b h", h=2)
                cuts += [(cells[:, :, 1], [[-2, P // 2]], 0, 1, ALU.not_equal, 1.0)]
                for tile, strict in ((k.upto_T, 0), (k.before_T, 1)):
                    cells = tile[:].rearrange("p (c t) -> p c t", c=2)
                    cuts += [(cells, [[CH, 2], [1, CH]], -strict, -1, ALU.is_ge, 0.0),
                             (cells, [[-CH, 2], [0, CH]], 0, 1, ALU.is_ge, 0.0)]
                cells = k.restart[:].rearrange("p (c t) -> p c t", c=NCH)
                cuts += [(cells, [[0, NCH], [1, CH]], 0, 0, ALU.not_equal, 0.0)]
                for n, c in enumerate(cuts):
                    select(n, *c)

            @block.scalar
            def _(act):
                for table, tile, row in ((VEC_A, vec_a, ROW_A), (VEC_B, vec_b, ROW_B)):
                    for name, n in table:
                        a = ins[name]
                        for half in range(2 if n == 1 else 1):
                            if n == 1:
                                flat, dst = a, tile[row[name]:row[name] + 1, half * HD:(half + 1) * HD]
                            else:
                                order = {1: "(r c) -> r c", 2: "l (r c) -> (l r) c", 3: "l n (r c) -> (l n r) c"}
                                if name == "rw_r_k":
                                    flat = a.rearrange("l (r h) c -> (l r) (h c)", h=2)
                                else:
                                    flat = a.rearrange(order[len(a.shape)], c=P)
                                dst = tile[row[name]:row[name] + n, :]
                            act.dma_start(dst, flat).then_inc(vec_landed, 16)
                for kv in range(2):
                    for half in range(2):
                        act.dma_start(pe_in[:, kv, half * HD:(half + 1) * HD],
                                      ins["nsa_cmp_pe_2"][0, kv]).then_inc(vec_landed, 16)
                for kt in range(KT):
                    act.wait_ge(x_turned, kt + 1)
                    act.copy(k.xT[:, kt, :], ps[:, kt % 4, :]).then_inc(x_copied, 1)

            @block.vector
            def _(dve):
                for n, value in enumerate((RMS_EPS, GN_EPS, KK_BIAS, 1.0)):
                    dve.memset(k.eps[:, n:n + 1], value)
                for j in range(4):
                    dve.wait_ge(mem_turned, j + 1)
                    dve.tensor_copy(k.memT[:, 2 * j:2 * j + 2, 0:M],
                                    ps[:, 4 + j % 2, :].rearrange("p (k m) -> p k m", k=2)).then_inc(mem_copied, 1)
                dve.wait_ge(vec_turned, 1)
                dve.tensor_copy(k.col_a[:], ps[:, 6, 0:N_A])
                dve.tensor_copy(k.col_b[:], ps[:, 6, P:P + N_B])
                dve.tensor_copy(k.pe_T[:], ps[:, 6, 2 * P:2 * P + 64].rearrange("p (v i) -> p v i", v=2))

            @block.tensor
            def _(pe):
                pe.wait_ge(cut, 1)
                pe.wait_ge(x_landed, 16 * TT)
                for kt in range(KT):
                    if kt >= 4:
                        pe.wait_ge(x_copied, kt - 3)
                    for t in range(TT):
                        last = pe.transpose(ps[:, kt % 4, t * P:(t + 1) * P], x_in[:, t, kt * P:(kt + 1) * P], k.ident[:])
                    last.then_inc(x_turned, 1)
                pe.wait_ge(mem_landed, 32)
                for j in range(4):
                    if j >= 2:
                        pe.wait_ge(mem_copied, j - 1)
                    for kt in (2 * j, 2 * j + 1):
                        for t in range(2):
                            c = (kt % 2) * M + t * P
                            last = pe.transpose(ps[:, 4 + j % 2, c:c + P], mem_in[:, t, kt * P:(kt + 1) * P], k.ident[:])
                    last.then_inc(mem_turned, 1)
                pe.wait_ge(vec_landed, 16 * (len(VEC_A) + len(VEC_B) + 2 + 4))
                pe.transpose(ps[:, 6, 0:N_A], vec_a[:], k.ident[0:N_A, 0:N_A])
                pe.transpose(ps[:, 6, P:P + N_B], vec_b[:], k.ident[0:N_B, 0:N_B])
                for kv in range(2):
                    last = pe.transpose(ps[:, 6, 2 * P + 32 * kv:2 * P + 32 * kv + 32], pe_in[:, kv, :], k.ident[0:32, 0:32])
                last.then_inc(vec_turned, 1)



def rms_norm(k, name, src, gain, dst, n=T, add=False):
    nc, ps = k.nc, k.ps
    with Phase(k, name) as f:
        squares, logs, rstd = f.sb("squares", [P, KT, n]), f.sb("logs", [P, n]), f.sb("rstd", [P, n])
        (squared, summed, logged, rooted, scaled), c = k.norm_sems, k.norms
        k.norms += 1
        with nc.Block() as block:

            @block.scalar
            def _(act):
                for kt in range(KT):
                    act.activation(squares[:, kt, :], src[:, kt, 0:n], ACT.Square).then_inc(squared, 1)
                act.wait_ge(summed, c + 1)
                act.activation(logs[:], ps[:, 0, 0:n], ACT.Ln, bias=k.eps[:, 0:1], scale=1.0 / D).then_inc(logged, 1)
                act.wait_ge(logged, c + 1)
                act.activation(rstd[:], logs[:], ACT.Exp, scale=-0.5).then_inc(rooted, 1)

            @block.tensor
            def _(pe):
                for kt in range(KT):
                    pe.wait_ge(squared, KT * c + kt + 1)
                    last = pe.matmul(ps[:, 0, 0:n], k.ones[:], squares[:, kt, :], start=kt == 0, stop=kt == KT - 1)
                last.then_inc(summed, 1)

            @block.vector
            def _(dve):
                dve.wait_ge(rooted, c + 1)
                for kt in range(KT):
                    to = squares if add else dst
                    dve.scalar_tensor_tensor(to[:, kt, 0:n], src[:, kt, 0:n], gain[:, kt:kt + 1], rstd[:], ALU.mult,
                                             ALU.mult).then_inc(scaled, 1)
                if add:
                    for kt in range(KT):
                        dve.wait_ge(scaled, KT * c + kt + 1)
                        dve.tensor_tensor(dst[:, kt, :], dst[:, kt, :], squares[:, kt, :], ALU.add)



def memory_kv(k):
    nc, ps, g0 = k.nc, k.ps, k.first_panel["mem_kv"]
    gain = k.col_a[:, ROW_A["mem_k_norm_g"]:ROW_A["mem_k_norm_g"] + 1]
    with Phase(k, "mem_kv") as f:
        squares, logs, rstd, raw = (f.sb(s, [P, 2, M]) for s in ("squares", "logs", "rstd", "raw"))
        copied, summed, logged, rooted = (f.sem(s) for s in ("copied", "summed", "logged", "rooted"))
        with nc.Block() as block:

            @block.sync
            def _(sp):
                k.load_panels(sp, k.lookahead("mem_kv"))

            @block.tensor
            def _(pe):
                w, landed, value = k.panel(g0, 0, 0, KT, PW)
                pe.wait_ge(landed, value)
                for m in range(2):
                    for kt in range(KT):
                        last = pe.matmul(ps[:, m, 0:M], w[:, kt, m * P:(m + 1) * P], k.hT[:, kt, 0:M], start=kt == 0,
                                         stop=kt == KT - 1)
                last.then_inc(k.panel_used, 1)
                w, landed, value = k.panel(g0, 0, 1, KT, PW)
                pe.wait_ge(landed, value)
                for t in range(2):
                    for kt in range(KT):
                        last = pe.matmul(ps[:, 2 + t, 0:M], k.hT[:, kt, t * P:(t + 1) * P], w[:, kt, :], start=kt == 0,
                                         stop=kt == KT - 1)
                last.then_inc(k.panel_used, 1)
                pe.wait_ge(copied, 2)
                for m in range(2):
                    last = pe.matmul(ps[:, 4, m * M:(m + 1) * M], k.head_ones[:], squares[:, m, :], start=True, stop=True)
                last.then_inc(summed, 1)

            @block.scalar
            def _(act):
                act.wait_ge(k.panel_used, g0 + 1)
                act.copy(raw[:], ps[:, 0:2, 0:M]).then_inc(copied, 1)
                act.activation(squares[:], ps[:, 0:2, 0:M], ACT.Square).then_inc(copied, 1)
                act.wait_ge(k.panel_used, g0 + 2)
                act.copy(k.v_mem[:], ps[:, 2:4, 0:M])
                act.wait_ge(summed, 1)
                act.activation(logs[:], ps[:, 4, :].rearrange("p (m t) -> p m t", m=2), ACT.Ln, bias=k.eps[:, 0:1],
                               scale=1.0 / HD).then_inc(logged, 1)
                act.wait_ge(logged, 1)
                act.activation(rstd[:], logs[:], ACT.Exp, scale=-0.5).then_inc(rooted, 1)

            @block.vector
            def _(dve):
                dve.wait_ge(rooted, 1)
                dve.scalar_tensor_tensor(k.k_mem[:], raw[:], gain, rstd[:], ALU.mult, ALU.mult)



def wait_block(eng, k, g0, made, i, b):
    if b % 2 == 0:
        eng.wait_ge(made, 4 * i + b // 2 + 1)
    else:
        eng.wait_ge(k.panel_used, 4 * i + (g0 + b // 2 + 1))


def stream_columns(pe, k, name, rhs, ps, made, bank_free, need=lambda b: b + 1):
    kts = KT
    g0 = k.first_panel[name]
    n = next(x[1] for x in k.phases if x[0] == name)

    def body(i, j):
        w, landed, value = k.panel(g0, i, j, kts, PW)
        pe.wait_ge(landed, value)
        for m in range(2):
            pe.wait_ge(bank_free, 8 * i + need(2 * j + m))
            for kt in range(kts):
                last = pe.matmul(ps[:, 2 * j + m, :], w[:, kt, m * P:(m + 1) * P], rhs[:, kt, :], start=kt == 0,
                                 stop=kt == kts - 1)
            last.then_inc(k.panel_used if m else made, 1)

    in_fours(pe, n, body)


def rwkv_in(k, slab):
    nc, ps, g0 = k.nc, k.ps, k.first_panel["rw_in"]
    mu, n_mu, n_all = k.col_a[:, ROW_A["rw_mu"]:ROW_A["rw_mu"] + 20], 20, 22
    with Phase(k, "rw_in") as f:
        z, step = f.sb("z", [P, 2, T + 1]), f.sb("step", [P, 2, T])
        made, bank_free, zeroed, stepped, shifted = (f.sem(s) for s in ("made", "bank_free", "zeroed", "stepped", "shifted"))
        with nc.Block() as block:

            @block.sync
            def _(sp):
                k.load_panels(sp, k.lookahead("rw_in"))

            @block.tensor
            def _(pe):
                stream_columns(pe, k, "rw_in", k.hT, ps, made, bank_free)

            @block.scalar
            def _(act):
                act.sem_inc(bank_free, 8)
                for b in range(n_all):
                    wait_block(act, k, g0, made, 0, b)
                    if b >= n_mu:
                        act.copy(slab[:, b, :], ps[:, b % 8, :]).then_inc(bank_free, 1)
                        continue
                    if b == 0:
                        act.wait_ge(zeroed, 1)
                    if b >= 2:
                        act.wait_ge(shifted, b - 1)
                    act.copy(z[:, b % 2, 1:T + 1], ps[:, b % 8, :]).then_inc(bank_free, 1)

            @block.vector
            def _(dve):
                dve.memset(z[:, :, 0:1], 0.0).then_inc(zeroed, 1)
                for b in range(n_mu):
                    dve.wait_ge(bank_free, 8 + b + 1)
                    if b >= 2:
                        dve.wait_ge(shifted, b - 1)
                    dve.tensor_tensor(step[:, b % 2, :], z[:, b % 2, 0:T], z[:, b % 2, 1:T + 1],
                                      ALU.subtract).then_inc(stepped, 1)
                    dve.wait_ge(stepped, b + 1)
                    dve.scalar_tensor_tensor(slab[:, b, :], step[:, b % 2, :], mu[:, b:b + 1], z[:, b % 2, 1:T + 1],
                                             ALU.mult, ALU.add).then_inc(shifted, 1)


def add_projection(k, name, rhs, kts, out=None):
    nc, ps, g0 = k.nc, k.ps, k.first_panel[name]
    chunks, k0 = [], 0
    for n in kts:
        chunks.append((k0, n))
        k0 += n
    with Phase(k, name) as f:
        made = f.sem("made")
        with nc.Block() as block:

            @block.sync
            def _(sp):
                k.load_panels(sp, k.lookahead(name))

            @block.tensor
            def _(pe):
                def pair(i, j, at, n, bank):
                    w, landed, value = k.panel(g0, i, j, n, PW)
                    pe.wait_ge(landed, value)
                    for m in range(2):
                        for kt in range(n):
                            last = pe.matmul(ps[:, bank + m, :] if isinstance(bank, int) else ps[:, bass.ds(bank + m, 1), :],
                                             w[:, kt, m * P:(m + 1) * P], rhs[:, at + kt, :],
                                             start=at + kt == 0, stop=at + kt == k0 - 1)
                        if m:
                            last.then_inc(k.panel_used, 1)
                        elif at + n == k0:
                            last.then_inc(made, 1)

                if len(chunks) == 1:
                    for j in range(4):
                        pair(0, j, 0, chunks[0][1], 2 * j)
                else:
                    for i in range(4):
                        for j, (at, n) in enumerate(chunks):
                            pair(i, j, at, n, 2 * i)

            @block.vector
            def _(dve):
                for b in range(KT):
                    if b % 2 == 0:
                        dve.wait_ge(made, b // 2 + 1)
                    else:
                        dve.wait_ge(k.panel_used, g0 + len(chunks) * (b // 2 + 1))
                    if out is None:
                        dve.tensor_tensor(k.xT[:, b, :], ps[:, b, :], k.xT[:, b, :], ALU.add)
                    else:
                        dve.tensor_copy(out[:, b, :], ps[:, b, :])


def squared_relu_ffn_in(k, hidden):
    nc, ps, n, g0 = k.nc, k.ps, 16, k.first_panel["ff1"]
    with Phase(k, "ff1") as f:
        made, bank_free = f.sem("made"), f.sem("bank_free")
        with nc.Block() as block:

            @block.sync
            def _(sp):
                k.load_panels(sp, k.lookahead("ff1"))

            @block.tensor
            def _(pe):
                stream_columns(pe, k, "ff1", k.hT, ps, made, bank_free)

            @block.scalar
            def _(act):
                act.sem_inc(bank_free, 8)
                with act.Fori(0, n // 4) as i:
                    for b in range(8):
                        wait_block(act, k, g0, made, i, b)
                        act.activation(hidden[:, bass.ds(8 * i + b, 1), :], ps[:, b:b + 1, :], ACT.Relu).then_inc(bank_free, 1)

            @block.vector
            def _(dve):
                with dve.Fori(0, n // 4) as i:
                    for b in range(8):
                        dve.wait_ge(bank_free, 8 * i + 8 + b + 1)
                        there = hidden[:, bass.ds(8 * i + b, 1), :]
                        dve.tensor_tensor(there, there, there, ALU.mult)


def swiglu_in(k, layer, hidden):
    nc, ps, name = k.nc, k.ps, f"gate_up{layer}"
    pairs, g0 = HID // PW, k.first_panel[name]
    with Phase(k, name) as f:
        gate = f.sb("gate", [P, 4, T])
        made, bank_free, gated = f.sem("made"), f.sem("bank_free"), f.sem("gated")
        with nc.Block() as block:

            @block.sync
            def _(sp):
                k.load_panels(sp, k.lookahead(name))

            @block.tensor
            def _(pe):
                stream_columns(pe, k, name, k.hT, ps, made, bank_free, need=lambda b: 4 * (b // 4) + 2 + 2 * (b % 2))

            @block.scalar
            def _(act):
                def pair(i, h):
                    for m in range(2):
                        wait_block(act, k, g0, made, i, 4 * h + m)
                        act.wait_ge(bank_free, 8 * i + 4 * h + 2 + 2 * m)
                        act.activation(gate[:, 2 * h + m, :], ps[:, 4 * h + m, :], ACT.Silu).then_inc(gated, 1)

                with act.Fori(0, pairs // 2) as i:
                    for h in range(2):
                        pair(i, h)
                pair(pairs // 2, 0)

            @block.vector
            def _(dve):
                dve.sem_inc(bank_free, 8)

                def pair(i, h):
                    for m in range(2):
                        wait_block(dve, k, g0, made, i, 4 * h + 2 + m)
                        dve.wait_ge(gated, 4 * i + 2 * h + m + 1)
                        dve.tensor_tensor(hidden[:, bass.ds(4 * i + 2 * h + m, 1), :], gate[:, 2 * h + m:2 * h + m + 1, :],
                                          ps[:, 4 * h + 2 + m:4 * h + 3 + m, :], ALU.mult).then_inc(bank_free, 2)

                with dve.Fori(0, pairs // 2) as i:
                    for h in range(2):
                        pair(i, h)
                pair(pairs // 2, 0)



class Steps:

    def __init__(self, f, name, steps):
        self.sem, self.n, self.at = f.sem(name), len(steps), {s: i for i, s in enumerate(steps)}
        self.next = 0

    def begin(self, eng):
        eng.sem_inc(self.sem, self.n)

    def did(self, name, ins):
        if self.at[name] != self.next % self.n:
            raise ValueError(f"step {name} out of order")
        self.next += 1
        ins.then_inc(self.sem, 1)

    def wait(self, eng, name, rnd, back=0):
        eng.wait_ge(self.sem, self.n * rnd + (self.n * (1 - back) + self.at[name] + 1))


SLAB_R, SLAB_K, SLAB_V, SLAB_WA, SLAB_G, SLAB_Q = 0, 6, 12, 18, 19, 20


def decay_and_rate(k, slab, lw, rate):
    nc, ps, ins = k.nc, k.ps, k.ins
    with Phase(k, "lora") as f:
        low = f.sb("weights", [P, MIX])
        landed, squashed, made, done = f.sem("landed"), f.sem("squashed"), f.sem("made"), f.sem("done")
        w0, a0 = (k.col_a[:, ROW_A[n]:ROW_A[n] + PAIRS] for n in ("rw_w0", "rw_a0"))
        with nc.Block() as block:

            @block.sync
            def _(sp):
                sp.dma_start(low[0:HD, :], ins["rw_w2"][0]).then_inc(landed, 16)
                sp.dma_start(low[HD:P, :], ins["rw_a2"][0]).then_inc(landed, 16)

            @block.scalar
            def _(act):
                act.activation(slab[0:HD, SLAB_WA, :], slab[0:HD, SLAB_WA, :], ACT.Tanh).then_inc(squashed, 1)
                for p in range(PAIRS):
                    act.wait_ge(made, 2 * p + 1)
                    act.activation(lw[:, p, :], ps[:, 2 * (p % 4), :], ACT.Sigmoid, bias=w0[:, p:p + 1]).then_inc(done, 1)
                    act.wait_ge(made, 2 * p + 2)
                    act.activation(rate[:, p, :], ps[:, 2 * (p % 4) + 1, :], ACT.Sigmoid, bias=a0[:, p:p + 1]).then_inc(done, 1)
                act.activation(slab[:, SLAB_G, :], slab[:, SLAB_G, :], ACT.Sigmoid)

            @block.tensor
            def _(pe):
                pe.wait_ge(landed, 32)
                pe.wait_ge(squashed, 1)
                for p in range(PAIRS):
                    for half in range(2):
                        if p >= 4:
                            pe.wait_ge(done, 2 * (p - 4) + half + 1)
                        rows = slice(half * HD, (half + 1) * HD)
                        pe.matmul(ps[:, 2 * (p % 4) + half, :], low[rows, p * P:(p + 1) * P], slab[rows, SLAB_WA, :],
                                  start=True, stop=True).then_inc(made, 1)


LEVELS = range(1, 6)
PREP_ACT = ["k_squared", "v_still", "kk_log", "kk_root", "e_pos", "e_neg", "e_prev", "pass"]
PREP_DVE = ["cum", "k_part", "k_new", "kk_clip", "kk", "rk", "ah", "bonus", "rh_kept"]
PREP_POOL = ["mid", "mid_prev", "ends", "passes", "b", "bh", "kh", "rh"]
PREP_PE = ["kk_sum", "rk_sum"]


def main_steps():
    both = range(2)
    act = [f"tok{q}" for q in range(TT)] + [f"ab{e}" for e in both]
    dve = [f"{n}{e}" for e in both for n in ("inv_T", "rb")] + [f"{n}{e}" for e in both for n in ("ak", "rk")]
    pool = [f"{n}{e}" for e in both for n in ("inv", "inv_eye", "inv_T_eye", "below1_")]
    pe = [f"turn{q}" for q in range(TT)] + [f"a1_{e}" for e in both] + [f"a2_{e}" for e in both]
    for lv in LEVELS:
        pe += [f"x{e}_{lv}" for e in both] + [f"tm{e}_{lv}" for e in both]
        act += [f"x{e}_{lv}" for e in both]
        dve += [f"{n}{e}_{lv}" for e in both for n in (("t", "m") if lv < 5 else ("m",))]
        pool += [f"below{lv + 1}_{e}" for e in both if lv < 5]
    pe += [f"{n}{e}" for n in ("av", "wu") for e in both] + ["out"]
    act += [f"{n}{e}" for n in ("a_side", "av", "wu") for e in both] + ["h", "y"]
    dve += ["g", "q"]
    return act, dve, pool, pe


def scan_chunks(k, slab, lw, rate, passes):
    nc, ps = k.nc, k.ps
    cols = {n: k.col_a[:, ROW_A[n]:ROW_A[n] + PAIRS] for n in ("rw_k_k", "rw_k_a", "rw_r_k")}
    with Phase(k, "scan") as f:
        sq, rn, kk, kn, cum, mid, prev, e_pos = (k.hT[:, i, :] for i in range(8))
        rk_sum, v_st, ah, bh, kh, rh = (f.sb(s, [P, T]) for s in ("rk", "v", "ah", "bh", "kh", "rh"))
        tok = f.sb("tok", [P, TT, 4, P])
        ends = f.sb("ends", [P, NCH - 1])

        def two(name):
            return [f.sb(f"{name}{e}", [P, TT, P]) for e in range(2)]

        ab, below, inv, inv_T, x, ak_T, rb_T, rk_T = (two(s) for s in ("ab", "below", "inv", "inv_T", "x", "ak", "rb", "rkT"))
        a_av, w_u = below, x
        act_s, dve_s, pool_s, pe_s = (Steps(f, n, s) for n, s in zip(
            ("act_done", "vector_done", "pool_done", "tensor_done"), main_steps()))
        act_p, dve_p, pool_p, pe_p = (Steps(f, n, s) for n, s in zip(
            ("act_prepared", "vector_prepared", "pool_prepared", "tensor_prepared"),
            (PREP_ACT, PREP_DVE, PREP_POOL, PREP_PE)))

        def blk(t, i):
            return t[:, i, :] if isinstance(i, int) else t[:, bass.ds(i, 1), :].rearrange("p a t -> p (a t)")

        def col(t, i):
            return t[:, i:i + 1] if isinstance(i, int) else t[:, bass.ds(i, 1)]

        def per_chunk(t):
            return t.rearrange("p (c t) -> p c t", c=NCH)

        def tiles(t):
            return t.rearrange("p (q t) -> p q t", q=TT)

        def on_tiles(mask):
            return mask[:].unsqueeze(1).broadcast_to([P, TT, P])

        def pair_of(bank, which):
            return ps[:, bank:bank + 2, :].rearrange("p b (q w t) -> p (b q) w t", q=2, w=2)[:, :, which, :]

        def four(bank):
            return ps[:, bank, :].rearrange("p (q t) -> p q t", q=TT)

        def by_parity(t):
            return t.rearrange("p (q c k) -> p c q k", c=2, k=HD)

        def halves(bank):
            return ps[:, bank:bank + 2, 0:TT * HD].rearrange("p c (q k) -> p c q k", q=TT)

        mids = per_chunk(cum)[:, :, CH // 2 - 1:CH // 2]

        with nc.Block() as block:

            @block.scalar
            def _(act):
                act_s.begin(act)
                act_p.begin(act)

                def prep(p, slot):
                    if slot == 1:
                        pe_p.wait(act, "kk_sum", p, 1)
                        act_p.did("k_squared", act.activation(sq, blk(slab, SLAB_K + p), ACT.Square, scale=col(cols["rw_k_k"], p)))
                        pe_s.wait(act, "turn3", p, 1)
                        dve_p.wait(act, "bonus", p, 1)
                        act_p.did("v_still", act.copy(v_st[:], blk(slab, SLAB_V + p)))
                    if slot == 2:
                        dve_p.wait(act, "kk_clip", p)
                        act_p.did("kk_log", act.activation(rn, rn, ACT.Ln, scale=KK_SCALE))
                        act_p.wait(act, "kk_log", p)
                        act_p.did("kk_root", act.activation(rn, rn, ACT.Exp, scale=-0.5, bias=k.eps[:, 2:3]))
                    if slot == 3:
                        pool_p.wait(act, "mid", p)
                        dve_p.wait(act, "rh_kept", p, 1)
                        act_p.did("e_pos", act.activation(e_pos, mid, ACT.Exp, scale=-LOG_DECAY))
                        pool_p.wait(act, "mid_prev", p)
                        act_p.wait(act, "e_pos", p)
                        act_p.did("e_neg", act.activation(mid, mid, ACT.Exp, scale=LOG_DECAY))
                        act_p.did("e_prev", act.activation(prev, prev, ACT.Exp, scale=-LOG_DECAY))
                        pool_p.wait(act, "passes", p)
                        act_p.did("pass", act.activation(blk(passes, p), ends[:], ACT.Exp, scale=-LOG_DECAY))

                def main(p, prep_next):
                    for q in range(TT):
                        pe_s.wait(act, f"turn{q}", p)
                        if q == 0:
                            pe_s.wait(act, "out", p, 1)
                        act_s.did(f"tok{q}", act.copy(tok[:, q, :, :], four((6, 4, 5, 6)[q])))
                    for e in range(2):
                        pe_s.wait(act, f"a1_{e}", p)
                        pool_s.wait(act, f"below5_{e}", p, 1)
                        act_s.did(f"ab{e}", act.copy(ab[e][:], four(3 * e)))
                    for lv in LEVELS:
                        for e in range(2):
                            pe_s.wait(act, f"x{e}_{lv}", p)
                            act_s.did(f"x{e}_{lv}", act.copy(x[e][:], four(3 * e)))
                        if prep_next and lv < 5:
                            prep(p + 1, lv)
                    for e in range(2):
                        act_s.wait(act, "tok3", p)
                        act_s.did(f"a_side{e}", act.copy(a_av[e][:, :, 0:HD], tok[:, :, 0, e * HD:(e + 1) * HD]))
                    for e in range(2):
                        pe_s.wait(act, f"av{e}", p)
                        act_s.did(f"av{e}", act.copy(a_av[e][:, :, HD:P], ps[:, 3 * e, 0:TT * HD].rearrange("p (q v) -> p q v", q=TT)))
                    for e in range(2):
                        pe_s.wait(act, f"wu{e}", p)
                        act_s.did(f"wu{e}", act.copy(w_u[e][:], four(3 * e + 1)))
                    pe_s.wait(act, "out", p)
                    act_s.did("h", act.copy(by_parity(blk(rate, p)), halves(4)))
                    act_s.did("y", act.copy(blk(slab, SLAB_K + p), ps[:, 3, :]))

                for slot in range(1, 5):
                    prep(0, slot)
                with act.Fori(0, PAIRS - 1) as p:
                    main(p, True)
                main(PAIRS - 1, False)

            @block.vector
            def _(dve):
                dve_s.begin(dve)
                dve_p.begin(dve)

                def prep(p, slot):
                    if slot == 1:
                        pool_p.wait(dve, "passes", p, 1)
                        dve_p.did("cum", dve.tensor_tensor_scan(cum, k.restart[:], blk(lw, p), 0.0, ALU.mult, ALU.add))
                        pool_p.wait(dve, "kh", p, 1)
                        dve_p.wait(dve, "rk", p, 1)
                        dve_p.did("k_part", dve.scalar_tensor_tensor(kn, blk(rate, p), 1.0, blk(slab, SLAB_K + p), ALU.subtract, ALU.mult))
                        dve_p.wait(dve, "k_part", p)
                        dve_p.did("k_new", dve.scalar_tensor_tensor(kn, kn, col(cols["rw_k_a"], p), blk(slab, SLAB_K + p), ALU.mult, ALU.add))
                    if slot == 2:
                        pe_p.wait(dve, "kk_sum", p)
                        dve_p.wait(dve, "kk", p, 1)
                        dve_p.did("kk_clip", dve.tensor_scalar(rn, ps[:, 7, :], 1e-24, None, ALU.max))
                    if slot == 3:
                        act_p.wait(dve, "kk_root", p)
                        pool_p.wait(dve, "b", p, 1)
                        dve_p.wait(dve, "ah", p, 1)
                        dve_p.did("kk", dve.scalar_tensor_tensor(kk, blk(slab, SLAB_K + p), col(cols["rw_k_k"], p), rn, ALU.mult, ALU.mult))
                        pe_p.wait(dve, "rk_sum", p, 1)
                        dve_p.wait(dve, "k_new", p)
                        dve_p.did("rk", dve.scalar_tensor_tensor(rk_sum[:], blk(slab, SLAB_R + p), col(cols["rw_r_k"], p), kn, ALU.mult, ALU.mult))
                    if slot == 4:
                        act_p.wait(dve, "e_prev", p)
                        dve_p.wait(dve, "kk", p)
                        pe_s.wait(dve, "a2_1", p, 1)
                        dve_p.did("ah", dve.scalar_tensor_tensor(ah[:], kk, -1.0, prev, ALU.mult, ALU.mult))
                        pe_p.wait(dve, "rk_sum", p)
                        act_p.wait(dve, "v_still", p)
                        dve_p.did("bonus", dve.tensor_tensor(blk(slab, SLAB_V + p), ps[:, 7, :], v_st[:], ALU.mult))
                        pool_p.wait(dve, "rh", p)
                        dve_p.wait(dve, "rk", p)
                        dve_p.did("rh_kept", dve.tensor_tensor(blk(slab, SLAB_R + p), blk(slab, SLAB_R + p), e_pos, ALU.mult))

                def main(p, prep_next):
                    for e in range(2):
                        pe_s.wait(dve, f"a1_{e}", p)
                        dve_s.did(f"inv_T{e}", dve.tensor_tensor(inv_T[e][:], pair_of(3 * e + 1, 0), on_tiles(k.level0_T), ALU.mult))
                        pe_s.wait(dve, "out", p, 1)
                        dve_s.did(f"rb{e}", dve.tensor_tensor(rb_T[e][:], pair_of(3 * e + 1, 1), on_tiles(k.upto_T), ALU.mult))
                    for e in range(2):
                        pe_s.wait(dve, f"a2_{e}", p)
                        dve_s.did(f"ak{e}", dve.tensor_tensor(ak_T[e][:], pair_of(3 * e + 1, 0), on_tiles(k.before_T), ALU.mult))
                        dve_s.did(f"rk{e}", dve.tensor_tensor(rk_T[e][:], pair_of(3 * e + 1, 1), on_tiles(k.upto_T), ALU.mult))
                    for lv in LEVELS:
                        for e in range(2):
                            pe_s.wait(dve, f"tm{e}_{lv}", p)
                            if lv == 1:
                                pool_s.wait(dve, f"inv_T_eye{e}", p)
                            if lv < 5:
                                dve_s.did(f"t{e}_{lv}", dve.tensor_tensor(inv[e][:], four(3 * e + 1), inv[e][:], ALU.add))
                            if lv > 1:
                                dve_s.wait(dve, f"m{e}_{lv - 1}", p)
                            dve_s.did(f"m{e}_{lv}", dve.tensor_tensor(inv_T[e][:], four(3 * e + 2), inv_T[e][:], ALU.add))
                        if prep_next and lv < 5:
                            prep(p + 1, lv)
                    pe_s.wait(dve, "out", p)
                    eye = k.eye64[:].unsqueeze(1).unsqueeze(1).broadcast_to([P, 2, TT, HD])
                    dve_s.did("g", dve.tensor_tensor(by_parity(blk(lw, p)), halves(0), eye, ALU.add))
                    dve_p.wait(dve, "rh_kept", p)
                    dve_s.did("q", dve.tensor_tensor(blk(slab, SLAB_R + p), ps[:, 2, :], blk(slab, SLAB_R + p), ALU.add))

                for slot in range(1, 5):
                    prep(0, slot)
                with dve.Fori(0, PAIRS - 1) as p:
                    main(p, True)
                main(PAIRS - 1, False)

            @block.gpsimd
            def _(pool):
                pool_s.begin(pool)
                pool_p.begin(pool)

                def prep(p, slot):
                    if slot == 2:
                        dve_p.wait(pool, "cum", p)
                        pool_p.wait(pool, "bh", p, 1)
                        pool_p.wait(pool, "kh", p, 1)
                        pool_p.did("mid", pool.tensor_tensor(per_chunk(mid), per_chunk(cum), mids.broadcast_to([P, NCH, CH]), ALU.subtract))
                        pool_p.wait(pool, "mid", p)
                        dve_p.wait(pool, "ah", p, 1)
                        pool_p.did("mid_prev", pool.tensor_tensor(prev, mid, blk(lw, p), ALU.subtract))
                        act_p.wait(pool, "pass", p, 1)
                        pool_p.did("ends", pool.tensor_tensor(ends[:].unsqueeze(2), per_chunk(cum)[:, 0:NCH - 1, CH - 1:CH], mids[:, 0:NCH - 1], ALU.subtract))
                        pool_p.wait(pool, "ends", p)
                        pool_p.did("passes", pool.tensor_tensor(ends[:].unsqueeze(2), ends[:].unsqueeze(2), mids[:, 1:NCH], ALU.add))
                    if slot == 3:
                        dve_p.wait(pool, "kk", p)
                        pe_s.wait(pool, "a2_1", p, 1)
                        pool_p.did("b", pool.tensor_tensor(bh[:], kk, blk(rate, p), ALU.mult))
                        act_p.wait(pool, "e_neg", p)
                        pool_p.wait(pool, "b", p)
                        pool_p.did("bh", pool.tensor_tensor(bh[:], bh[:], mid, ALU.mult))
                        dve_p.wait(pool, "k_new", p)
                        pool_p.did("kh", pool.tensor_tensor(kh[:], kn, mid, ALU.mult))
                    if slot == 4:
                        act_p.wait(pool, "e_pos", p)
                        pool_p.did("rh", pool.tensor_tensor(rh[:], blk(slab, SLAB_R + p), e_pos, ALU.mult))

                def main(p, prep_next):
                    for e in range(2):
                        act_s.wait(pool, f"ab{e}", p)
                        pool_s.did(f"inv{e}", pool.tensor_tensor(inv[e][:], ab[e][:], on_tiles(k.level[:, 0, :]), ALU.mult))
                        pool_s.wait(pool, f"inv{e}", p)
                        pool_s.did(f"inv_eye{e}", pool.tensor_tensor(inv[e][:], inv[e][:], on_tiles(k.ident), ALU.add))
                        dve_s.wait(pool, f"inv_T{e}", p)
                        pool_s.did(f"inv_T_eye{e}", pool.tensor_tensor(inv_T[e][:], inv_T[e][:], on_tiles(k.ident), ALU.add))
                        pe_s.wait(pool, f"wu{e}", p, 1)
                        pool_s.did(f"below1_{e}", pool.tensor_tensor(below[e][:], ab[e][:], on_tiles(k.level[:, 1, :]), ALU.mult))
                    for lv in range(1, 5):
                        for e in range(2):
                            pe_s.wait(pool, f"x{e}_{lv}", p)
                            pool_s.did(f"below{lv + 1}_{e}", pool.tensor_tensor(below[e][:], ab[e][:], on_tiles(k.level[:, lv + 1, :]), ALU.mult))
                        if prep_next:
                            prep(p + 1, lv)

                for slot in range(1, 5):
                    prep(0, slot)
                with pool.Fori(0, PAIRS - 1) as p:
                    main(p, True)
                main(PAIRS - 1, False)

            @block.tensor
            def _(pe):
                pe_s.begin(pe)
                pe_p.begin(pe)

                def mm(out, lhsT, rhs, start=True, stop=True):
                    return pe.matmul(out, lhsT, rhs, start=start, stop=stop)

                def prep(p, slot):
                    if slot == 1:
                        act_p.wait(pe, "k_squared", p)
                        dve_p.wait(pe, "bonus", p, 1)
                        pe_p.did("kk_sum", mm(ps[:, 7, :], k.head_ones[:], sq))
                    if slot == 4:
                        dve_p.wait(pe, "kk_clip", p)
                        dve_p.wait(pe, "rk", p)
                        pe_p.did("rk_sum", mm(ps[:, 7, :], k.head_ones[:], rk_sum[:]))

                def main(p, prep_next):
                    dve_p.wait(pe, "ah", p)
                    pool_p.wait(pe, "rh", p)
                    act_p.wait(pe, "v_still", p)
                    act_s.wait(pe, "tok3", p, 1)
                    for q in range(TT):
                        if q == 1:
                            act_s.wait(pe, "h", p, 1)
                            dve_s.wait(pe, "g", p, 1)
                        if q == 3:
                            act_s.wait(pe, "tok0", p)
                        for n, src in enumerate((ah, bh, kh, v_st)):
                            last = pe.transpose(ps[:, (6, 4, 5, 6)[q], n * P:(n + 1) * P], src[:, q * P:(q + 1) * P], k.ident[:])
                        pe_s.did(f"turn{q}", last)
                    act_s.wait(pe, "y", p, 1)
                    dve_s.wait(pe, "q", p, 1)
                    for e in range(2):
                        rows = slice(e * HD, (e + 1) * HD)
                        if e == 1:
                            act_s.wait(pe, "tok3", p)
                        for q in range(TT):
                            at = slice(q * P, (q + 1) * P)
                            mm(ps[:, 3 * e, at], ah[rows, at], bh[rows, at])
                        for q in range(TT):
                            at, bank, c = slice(q * P, (q + 1) * P), 3 * e + 1 + q // 2, (q % 2) * 2 * P
                            mm(ps[:, bank, c:c + P], bh[rows, at], ah[rows, at])
                            last = mm(ps[:, bank, c + P:c + 2 * P], bh[rows, at], rh[rows, at])
                        pe_s.did(f"a1_{e}", last)
                    for e in range(2):
                        rows = slice(e * HD, (e + 1) * HD)
                        dve_s.wait(pe, f"rb{e}", p)
                        for q in range(TT):
                            at, bank, c = slice(q * P, (q + 1) * P), 3 * e + 1 + q // 2, (q % 2) * 2 * P
                            mm(ps[:, bank, c:c + P], kh[rows, at], ah[rows, at])
                            last = mm(ps[:, bank, c + P:c + 2 * P], kh[rows, at], rh[rows, at])
                        pe_s.did(f"a2_{e}", last)
                    for lv in LEVELS:
                        for e in range(2):
                            pool_s.wait(pe, f"below{lv}_{e}", p)
                            if lv == 1:
                                act_s.wait(pe, f"ab{e}", p)
                            else:
                                act_s.wait(pe, f"x{e}_{lv - 1}", p)
                                dve_s.wait(pe, f"m{e}_{lv - 1}", p)
                            for q in range(TT):
                                last = mm(ps[:, 3 * e, q * P:(q + 1) * P], below[e][:, q, :], inv_T[e][:, q, :])
                            pe_s.did(f"x{e}_{lv}", last)
                        for e in range(2):
                            act_s.wait(pe, f"x{e}_{lv}", p)
                            if lv == 1:
                                dve_s.wait(pe, f"rk{e}", p)
                            for q in range(TT):
                                at = slice(q * P, (q + 1) * P)
                                if lv < 5:
                                    mm(ps[:, 3 * e + 1, at], x[e][:, q, :], inv[e][:, q, :])
                                last = mm(ps[:, 3 * e + 2, at], inv[e][:, q, :], x[e][:, q, :])
                            pe_s.did(f"tm{e}_{lv}", last)
                        if prep_next and lv < 5:
                            prep(p + 1, lv)
                    for e in range(2):
                        for q in range(TT):
                            last = mm(ps[:, 3 * e, q * HD:(q + 1) * HD], ak_T[e][:, q, :], tok[:, q, 3, e * HD:(e + 1) * HD])
                        pe_s.did(f"av{e}", last)
                    for e in range(2):
                        act_s.wait(pe, f"av{e}", p)
                        dve_s.wait(pe, f"m{e}_5", p)
                        for q in range(TT):
                            last = mm(ps[:, 3 * e + 1, q * P:(q + 1) * P], inv_T[e][:, q, :], a_av[e][:, q, :])
                        pe_s.did(f"wu{e}", last)
                    for e in range(2):
                        act_s.wait(pe, f"wu{e}", p)
                        if e == 0:
                            act_s.wait(pe, "wu1", p)
                        rows, w, u = slice(e * HD, (e + 1) * HD), slice(0, HD), slice(HD, P)
                        for q in range(TT):
                            at = slice(q * P, (q + 1) * P)
                            mm(ps[rows, 2, at], w_u[e][:, q, w], rb_T[e][:, q, :])
                            mm(ps[rows, 3, at], w_u[e][:, q, u], rb_T[e][:, q, :], stop=False)
                            mm(ps[rows, 3, at], tok[:, q, 3, rows], rk_T[e][:, q, :], start=False)
                            for c in range(2):
                                cs, to = slice(c * CH, (c + 1) * CH), slice(q * HD, (q + 1) * HD)
                                mm(ps[rows, c, to], w_u[e][cs, q, w], tok[cs, q, 1, rows])
                                mm(ps[rows, 4 + c, to], tok[cs, q, 1, rows], w_u[e][cs, q, u], stop=False)
                                last = mm(ps[rows, 4 + c, to], tok[cs, q, 2, rows], tok[cs, q, 3, rows], start=False)
                    pe_s.did("out", last)

                for slot in range(1, 5):
                    prep(0, slot)
                with pe.Fori(0, PAIRS - 1) as p:
                    main(p, True)
                main(PAIRS - 1, False)


def scan_states(k, slab, lw, rate, passes):
    nc, ps = k.nc, k.ps
    with Phase(k, "states") as f:
        state = f.sb("state", [P, NCH - 1, PAIRS, HD])
        moved, grown, passed, read, added = (f.sem(s) for s in ("moved", "grown", "passed", "read", "added"))

        def chunk(t, n, pairs=slice(0, PAIRS)):
            return t[:, pairs, n * CH:(n + 1) * CH]

        with nc.Block() as block:

            @block.tensor
            def _(pe):
                def outputs(n):
                    for p in range(PAIRS):
                        for e in range(2):
                            rows = slice(e * HD, (e + 1) * HD)
                            last = pe.matmul(ps[rows, 2 + p, (n + 1) * CH:(n + 2) * CH], state[rows, n, p, :],
                                             slab[rows, SLAB_R + p, (n + 1) * CH:(n + 2) * CH], start=True, stop=True)
                    last.then_inc(read, 1)

                for n in range(NCH - 2):
                    pe.wait_ge(passed, n + 1)
                    if n >= 2:
                        pe.wait_ge(grown, n - 1)
                    for p in range(PAIRS):
                        for e in range(2):
                            rows = slice(e * HD, (e + 1) * HD)
                            last = pe.matmul(ps[rows, n % 2, p * HD:(p + 1) * HD], lw[rows, p, (n + 1) * CH:(n + 2) * CH],
                                             state[rows, n, p, :], start=True, stop=True)
                    last.then_inc(moved, 1)
                    outputs(n)
                pe.wait_ge(passed, NCH - 1)
                outputs(NCH - 2)

            @block.vector
            def _(dve):
                def by_pass(n):
                    return passes[:, :, n:n + 1].broadcast_to([P, PAIRS, HD])

                dve.tensor_tensor(state[:, 0], chunk(rate, 0), by_pass(0), ALU.mult).then_inc(passed, 1)
                for n in range(1, NCH - 1):
                    dve.wait_ge(moved, n)
                    dve.tensor_tensor(state[:, n], ps[:, (n - 1) % 2, 0:PAIRS * HD].rearrange("p (h v) -> p h v", h=PAIRS),
                                      chunk(rate, n), ALU.add).then_inc(grown, 1)
                    dve.wait_ge(grown, n)
                    dve.tensor_tensor(state[:, n], state[:, n], by_pass(n), ALU.mult).then_inc(passed, 1)
                dve.wait_ge(read, NCH - 1)
                for p in range(PAIRS):
                    y = slab[:, SLAB_K + p, CH:T]
                    dve.tensor_tensor(y, ps[:, 2 + p, CH:T], y, ALU.add)


def rwkv_out(k, slab):
    nc, ps, ins = k.nc, k.ps, k.ins
    gain, shift = (k.col_a[:, ROW_A[n]:ROW_A[n] + PAIRS] for n in ("rw_lnx_g", "rw_lnx_b"))
    with Phase(k, "rwkv_out") as f:
        g2, mean_of = f.sb("g2", [P, MIX]), f.sb("mean_of", [P, P])
        logs, rstd, out = f.sb("logs", [P, 2, T]), f.sb("rstd", [P, 2, T]), k.hT
        landed, meant, averaged, centred, squared, spread, logged, rooted, scaled, shifted, gated = (f.sem(s) for s in (
            "landed", "meant", "averaged", "centred", "squared", "spread", "logged", "rooted", "scaled", "shifted", "gated"))
        with nc.Block() as block:

            @block.sync
            def _(sp):
                sp.dma_start(g2[:], ins["rw_g2"][0]).then_inc(landed, 16)

            @block.tensor
            def _(pe):
                pe.wait_ge(landed, 16)
                pe.wait_ge(meant, 1)

                def mean(p):
                    if p >= 2:
                        pe.wait_ge(centred, p - 1)
                    pe.matmul(ps[:, p % 2, :], mean_of[:], slab[:, SLAB_K + p, :], start=True, stop=True).then_inc(averaged, 1)

                mean(0)
                for p in range(PAIRS):
                    if p + 1 < PAIRS:
                        mean(p + 1)
                    pe.wait_ge(squared, p + 1)
                    if p >= 2:
                        pe.wait_ge(logged, p - 1)
                    pe.matmul(ps[:, 2 + p % 2, :], mean_of[:], out[:, p, :], start=True, stop=True).then_inc(spread, 1)
                    if p >= 2:
                        pe.wait_ge(gated, p - 1)
                    pe.matmul(ps[:, 4 + p % 2, :], g2[:, p * P:(p + 1) * P], slab[:, SLAB_G, :], start=True, stop=True)\
                        .then_inc(spread, 1)

            @block.vector
            def _(dve):
                dve.tensor_scalar(mean_of[:], k.head_ones[:], 1.0 / HD, None, ALU.mult).then_inc(meant, 1)

                def centre(p):
                    dve.wait_ge(averaged, p + 1)
                    y = slab[:, SLAB_K + p, :]
                    dve.tensor_tensor(y, y, ps[:, p % 2, :], ALU.subtract).then_inc(centred, 1)

                centre(0)
                for p in range(PAIRS):
                    if p + 1 < PAIRS:
                        centre(p + 1)
                    y = slab[:, SLAB_K + p, :]
                    dve.wait_ge(rooted, p + 1)
                    dve.scalar_tensor_tensor(y, y, gain[:, p:p + 1], rstd[:, p % 2, :], ALU.mult, ALU.mult).then_inc(scaled, 1)
                    dve.wait_ge(scaled, p + 1)
                    dve.scalar_tensor_tensor(y, y, shift[:, p:p + 1], slab[:, SLAB_V + p, :], ALU.add, ALU.add).then_inc(shifted, 1)
                    dve.wait_ge(shifted, p + 1)
                    dve.wait_ge(spread, 2 * p + 2)
                    dve.tensor_tensor(out[:, p, :], y, ps[:, 4 + p % 2, :], ALU.mult).then_inc(gated, 1)

            @block.scalar
            def _(act):
                for p in range(PAIRS):
                    act.wait_ge(centred, p + 1)
                    act.activation(out[:, p, :], slab[:, SLAB_K + p, :], ACT.Square).then_inc(squared, 1)
                    act.wait_ge(spread, 2 * p + 1)
                    if p >= 2:
                        act.wait_ge(rooted, p - 1)
                    act.activation(logs[:, p % 2, :], ps[:, 2 + p % 2, :], ACT.Ln, bias=k.eps[:, 1:2]).then_inc(logged, 1)
                    act.wait_ge(logged, p + 1)
                    if p >= 2:
                        act.wait_ge(scaled, p - 1)
                    act.activation(rstd[:, p % 2, :], logs[:, p % 2, :], ACT.Exp, scale=-0.5).then_inc(rooted, 1)


def memory_attention(k, slab):
    nc, ps = k.nc, k.ps
    gain = k.col_a[:, ROW_A["mem_q_norm_g"]:ROW_A["mem_q_norm_g"] + 1]
    heads, scale = 4, HD ** -0.5
    with Phase(k, "mem_attn") as f:
        q, squares, logs, rstd = (f.sb(s, [P, 2, T]) for s in ("q", "squares", "logs", "rstd"))
        probs = f.sb("probs", [P, 2, TT, M])
        probs_T = f.sb("probs_T", [P, 2, 2, T])
        top, total, inv = (f.sb(s, [P, heads, TT]) for s in ("top", "total", "inv"))
        squared, summed, logged, rooted, normed = (f.sem(s) for s in ("squared", "summed", "logged", "rooted", "normed"))
        scored, topped, negated, exped, inverted, scaled, turned, copied, mixed, kept = (f.sem(s) for s in (
            "scored", "topped", "negated", "exped", "inverted", "scaled", "turned", "copied", "mixed", "kept"))
        with nc.Block() as block:

            @block.tensor
            def _(pe):
                pe.wait_ge(squared, 1)
                for m in range(2):
                    last = pe.matmul(ps[:, m, :], k.head_ones[:], squares[:, m, :], start=True, stop=True)
                last.then_inc(summed, 1)
                pe.wait_ge(normed, 1)

                def scores(h):
                    rows = slice((h % 2) * HD, (h % 2 + 1) * HD)
                    if h:
                        pe.wait_ge(exped, TT * h)
                    for t in range(TT):
                        last = pe.matmul(ps[:, 2 + t // 2, (t % 2) * M:(t % 2 + 1) * M], q[rows, h // 2, t * P:(t + 1) * P],
                                         k.k_mem[rows, h // 2, :], start=True, stop=True)
                    last.then_inc(scored, 1)

                scores(0)
                for h in range(heads):
                    if h + 1 < heads:
                        scores(h + 1)
                    pe.wait_ge(scaled, h + 1)
                    if h:
                        pe.wait_ge(copied, h)
                    for m in range(2):
                        for t in range(TT):
                            last = pe.transpose(ps[:, 4 + m, t * P:(t + 1) * P], probs[:, h % 2, t, m * P:(m + 1) * P], k.ident[:])
                    last.then_inc(turned, 1)
                    pe.wait_ge(copied, h + 1)
                    if h >= 2:
                        pe.wait_ge(kept, h - 1)
                    rows = slice((h % 2) * HD, (h % 2 + 1) * HD)
                    for m in range(2):
                        last = pe.matmul(ps[rows, 6 + h % 2, :], k.v_mem[:, m, h * HD:(h + 1) * HD], probs_T[:, h % 2, m, :],
                                         start=m == 0, stop=m == 1)
                    last.then_inc(mixed, 1)

            @block.scalar
            def _(act):
                act.activation(squares[:], slab[:, SLAB_Q:SLAB_Q + 2, :], ACT.Square).then_inc(squared, 1)
                act.wait_ge(summed, 1)
                act.activation(logs[:], ps[:, 0:2, :], ACT.Ln, bias=k.eps[:, 0:1], scale=1.0 / HD).then_inc(logged, 1)
                act.wait_ge(logged, 1)
                act.activation(rstd[:], logs[:], ACT.Exp, scale=-0.5).then_inc(rooted, 1)
                for h in range(heads):
                    act.wait_ge(negated, h + 1)
                    if h >= 2:
                        act.wait_ge(turned, h - 1)
                    for t in range(TT):
                        act.activation(probs[:, h % 2, t, :], ps[:, 2 + t // 2, (t % 2) * M:(t % 2 + 1) * M], ACT.Exp,
                                       bias=top[:, h, t:t + 1], scale=scale, accum_out=total[:, h, t:t + 1]).then_inc(exped, 1)
                    act.wait_ge(turned, h + 1)
                    if h >= 2:
                        act.wait_ge(mixed, h - 1)
                    act.copy(probs_T[:, h % 2], ps[:, 4:6, :]).then_inc(copied, 1)

            @block.vector
            def _(dve):
                dve.wait_ge(rooted, 1)
                dve.scalar_tensor_tensor(q[:], slab[:, SLAB_Q:SLAB_Q + 2, :], gain, rstd[:], ALU.mult, ALU.mult).then_inc(normed, 1)

                def tops(h):
                    dve.wait_ge(scored, h + 1)
                    dve.tensor_reduce(top[:, h, :], ps[:, 2:4, :].rearrange("p b (t m) -> p (b t) m", t=2), AX.X, ALU.max)\
                        .then_inc(topped, 1)
                    dve.wait_ge(topped, h + 1)
                    dve.tensor_scalar(top[:, h, :], top[:, h, :], -scale, None, ALU.mult).then_inc(negated, 1)

                tops(0)
                for h in range(heads):
                    dve.wait_ge(exped, TT * (h + 1))
                    dve.reciprocal(inv[:, h, :], total[:, h, :]).then_inc(inverted, 1)
                    if h + 1 < heads:
                        tops(h + 1)
                    dve.wait_ge(mixed, h + 1)
                    rows = slice((h % 2) * HD, (h % 2 + 1) * HD)
                    dve.tensor_copy(k.hT[rows, PAIRS + h // 2, :], ps[rows, 6 + h % 2, :]).then_inc(kept, 1)

            @block.gpsimd
            def _(pool):
                for h in range(heads):
                    pool.wait_ge(inverted, h + 1)
                    pool.tensor_tensor(probs[:, h % 2], probs[:, h % 2], inv[:, h, :].unsqueeze(2).broadcast_to([P, TT, M]),
                                       ALU.mult).then_inc(scaled, 1)


def rwkv_block(k):
    with Phase(k, "rwkv") as f:
        slab, lw, rate = f.sb("slab", [P, 22, T]), f.sb("lw", [P, PAIRS, T]), f.sb("rate", [P, PAIRS, T])
        passes = f.sb("passes", [P, PAIRS, NCH - 1])
        rwkv_in(k, slab)
        decay_and_rate(k, slab, lw, rate)
        scan_chunks(k, slab, lw, rate, passes)
        scan_states(k, slab, lw, rate, passes)
        rwkv_out(k, slab)
        memory_attention(k, slab)
    add_projection(k, "w_out", k.hT, (KT,))
    rms_norm(k, "ffn_norm", k.xT, k.col_a[:, ROW_A["norm_ffn_g"]:], k.hT)
    with Phase(k, "ffn") as f:
        hidden = f.sb("hidden", [P, 32, T])
        squared_relu_ffn_in(k, hidden)
        add_projection(k, "ff2", hidden, (8, 8, 8, 8))



FOX_H, NSA_H, GROUPS = 8, 8, 2
NCMP = T // 16 - 1
ATTN_WIDTHS = [PW] * 11 + [FOX_H, 24]


class Attention:

    def __init__(self, f):
        self.fq, self.fk = f.sb("fq", [P, 4, T]), f.sb("fk", [P, 4, T])
        self.fv = f.sb("fv", [P, TT, FOX_H * HD])
        self.nq = f.sb("nq", [P, 4, T])
        self.cmp_in = f.sb("cmp_in", [P, 2, T])
        self.ks, self.kw = f.sb("ks", [P, GROUPS, T]), f.sb("kw", [P, GROUPS, T])
        self.vs, self.vw = f.sb("vs", [P, TT, P]), f.sb("vw", [P, TT, P])
        self.kc, self.vc = f.sb("kc", [P, GROUPS, 32]), f.sb("vc", [32, GROUPS, HD])
        self.u = f.sb("forget_in", [FOX_H, T])
        self.gates = f.sb("gates", [P, TT, 24])
        self.forget = f.sb("forget", [P, FOX_H, T])
        self.alibi = f.sb("alibi", [P, NSA_H, T])
        self.cmp_dist = f.sb("cmp_dist", [P, TT, 32])
        self.future = f.sb("future", [P, P])


def attn_project(k, a):
    nc, ps, ins, g0 = k.nc, k.ps, k.ins, k.first_panel["attn_in"]
    n_pairs, n_all = 11, 24
    with Phase(k, "attn_in") as f:
        b_f, ks_raw, kw_raw = f.sb("b_f", [FOX_H, 1]), f.sb("ks_raw", [P, T]), f.sb("kw_raw", [P, T])
        landed, first, copied, doubled = f.sem("landed"), f.sem("first"), f.sem("copied"), f.sem("doubled")
        features = {0: (a.fq, 0, -0.125), 1: (a.fq, 2, -0.125), 2: (a.fk, 0, 1.0), 3: (a.fk, 2, 1.0),
                    6: (a.nq, 0, -0.125), 7: (a.nq, 2, -0.125), 8: (a.cmp_in, 0, 1.0)}
        with nc.Block() as block:

            @block.sync
            def _(sp):
                with nc.allow_non_contiguous_dma(reason="eight numbers"):
                    sp.dma_start(b_f[:], ins["fox_b_f_2"].rearrange("l h -> h l")).then_inc(landed, 16)
                k.load_panels(sp, k.lookahead("attn_in"))
                sp.wait_ge(copied, 21)
                for g in range(GROUPS):
                    for half in range(2):
                        for src, dst in ((ks_raw, a.ks), (kw_raw, a.kw)):
                            sp.dma_start(dst[half * HD:(half + 1) * HD, g, :], src[g * HD:(g + 1) * HD, :]).then_inc(doubled, 16)
                sp.wait_ge(doubled, 16 * 4 * GROUPS)

            @block.tensor
            def _(pe):
                def start(b, n):
                    w, landed_s, value = k.panel(g0, n // 4, n % 4, KT, ATTN_WIDTHS[n])
                    pe.wait_ge(landed_s, value)
                    if b >= 8:
                        pe.wait_ge(copied, b - 7)
                    return w

                def columns(b, n, m, width=P):
                    w = start(b, n)
                    for kt in range(KT):
                        last = pe.matmul(ps[0:width, b % 8, :], w[:, kt, m * P:m * P + width], k.hT[:, kt, :],
                                         start=kt == 0, stop=kt == KT - 1)
                    return last

                def tokens(b, n, c0, cols, tiles):
                    w = start(b, n)
                    for i, t in enumerate(tiles):
                        for kt in range(KT):
                            last = pe.matmul(ps[:, b % 8, i * cols:(i + 1) * cols], k.hT[:, kt, t * P:(t + 1) * P],
                                             w[:, kt, c0:c0 + cols], start=kt == 0, stop=kt == KT - 1)
                    return last

                for n in range(n_pairs):
                    for m in range(2):
                        b = 2 * n + m
                        if n in features or (n > 8 and m == 0):
                            last = columns(b, n, m)
                        elif n in (4, 5):
                            last = tokens(b, n, 0, PW, (2 * m, 2 * m + 1))
                        else:
                            last = tokens(b, n, P, P, range(TT))
                        last.then_inc(k.panel_used if m else first, 1)
                columns(22, 11, 0, FOX_H).then_inc(k.panel_used, 1)
                tokens(23, 12, 0, 24, range(TT)).then_inc(k.panel_used, 1)

            @block.scalar
            def _(act):
                for b in range(n_all):
                    n, m, bank = b // 2, b % 2, ps[:, b % 8, :]
                    if b >= 2 * n_pairs:
                        act.wait_ge(k.panel_used, g0 + n_pairs + b - 2 * n_pairs + 1)
                    elif m:
                        act.wait_ge(k.panel_used, g0 + n + 1)
                    else:
                        act.wait_ge(first, n + 1)
                    if b == 22:
                        act.wait_ge(landed, 16)
                        made = act.activation(a.u[:], bank[0:FOX_H], ACT.Identity, bias=b_f[:])
                    elif b == 23:
                        made = act.activation(a.gates[:], bank[:, 0:TT * 24].rearrange("p (t c) -> p t c", t=TT), ACT.Sigmoid)
                    elif n in features:
                        tile, at, scale = features[n]
                        made = act.mul(tile[:, at + m, :], bank, scale)
                    elif n in (4, 5):
                        made = act.copy(a.fv[:, 2 * m:2 * m + 2, (n - 4) * PW:(n - 3) * PW],
                                        bank.rearrange("p (t c) -> p t c", t=2))
                    elif m == 0:
                        made = act.copy((ks_raw if n == 9 else kw_raw)[:], bank)
                    else:
                        made = act.copy((a.vs if n == 9 else a.vw)[:], bank.rearrange("p (t c) -> p t c", t=TT))
                    made.then_inc(copied, 1)


def attn_prepare(k, a):
    nc, ps, ins = k.nc, k.ps, k.ins
    with Phase(k, "attn_pre") as f:
        w1, w2 = f.sb("w1", [P, 2, 32, HD]), f.sb("w2", [P, 2, HD])
        flat, hidden = f.sb("flat", [P, 2, 32, NCMP]), f.sb("hidden", [P, 2, 32])
        soft, neg, steep = (f.sb(s, [FOX_H, T]) for s in ("soft", "neg", "steep"))
        pick, dist = f.sb("pick", [FOX_H, FOX_H, P]), f.sb("dist", [P, T])
        ones = k.ones[0:FOX_H, 0:1].broadcast_to([FOX_H, T])
        landed, filled, cut, opened, negated, softened, summed, spread, kept, blocked, mapped, bent, made, zeroed = (
            f.sem(s) for s in ("landed", "filled", "cut", "opened", "negated", "softened", "summed", "spread", "kept",
                               "blocked", "mapped", "bent", "made", "zeroed"))
        with nc.Block() as block:

            @block.sync
            def _(sp):
                for half in range(2):
                    rows = slice(half * HD, (half + 1) * HD)
                    for kv in range(2):
                        sp.dma_start(w1[rows, kv], ins["nsa_cmp_w1_2"][0, kv].rearrange("(i d) h -> d i h", d=HD)).then_inc(landed, 16)
                        sp.dma_start(w2[rows, kv, :], ins["nsa_cmp_w2_2"][0, kv]).then_inc(landed, 16)

            @block.gpsimd
            def _(pool):
                pool.memset(pick[:], 0.0).then_inc(filled, 1)
                pool.iota(dist[:], [[-1, T]], base=T - P, channel_multiplier=1, allow_small_or_imprecise_dtypes=True).then_inc(filled, 1)
                pool.iota(a.cmp_dist[:], [[P, TT], [-16, 32]], base=-31, channel_multiplier=1,
                          allow_small_or_imprecise_dtypes=True).then_inc(filled, 1)
                pool.memset(a.future[:], 0.0).then_inc(filled, 1)
                pool.wait_ge(filled, 4)
                pool.affine_select(out=pick[:], in_=pick[:], pattern=[[-1, FOX_H], [0, P]], compare_op=ALU.not_equal, fill=-1.0,
                                   base=0, channel_multiplier=1).then_inc(cut, 1)
                pool.affine_select(out=dist[:], in_=dist[:], pattern=[[-1, T]], compare_op=ALU.is_ge, fill=BIG, base=T - P,
                                   channel_multiplier=1).then_inc(cut, 1)
                pool.affine_select(out=a.cmp_dist[:], in_=a.cmp_dist[:], pattern=[[P, TT], [-16, 32]], compare_op=ALU.is_ge,
                                   fill=BIG, base=-31, channel_multiplier=1).then_inc(cut, 1)
                pool.affine_select(out=a.future[:], in_=a.future[:], pattern=[[-1, P]], compare_op=ALU.is_ge, fill=BIG, base=0,
                                   channel_multiplier=1).then_inc(cut, 1)

            @block.scalar
            def _(act):
                act.activation(soft[:], a.u[:], ACT.Abs).then_inc(opened, 1)
                act.wait_ge(opened, 1)
                act.activation(soft[:], soft[:], ACT.Exp, scale=-1.0).then_inc(opened, 1)
                act.wait_ge(opened, 2)
                act.activation(soft[:], soft[:], ACT.Ln, bias=k.eps[0:FOX_H, 3:4]).then_inc(opened, 1)
                for h in range(FOX_H):
                    act.wait_ge(spread, h + 1)
                    act.copy(a.forget[:, h, :], ps[:, h % 4, :]).then_inc(kept, 1)
                act.wait_ge(mapped, 1)
                act.wait_ge(zeroed, 1)
                act.activation(hidden[:, :, 0:NCMP], ps[:, 4, :].rearrange("p (v n) -> p v n", v=2)[:, :, 0:NCMP],
                               ACT.Gelu_apprx_tanh).then_inc(bent, 1)
                act.wait_ge(made, 1)
                act.copy(a.kc[:], ps[:, 5:8:2, 0:32])
                act.copy(a.vc[:], ps[0:32, 5:8:2, HD:2 * HD])

            @block.vector
            def _(dve):
                dve.memset(hidden[:], 0.0).then_inc(zeroed, 1)
                dve.tensor_scalar(neg[:], a.u[:], -1.0, 0.0, ALU.mult, ALU.max).then_inc(negated, 1)
                dve.wait_ge(opened, 3)
                dve.wait_ge(negated, 1)
                dve.tensor_tensor(neg[:], neg[:], soft[:], ALU.add).then_inc(softened, 1)
                dve.wait_ge(softened, 1)
                dve.tensor_tensor_scan(steep[:], ones, neg[:], 0.0, ALU.mult, ALU.add).then_inc(summed, 1)
                for kv in range(2):
                    by_16 = a.cmp_in[:, kv, :].rearrange("p (n i) -> p i n", i=16)
                    for half in range(2):
                        at = slice(16 * half, 16 * half + 16)
                        dve.tensor_tensor(flat[:, kv, at, :], by_16[:, :, half:half + NCMP],
                                          k.pe_T[:, kv, at].unsqueeze(2).broadcast_to([P, 16, NCMP]), ALU.add).then_inc(blocked, 1)
                dve.wait_ge(cut, 2)
                for h in range(NSA_H):
                    dve.tensor_scalar(a.alibi[:, h, :], dist[:], 2.0 ** -(h + 1), None, ALU.mult)

            @block.tensor
            def _(pe):
                pe.wait_ge(summed, 1)
                pe.wait_ge(cut, 1)
                for h in range(FOX_H):
                    if h >= 4:
                        pe.wait_ge(kept, h - 3)
                    pe.matmul(ps[:, h % 4, :], pick[:, h, :], steep[:], start=True, stop=True).then_inc(spread, 1)
                pe.wait_ge(blocked, 4)
                pe.wait_ge(landed, 16 * 8)
                for kv in range(2):
                    for g in range(GROUPS):
                        rows = slice(g * HD, (g + 1) * HD)
                        for i in range(32):
                            last = pe.matmul(ps[rows, 4, kv * 256:kv * 256 + NCMP], w1[rows, kv, i, :], flat[rows, kv, i, :],
                                             start=i == 0, stop=i == 31)
                last.then_inc(mapped, 1)
                pe.wait_ge(bent, 1)
                for g in range(GROUPS):
                    rows, bank = slice(g * HD, (g + 1) * HD), 5 + 2 * g
                    for half in range(2):
                        pe.matmul(ps[half * HD:(half + 1) * HD, bank, 0:32], w2[rows, 0, :], hidden[rows, 0, :], start=True, stop=True)
                    last = pe.matmul(ps[0:32, bank, HD:2 * HD], hidden[rows, 1, :], w2[rows, 1, :], start=True, stop=True)
                last.then_inc(made, 1)


def attention(k, a):
    nc, ps = k.nc, k.ps
    units = [("fox", h) for h in range(FOX_H)]
    for h in range(NSA_H):
        units += [("slc", h), ("win", h), ("cmp", h)]
    n_units = len(units)
    s_at = {3: (0, 0), 2: (1, 0), 0: (1, 384), 1: (2, 0)}
    z_at = {3: 0, 2: 512, 0: 896, 1: 1024}
    t_at = {0: (3, 0), 1: (4, 0), 3: (4, 384), 2: (5, 0)}
    w_at = {0: 0, 1: 512, 3: 896, 2: 1024}
    with Phase(k, "attn") as f:
        z, w_T = f.sb("z", [P, 2, 1280]), f.sb("w_T", [P, 2, 1280])
        top, total, weight = (f.sb(s, [P, 2, TT]) for s in ("top", "total", "weight"))
        scored, lowered, exped, weighted, scaled, turned, copied_a, copied_v, mixed, kept, floored, inverted, clamped = (
            f.sem(s) for s in ("scored", "lowered", "exped", "weighted", "scaled", "turned", "copied_a", "copied_v", "mixed",
                               "kept", "floored", "inverted", "clamped"))

        def rows_of_head(h):
            return slice((h % 2) * HD, (h % 2 + 1) * HD)

        def head_no(u):
            kind, h = units[u]
            return h if kind == "fox" else FOX_H + h

        def last_of_head(u):
            return u + 1 == n_units or head_no(u + 1) != head_no(u)

        cmp_units = [sum(x[0] == "cmp" for x in units[:u + 1]) for u in range(n_units)]

        with nc.Block() as block:

            @block.tensor
            def _(pe):
                def scores(u):
                    kind, h = units[u]
                    rows = rows_of_head(h)
                    if u:
                        pe.wait_ge(lowered, u)
                    q, keys = {"fox": (a.fq, a.fk[rows, h // 2, :]), "slc": (a.nq, a.ks[rows, h // 4, :]),
                               "win": (a.nq, a.kw[rows, h // 4, :]), "cmp": (a.nq, a.kc[rows, h // 4, :])}[kind]
                    for t in range(TT):
                        q_t = q[rows, h // 2, t * P:(t + 1) * P]
                        if kind == "cmp":
                            last = pe.matmul(ps[:, 0, t * 32:(t + 1) * 32], q_t, keys, start=True, stop=True)
                            continue
                        bank, c = s_at[t]
                        n = (t + 1) * P
                        last = pe.matmul(ps[:, bank, c:c + n], q_t, keys[:, 0:n], start=True, stop=kind != "fox")
                        if kind == "fox":
                            last = pe.matmul(ps[:, bank, c + n - P:c + n], k.ident[:], a.future[:], start=False, stop=True)
                    last.then_inc(scored, 1)

                def turn(u):
                    pe.wait_ge(scaled, u + 1)
                    if u:
                        pe.wait_ge(copied_a, u - cmp_units[u - 1])
                        pe.wait_ge(copied_v, u)
                    if units[u][0] == "cmp":
                        for t in range(TT):
                            last = pe.transpose(ps[0:32, 3, t * P:(t + 1) * P], z[:, u % 2, t * 32:(t + 1) * 32], k.ident[:])
                    else:
                        for j in range(TT):
                            bank, c = t_at[j]
                            for t in range(j, TT):
                                at = z_at[t] + j * P
                                last = pe.transpose(ps[:, bank, c + (t - j) * P:c + (t - j + 1) * P], z[:, u % 2, at:at + P], k.ident[:])
                    last.then_inc(turned, 1)

                def mix(u):
                    kind, h = units[u]
                    pe.wait_ge(copied_a, u + 1 - cmp_units[u])
                    pe.wait_ge(copied_v, u + 1)
                    n, rows = head_no(u), rows_of_head(h)
                    first, final = u == 0 or head_no(u - 1) != n, last_of_head(u)
                    if first and n >= 2:
                        pe.wait_ge(kept, n - 1)
                    out, vcol = ps[rows, 6 + n % 2, :], slice((h // 4) * HD, (h // 4 + 1) * HD)
                    if kind == "cmp":
                        last = pe.matmul(out, a.vc[:, h // 4, :], w_T[0:32, u % 2, 0:T], start=first, stop=final)
                    else:
                        for j in range(TT):
                            v = a.fv[:, j, h * HD:(h + 1) * HD] if kind == "fox" else (a.vs if kind == "slc" else a.vw)[:, j, vcol]
                            last = pe.matmul(out[:, j * P:T], v, w_T[:, u % 2, w_at[j]:w_at[j] + T - j * P], start=first and j == 0,
                                             stop=final and j == TT - 1)
                    last.then_inc(mixed, 1)

                scores(0)
                for u in range(n_units):
                    if u + 1 < n_units:
                        scores(u + 1)
                    turn(u)
                    if u:
                        mix(u - 1)
                mix(n_units - 1)

            @block.vector
            def _(dve):
                def lower(u):
                    kind, h = units[u]
                    dve.wait_ge(scored, u + 1)
                    if u >= 2:
                        dve.wait_ge(turned, u - 1)
                    if kind == "cmp":
                        zc = z[:, u % 2, 0:TT * 32].rearrange("p (t n) -> p t n", t=TT)
                        dve.scalar_tensor_tensor(zc, a.cmp_dist[:], 2.0 ** -(h + 1), ps[:, 0, 0:TT * 32].rearrange("p (t n) -> p t n", t=TT),
                                                 ALU.mult, ALU.add).then_inc(floored, 1)
                        dve.wait_ge(floored, 2 * cmp_units[u] - 1)
                        dve.tensor_reduce(top[:, u % 2, :], zc, AX.X, ALU.min).then_inc(floored, 1)
                        dve.wait_ge(floored, 2 * cmp_units[u])
                        dve.tensor_scalar(top[:, u % 2, :], top[:, u % 2, :], 1e26, None, ALU.min).then_inc(lowered, 1)
                        return
                    for t in range(TT):
                        bank, c = s_at[t]
                        n = (t + 1) * P
                        bias = a.forget[:, h, 0:n] if kind == "fox" else a.alibi[:, h, T - n:T]
                        last = dve.tensor_tensor_reduce(z[:, u % 2, z_at[t]:z_at[t] + n], ps[:, bank, c:c + n], bias, 1.0, 3e38,
                                                        ALU.add, ALU.min, top[:, u % 2, t:t + 1])
                    last.then_inc(lowered, 1)

                def weigh(u):
                    kind, h = units[u]
                    dve.wait_ge(exped, u + 1)
                    if u >= 2:
                        dve.wait_ge(scaled, u - 1)
                    if kind == "cmp":
                        dve.tensor_scalar(total[:, u % 2, :], total[:, u % 2, :], 1e-30, None, ALU.max).then_inc(clamped, 1)
                        dve.wait_ge(clamped, cmp_units[u])
                    if kind == "fox":
                        dve.reciprocal(weight[:, u % 2, :], total[:, u % 2, :]).then_inc(weighted, 1)
                        return
                    dve.reciprocal(weight[:, u % 2, :], total[:, u % 2, :]).then_inc(inverted, 1)
                    dve.wait_ge(inverted, u - FOX_H + 1)
                    gate = a.gates[:, :, 3 * h + ("cmp", "slc", "win").index(kind)]
                    dve.tensor_tensor(weight[:, u % 2, :], weight[:, u % 2, :], gate, ALU.mult).then_inc(weighted, 1)

                def copy(u):
                    dve.wait_ge(turned, u + 1)
                    if u >= 2:
                        dve.wait_ge(mixed, u - 1)
                    if units[u][0] == "cmp":
                        dve.tensor_copy(w_T[0:32, u % 2, 0:T], ps[0:32, 3, :]).then_inc(copied_v, 1)
                    else:
                        dve.tensor_copy(w_T[:, u % 2, 0:T], ps[:, 3, :]).then_inc(copied_v, 1)

                lower(0)
                for u in range(n_units):
                    weigh(u)
                    if u + 1 < n_units:
                        lower(u + 1)
                    copy(u)

            @block.scalar
            def _(act):
                def exps(u):
                    act.wait_ge(lowered, u + 1)
                    if u >= 2:
                        act.wait_ge(weighted, u - 1)
                    for t in range(TT):
                        at, n = (t * 32, 32) if units[u][0] == "cmp" else (z_at[t], (t + 1) * P)
                        last = act.activation(z[:, u % 2, at:at + n], z[:, u % 2, at:at + n], ACT.Exp, bias=top[:, u % 2, t:t + 1],
                                              scale=-1.0, accum_out=total[:, u % 2, t:t + 1])
                    last.then_inc(exped, 1)

                def copy(u):
                    if units[u][0] == "cmp":
                        return
                    act.wait_ge(turned, u + 1)
                    if u >= 2:
                        act.wait_ge(mixed, u - 1)
                    act.copy(w_T[:, u % 2, T:1280], ps[:, 4:6, :].rearrange("p b c -> p (b c)")[:, 0:768]).then_inc(copied_a, 1)

                def keep(u):
                    act.wait_ge(mixed, u + 1)
                    n, rows = head_no(u), rows_of_head(units[u][1])
                    act.copy(k.hT[rows, n // 2, :], ps[rows, 6 + n % 2, :]).then_inc(kept, 1)

                exps(0)
                for u in range(n_units):
                    if u + 1 < n_units:
                        exps(u + 1)
                    copy(u)
                    if u and last_of_head(u - 1):
                        keep(u - 1)
                keep(n_units - 1)

            @block.gpsimd
            def _(pool):
                for u in range(n_units):
                    pool.wait_ge(weighted, u + 1)
                    for t in range(TT):
                        at, n = (t * 32, 32) if units[u][0] == "cmp" else (z_at[t], (t + 1) * P)
                        last = pool.tensor_scalar(z[:, u % 2, at:at + n], z[:, u % 2, at:at + n], weight[:, u % 2, t:t + 1], None, ALU.mult)
                    last.then_inc(scaled, 1)



POOL_WINDOWS = (2, 4, 8, 16)


def pool_mixer(k, out):
    nc, ps, g0 = k.nc, k.ps, k.first_panel["pool"]
    gain = k.col_b[:, ROW_B["pool_scale_2"]:ROW_B["pool_scale_2"] + KT]
    with Phase(k, "pool") as f:
        sums, pooled, diff = f.sb("sums", [P, KT, T]), f.sb("pooled", [P, KT, T]), f.sb("diff", [P, KT, T])
        count, inv = f.sb("count", [P, 16]), f.sb("inv", [P, 16])
        one = k.ones[:, 0:1].broadcast_to([P, T])
        counted, inverted, summed, apart, headed, pooled_s, first = (f.sem(s) for s in (
            "counted", "inverted", "summed", "apart", "headed", "pooled", "first"))
        with nc.Block() as block:

            @block.sync
            def _(sp):
                k.load_panels(sp, k.lookahead("pool"))

            @block.gpsimd
            def _(pool):
                pool.iota(count[:], [[1, 16]], base=1, channel_multiplier=0, allow_small_or_imprecise_dtypes=True).then_inc(counted, 1)

            @block.vector
            def _(dve):
                dve.wait_ge(counted, 1)
                dve.reciprocal(inv[:], count[:]).then_inc(inverted, 1)
                dve.wait_ge(inverted, 1)
                for b in range(KT):
                    w = POOL_WINDOWS[b // 2]
                    h = k.hT[:, b, :]
                    dve.tensor_tensor_scan(sums[:, b, :], one, h, 0.0, ALU.mult, ALU.add).then_inc(summed, 1)
                    dve.wait_ge(summed, b + 1)
                    dve.tensor_tensor(diff[:, b, w:T], sums[:, b, w:T], sums[:, b, 0:T - w], ALU.subtract)
                    dve.tensor_tensor(diff[:, b, 0:w], sums[:, b, 0:w], inv[:, 0:w], ALU.mult).then_inc(apart, 1)
                    dve.wait_ge(apart, b + 1)
                    dve.tensor_tensor(pooled[:, b, 0:w], diff[:, b, 0:w], h[:, 0:w], ALU.subtract)
                    dve.scalar_tensor_tensor(pooled[:, b, w:T], diff[:, b, w:T], 1.0 / w, h[:, w:T], ALU.mult, ALU.subtract)\
                        .then_inc(pooled_s, 1)

            @block.tensor
            def _(pe):
                for g in range(4):
                    w, landed, value = k.panel(g0, 0, g, 2, PW)
                    pe.wait_ge(landed, value)
                    pe.wait_ge(pooled_s, 2 * g + 2)
                    for m in range(2):
                        for kt in range(2):
                            last = pe.matmul(ps[:, 2 * g + m, :], w[:, kt, m * P:(m + 1) * P], pooled[:, 2 * g + kt, :],
                                             start=kt == 0, stop=kt == 1)
                        last.then_inc(k.panel_used if m else first, 1)

            @block.scalar
            def _(act):
                for b in range(KT):
                    if b % 2:
                        act.wait_ge(k.panel_used, g0 + b // 2 + 1)
                    else:
                        act.wait_ge(first, b // 2 + 1)
                    act.mul(out[:, b, :], ps[:, b, :], gain[:, b:b + 1])


def second_block(k):
    def gain(layer, n):
        at = ROW_B["norm_g_2"] + (4 * layer + n) * KT
        return k.col_b[:, at:at + KT]

    for layer in range(2):
        rms_norm(k, f"mix_norm{layer}", k.xT, gain(layer, 0), k.hT)
        if layer == 0:
            with Phase(k, "attn_all") as f:
                a = Attention(f)
                attn_project(k, a)
                attn_prepare(k, a)
                attention(k, a)
        with Phase(k, f"mixer{layer}") as f:
            mixed = f.sb("mixed", [P, KT, T])
            if layer == 0:
                add_projection(k, "attn_out", k.hT, (KT,), mixed)
            else:
                pool_mixer(k, mixed)
            rms_norm(k, f"mixed_norm{layer}", mixed, gain(layer, 1), k.xT, add=True)
        rms_norm(k, f"glu_norm{layer}", k.xT, gain(layer, 2), k.hT)
        with Phase(k, f"glu{layer}") as f:
            mixed = f.sb("out", [P, KT, T])
            with Phase(k, f"glu_in{layer}") as g:
                hidden = g.sb("hidden", [P, HK, T])
                swiglu_in(k, layer, hidden)
                add_projection(k, f"down{layer}", hidden, DOWN_CHUNKS, mixed)
            rms_norm(k, f"out_norm{layer}", mixed, gain(layer, 3), k.xT, add=True)


def store(k):
    nc, ps = k.nc, k.ps
    with Phase(k, "store") as f:
        y = f.sb("y", [P, TT, D])
        turned, copied, stored = f.sem("turned"), f.sem("copied"), f.sem("stored")
        with nc.Block() as block:

            @block.tensor
            def _(pe):
                for t in range(TT):
                    for kt in range(KT):
                        last = pe.transpose(ps[:, 2 * t + kt // 4, (kt % 4) * P:(kt % 4 + 1) * P], k.xT[:, kt, t * P:(t + 1) * P], k.ident[:])
                    last.then_inc(turned, 1)

            @block.scalar
            def _(act):
                for t in range(TT):
                    act.wait_ge(turned, t + 1)
                    act.copy(y[:, t, 0:BANK], ps[:, 2 * t, :]).then_inc(copied, 1)

            @block.vector
            def _(dve):
                for t in range(TT):
                    dve.wait_ge(turned, t + 1)
                    dve.tensor_copy(y[:, t, BANK:D], ps[:, 2 * t + 1, :]).then_inc(stored, 1)

            @block.sync
            def _(sp):
                done = k.output_stored
                for t in range(TT):
                    sp.wait_ge(copied, t + 1)
                    sp.wait_ge(stored, t + 1)
                    sp.dma_start(k.out[0, t * P:(t + 1) * P, :], y[:, t, :]).then_inc(done, 16)
                sp.wait_ge(done, 16 * TT)


def build(nc, ins, out):
    with ExitStack() as ctx:
        k = Kernel(nc, ctx, ins, out)
        k.output_stored = ctx.enter_context(nc.semaphore("output_stored"))
        setup(k)
        gain = k.col_a[:, ROW_A["mem_norm_g"]:ROW_A["mem_norm_g"] + KT]
        rms_norm(k, "mem_norm", k.memT, gain, k.hT, n=M)
        memory_kv(k)
        rms_norm(k, "norm", k.xT, k.col_a[:, ROW_A["norm_mix_g"]:ROW_A["norm_mix_g"] + KT], k.hT)
        rwkv_block(k)
        second_block(k)
        store(k)


_UNUSED = ("df_in", "df_q_norm_g", "df_k_norm_g", "df_lq1", "df_lk1", "df_lq2", "df_lk2", "df_subln_g")


def kernel(**inputs):
    import numpy as np
    import concourse.bacc as bacc
    from concourse.bass_utils import run_bass_kernel_spmd

    nc = bacc.Bacc("TRN2", target_bir_lowering=False, num_devices=1)
    arrays, ins = {}, {}
    for name, value in inputs.items():
        if name in _UNUSED:
            continue
        arrays[f"in_{name}"] = np.ascontiguousarray(value)
        ins[name] = nc.dram_tensor(f"in_{name}", arrays[f"in_{name}"].shape, F32, kind="ExternalInput").ap()
    out = nc.dram_tensor("out_x", (1, T, D), F32, kind="ExternalOutput").ap()
    build(nc, ins, out)
    result = run_bass_kernel_spmd(nc, [arrays], core_ids=[0])
    return result.results[0]["out_x"]
```

```python
from contextlib import ExitStack

import concourse.bass as bass
from concourse import mybir

F32 = mybir.dt.float32
F32R = mybir.dt.float32r
ALU = mybir.AluOpType
ACT = mybir.ActivationFunctionType
AX = mybir.AxisListType

P = 128
T = 512
D = 1024
KT = D // P
TT = T // P
M = 256
HD = 64
MIX = 768
PAIRS = MIX // P
LOG_DECAY = 0.6065306597126334
CH = 64
NCH = T // CH
RING = 2
AHEAD = 2 * RING
PW = 256
HID = 2816
HK = HID // P
DOWN_CHUNKS = (6, 6, 5, 5)
BANK = 512
BIG = 1e30
RMS_EPS = 1e-6
GN_EPS = 64e-5
KK_SCALE = 2.0 ** 24
KK_BIAS = 12.0 * 0.6931471805599453

VEC_A = (("norm_mix_g", 8), ("norm_ffn_g", 8), ("mem_norm_g", 8), ("rw_mu", 20), ("rw_w0", 6), ("rw_a0", 6),
         ("rw_k_k", 6), ("rw_k_a", 6), ("rw_r_k", 6), ("rw_lnx_g", 6), ("rw_lnx_b", 6),
         ("mem_q_norm_g", 1), ("mem_k_norm_g", 1))
VEC_B = (("norm_g_2", 64), ("pool_scale_2", 8))


def rows_of(table):
    at, out = 0, {}
    for name, n in table:
        out[name] = at
        at += n
    return out, at


ROW_A, N_A = rows_of(VEC_A)
ROW_B, N_B = rows_of(VEC_B)

FQ, FK, FV, FF, NQ, KC, VC, KS, VS, KW, VW, NG = 0, 512, 1024, 1536, 1544, 2056, 2184, 2312, 2440, 2568, 2696, 2824


class Kernel:

    def __init__(self, nc, ctx, ins, out):
        self.nc, self.ins, self.out = nc, ins, out
        self.n_blocks = 0

        def sb(name, shape):
            return ctx.enter_context(nc.sbuf_tensor(name, shape, F32))

        self.ring = sb("weight_ring", [P, RING, KT * PW])
        self.xT = sb("residual_T", [P, KT, T])
        self.w_hi = ctx.enter_context(nc.sbuf_tensor("weight_high", [P, RING, KT * PW], F32R))
        self.w_lo = ctx.enter_context(nc.sbuf_tensor("weight_low", [P, RING, KT * PW], F32R))
        self.rstd = sb("rstd", [P, T])
        self.ident = sb("identity", [P, P])
        self.ones = sb("ones", [P, P])
        self.head_ones = sb("head_ones", [P, P])
        self.eye64 = sb("eye64", [P, HD])
        self.level = sb("level_masks", [P, 6, P])
        self.level0_T = sb("level0_mask_T", [P, P])
        self.upto_T = sb("upto_mask_T", [P, P])
        self.before_T = sb("before_mask_T", [P, P])
        self.restart = sb("restart", [P, T])
        self.eps = sb("eps_columns", [P, 4])
        self.col_a = sb("columns_a", [P, N_A])
        self.col_b = sb("columns_b", [P, N_B])
        self.pe_T = sb("position_T", [P, 2, 32])
        self.k_mem = sb("k_mem_T", [P, 2, M])
        self.v_mem = sb("v_mem", [P, 2, M])
        self.ps = ctx.enter_context(nc.psum_tensor("psum", [P, 8, BANK], F32))
        self.panel_landed = [ctx.enter_context(nc.semaphore(f"panel_landed_{s}")) for s in range(RING)]
        self.panel_high, self.panel_low, self.panel_used = (
            ctx.enter_context(nc.semaphore(f"panel_{s}")) for s in ("high", "low", "used"))
        self.squared, self.counted, self.logged, self.rooted, self.scaled, self.high, self.low = (
            ctx.enter_context(nc.semaphore(f"rows_{s}"))
            for s in ("squared", "counted", "logged", "rooted", "scaled", "high", "low"))
        self.take_sems, self.projection_sems = ([ctx.enter_context(nc.semaphore(f"{phase}_{s}")) for s in names] for phase, names in (
            ("take_in", ("parted", "taken")), ("projection", ("made", "taken"))))
        self.takes, self.projections = 0, 0
        self.stats_made, self.blocks_scaled, self.blocks_split = 0, 0, 0
        self.plan_panels()
        self.loaded = 0

    def plan_panels(self):
        ins, self.phases, self.first_panel = self.ins, [], {}

        def tall(w):
            return w.rearrange("(k p) m -> p k m", p=P)

        def columns(w, c0=0):
            view = tall(w)
            return lambda i: (view[:, :, bass.ds(c0 + PW * i, PW)], view.shape[1], PW)

        def listed(parts):
            return lambda i: parts[i]

        def chunked(w, chunks):
            view, parts, k0 = tall(w), [], 0
            for n in chunks:
                parts.append((k0, n))
                k0 += n
            return lambda i, j: (view[:, parts[j][0]:parts[j][0] + parts[j][1], bass.ds(PW * i, PW)], parts[j][1], PW)

        def halved(w, half):
            view = tall(w)
            return listed([(view[:, 16 * half + 8 * c:16 * half + 8 * c + 8, PW * i:PW * (i + 1)], KT, PW)
                           for i in range(4) for c in range(2)])

        def add(name, n, view, kind="columns"):
            self.first_panel[name] = sum(x[1] for x in self.phases)
            self.phases.append((name, n, view, kind))

        add("mem_kv", 2, columns(ins["w_mem_kv"]))
        add("rw_in", 11, columns(ins["rw_in"][0]))
        add("w_out", 4, columns(ins["w_out"][0]))
        for half in range(2):
            add(f"ff1{half}", 8, columns(ins["w_ff1"][0], 8 * PW * half))
            add(f"ff2{half}", 8, halved(ins["w_ff2"][0], half), "listed")
        w = tall(ins["attn_w_in_2"][0])
        cuts = [(FQ, 256), (FQ + 256, 256), (FK, 256), (FK + 256, 256), (FV, 256), (FV + 256, 256), (NQ, 256),
                (NQ + 256, 256), (KC, 256), (KS, 256), (KW, 256), (FF, P), (NG, 24)]
        add("attn_in", len(cuts), listed([(w[:, :, c:c + n], KT, n) for c, n in cuts]), "listed")
        add("attn_out", 4, columns(ins["attn_w_out_2"][0]))
        for layer in range(2):
            gate, up = tall(ins["ffn_w_gate_2"][layer]), tall(ins["ffn_w_up_2"][layer])

            def gate_up(i, j, gate=gate, up=up):
                return ((gate, up)[j % 2][:, :, bass.ds(2 * PW * i + PW * (j // 2), PW)], KT, PW)

            add(f"gate_up{layer}", 2 * HID // PW, gate_up, "chunks")
            add(f"down{layer}", 16, chunked(ins["ffn_w_down_2"][layer], DOWN_CHUNKS), "chunks")
            if layer == 0:
                pool = [(ins["pool_w_2"][0, g].rearrange("(k p) m -> p k m", p=P), 2, PW) for g in range(4)]
                add("pool", 4, listed(pool), "listed")
        self.n_panels = sum(x[1] for x in self.phases)

    def panel_columns(self, g):
        for name, n, view, kind in self.phases:
            at = g - self.first_panel[name]
            if 0 <= at < n:
                _, kt, width = view(at // 4, at % 4) if kind == "chunks" else view(at)
                return kt * width
        return 0

    def load_panels(self, sp, until):
        until = min(until, self.n_panels)
        start = 0
        for name, n, view, kind in self.phases:
            lo, hi = max(self.loaded, start), min(until, start + n)
            g0, start = start, start + n

            def load(i, j, g0=g0, view=view, kind=kind):
                slot, g = (g0 + j) % RING, g0 + j
                src, kt, width = view(i, j) if kind == "chunks" else view(4 * i + j)
                if not isinstance(i, int) or g + 4 * i >= RING:
                    sp.wait_ge(self.panel_low, 4 * i + (g - RING + 1))
                dst = self.ring[:, slot, 0:kt * width].rearrange("p (k m) -> p k m", k=kt)
                sp.dma_start(dst, src).then_inc(self.panel_landed[slot], 16)

            at = lo - g0
            while at < hi - g0:
                fours = (hi - g0 - at) // 4
                if at % 4 == 0 and fours >= 2 and kind != "listed" and g0 + at >= RING:
                    with sp.Fori(at // 4, at // 4 + fours) as i:
                        for j in range(4):
                            load(i, j)
                    at += 4 * fours
                else:
                    load(at // 4, at % 4)
                    at += 1
        self.loaded = max(self.loaded, until)

    def split_high(self, act, g0, i, j):
        g = g0 + j
        if isinstance(i, int) and g + 4 * i >= self.n_panels:
            return
        slot, n = g % RING, self.panel_columns(g + 4 * i if isinstance(i, int) else g)
        if not isinstance(i, int) or g + 4 * i >= RING:
            act.wait_ge(self.panel_used, 4 * i + (g - RING + 1))
        act.wait_ge(self.panel_landed[slot], 32 * i + 16 * (g // RING + 1))
        act.copy(self.w_hi[:, slot, 0:n], self.ring[:, slot, 0:n]).then_inc(self.panel_high, 1)

    def split_low(self, dve, g0, i, j):
        g = g0 + j
        if isinstance(i, int) and g + 4 * i >= self.n_panels:
            return
        slot, n = g % RING, self.panel_columns(g + 4 * i if isinstance(i, int) else g)
        dve.wait_ge(self.panel_high, 4 * i + (g + 1))
        dve.tensor_tensor(self.w_lo[:, slot, 0:n], self.ring[:, slot, 0:n], self.w_hi[:, slot, 0:n],
                          ALU.subtract).then_inc(self.panel_low, 1)

    def panel(self, pe, g0, i, j, kt, width):
        slot = (g0 + j) % RING
        pe.wait_ge(self.panel_low, 4 * i + (g0 + j + 1))
        return [w[:, slot, 0:kt * width].rearrange("p (k m) -> p k m", k=kt) for w in (self.w_hi, self.w_lo)]

    def lookahead(self, name):
        n = next(x[1] for x in self.phases if x[0] == name)
        return self.first_panel[name] + n + AHEAD


def product(pe, out, w, x, start, stop):
    (w_hi, w_lo), (x_hi, x_lo) = w, x
    pe.matmul(out, w_hi, x_hi, start=start, stop=False)
    pe.matmul(out, w_hi, x_lo, start=False, stop=False)
    return pe.matmul(out, w_lo, x_hi, start=False, stop=stop)


class Phase:

    def __init__(self, k, name):
        self.k, self.name, self.ctx = k, name, ExitStack()

    def __enter__(self):
        self.ctx.__enter__()
        return self

    def __exit__(self, *a):
        return self.ctx.__exit__(*a)

    def sem(self, name):
        return self.ctx.enter_context(self.k.nc.semaphore(f"{self.name}_{name}"))

    def sb(self, name, shape, dtype=F32):
        return self.ctx.enter_context(self.k.nc.sbuf_tensor(f"{self.name}_{name}", shape, dtype))


def in_fours(eng, n, body):
    fours = (n - 2) // 4
    done = 0
    if fours >= 3:
        for j in range(4):
            body(0, j)
        with eng.Fori(1, fours) as i:
            for j in range(4):
                body(i, j)
        done = 4 * fours
    for at in range(done, n):
        body(at // 4, at % 4)



def setup(k, mem_T):
    nc, ps, ins = k.nc, k.ps, k.ins
    with Phase(k, "setup") as f:
        x_in, mem_in = f.sb("x", [P, TT, D]), f.sb("mem", [P, 2, D])
        vec_a, vec_b, pe_in = f.sb("vec_a", [N_A, P]), f.sb("vec_b", [N_B, P]), f.sb("pe", [32, 2, P])
        x_landed, vec_landed, mem_landed = f.sem("x_landed"), f.sem("vec_landed"), f.sem("mem_landed")
        filled, cut = f.sem("filled"), f.sem("cut")
        x_turned, x_copied, mem_turned, mem_copied = (f.sem(n) for n in ("x_turned", "x_copied", "mem_turned", "mem_copied"))
        vec_turned = f.sem("vec_turned")
        with nc.Block() as block:

            @block.sync
            def _(sp):
                for t in range(TT):
                    sp.dma_start(x_in[:, t, :], ins["x"][0, t * P:(t + 1) * P, :]).then_inc(x_landed, 16)
                for t in range(2):
                    sp.dma_start(mem_in[:, t, :], ins["mem"][0, t * P:(t + 1) * P, :]).then_inc(mem_landed, 16)
                k.load_panels(sp, AHEAD)

            @block.gpsimd
            def _(pool):
                for n, (tile, value) in enumerate(((k.ident, 0.0), (k.head_ones, 1.0), (k.eye64, 0.0), (k.level, 1.0),
                                                   (k.level0_T, 0.0), (k.upto_T, 1.0), (k.before_T, 1.0),
                                                   (k.restart, 1.0), (k.ones, 1.0))):
                    pool.memset(tile[:], value).then_inc(filled, 1)
                pool.wait_ge(filled, 9)

                def select(n, view, pattern, base, channel, op, fill):
                    if n:
                        pool.wait_ge(cut, n)
                    pool.affine_select(out=view, in_=view, pattern=pattern, compare_op=op, fill=fill, base=base,
                                       channel_multiplier=channel).then_inc(cut, 1)

                cuts = [(k.ident[:], [[-1, P]], 0, 1, ALU.not_equal, 1.0),
                        (k.eye64[:], [[-1, HD]], 0, 1, ALU.not_equal, 1.0),
                        (k.eye64[:], [[-1, HD]], -HD, 1, ALU.not_equal, 1.0)]
                halves = k.head_ones[:].rearrange("p (h c) -> p h c", h=2)
                cuts += [(halves, [[-HD, 2], [0, HD]], 0, 1, ALU.is_ge, 0.0),
                         (halves, [[HD, 2], [0, HD]], HD - 1, -1, ALU.is_ge, 0.0)]
                for lv in range(6):
                    s = 1 << lv
                    cells = k.level[:, lv, :].rearrange("p (b h s) -> p b h s", h=2, s=s)
                    cuts += [(cells, [[-2 * s, P // (2 * s)], [-P * 2, 2], [0, s]], -s, 1, ALU.is_ge, 0.0),
                             (cells, [[2 * s, P // (2 * s)], [0, 2], [0, s]], 2 * s - 1, -1, ALU.is_ge, 0.0)]
                cells = k.level0_T[:].rearrange("p (b h) -> p b h", h=2)
                cuts += [(cells[:, :, 1], [[-2, P // 2]], 0, 1, ALU.not_equal, 1.0)]
                for tile, strict in ((k.upto_T, 0), (k.before_T, 1)):
                    cells = tile[:].rearrange("p (c t) -> p c t", c=2)
                    cuts += [(cells, [[CH, 2], [1, CH]], -strict, -1, ALU.is_ge, 0.0),
                             (cells, [[-CH, 2], [0, CH]], 0, 1, ALU.is_ge, 0.0)]
                cells = k.restart[:].rearrange("p (c t) -> p c t", c=NCH)
                cuts += [(cells, [[0, NCH], [1, CH]], 0, 0, ALU.not_equal, 0.0)]
                for n, c in enumerate(cuts):
                    select(n, *c)

            @block.scalar
            def _(act):
                for table, tile, row in ((VEC_A, vec_a, ROW_A), (VEC_B, vec_b, ROW_B)):
                    for name, n in table:
                        a = ins[name]
                        for half in range(2 if n == 1 else 1):
                            if n == 1:
                                flat, dst = a, tile[row[name]:row[name] + 1, half * HD:(half + 1) * HD]
                            else:
                                order = {1: "(r c) -> r c", 2: "l (r c) -> (l r) c", 3: "l n (r c) -> (l n r) c"}
                                if name == "rw_r_k":
                                    flat = a.rearrange("l (r h) c -> (l r) (h c)", h=2)
                                else:
                                    flat = a.rearrange(order[len(a.shape)], c=P)
                                dst = tile[row[name]:row[name] + n, :]
                            act.dma_start(dst, flat).then_inc(vec_landed, 16)
                for kv in range(2):
                    for half in range(2):
                        act.dma_start(pe_in[:, kv, half * HD:(half + 1) * HD],
                                      ins["nsa_cmp_pe_2"][0, kv]).then_inc(vec_landed, 16)
                for kt in range(KT):
                    act.wait_ge(x_turned, kt + 1)
                    act.copy(k.xT[:, kt, :], ps[:, kt % 4, :]).then_inc(x_copied, 1)
                for g in range(RING):
                    k.split_high(act, 0, 0, g)

            @block.vector
            def _(dve):
                for n, value in enumerate((RMS_EPS, GN_EPS, KK_BIAS, 1.0)):
                    dve.memset(k.eps[:, n:n + 1], value)
                for j in range(4):
                    dve.wait_ge(mem_turned, j + 1)
                    dve.tensor_copy(mem_T[:, 2 * j:2 * j + 2, :],
                                    ps[:, 4 + j % 2, :].rearrange("p (k m) -> p k m", k=2)).then_inc(mem_copied, 1)
                dve.wait_ge(vec_turned, 1)
                dve.tensor_copy(k.col_a[:], ps[:, 6, 0:N_A])
                dve.tensor_copy(k.col_b[:], ps[:, 6, P:P + N_B])
                dve.tensor_copy(k.pe_T[:], ps[:, 6, 2 * P:2 * P + 64].rearrange("p (v i) -> p v i", v=2))
                for g in range(RING):
                    k.split_low(dve, 0, 0, g)

            @block.tensor
            def _(pe):
                pe.wait_ge(cut, 1)
                pe.wait_ge(x_landed, 16 * TT)
                for kt in range(KT):
                    if kt >= 4:
                        pe.wait_ge(x_copied, kt - 3)
                    for t in range(TT):
                        last = pe.transpose(ps[:, kt % 4, t * P:(t + 1) * P], x_in[:, t, kt * P:(kt + 1) * P], k.ident[:])
                    last.then_inc(x_turned, 1)
                pe.wait_ge(mem_landed, 32)
                for j in range(4):
                    if j >= 2:
                        pe.wait_ge(mem_copied, j - 1)
                    for kt in (2 * j, 2 * j + 1):
                        for t in range(2):
                            c = (kt % 2) * M + t * P
                            last = pe.transpose(ps[:, 4 + j % 2, c:c + P], mem_in[:, t, kt * P:(kt + 1) * P], k.ident[:])
                    last.then_inc(mem_turned, 1)
                pe.wait_ge(vec_landed, 16 * (len(VEC_A) + len(VEC_B) + 2 + 4))
                pe.transpose(ps[:, 6, 0:N_A], vec_a[:], k.ident[0:N_A, 0:N_A])
                pe.transpose(ps[:, 6, P:P + N_B], vec_b[:], k.ident[0:N_B, 0:N_B])
                for kv in range(2):
                    last = pe.transpose(ps[:, 6, 2 * P + 32 * kv:2 * P + 32 * kv + 32], pe_in[:, kv, :], k.ident[0:32, 0:32])
                last.then_inc(vec_turned, 1)



class Stats:

    def __init__(self, k, f, n=T):
        self.k, self.n, self.c = k, n, k.stats_made
        k.stats_made += 1
        self.squares, self.logs = f.sb("squares", [P, 2, n]), f.sb("logs", [P, n])

    def square(self, act, b, src):
        if b >= 2:
            act.wait_ge(self.k.counted, KT * self.c + b - 1)
        act.activation(self.squares[:, b % 2, :], src, ACT.Square).then_inc(self.k.squared, 1)

    def count(self, pe, b):
        pe.wait_ge(self.k.squared, KT * self.c + b + 1)
        pe.matmul(self.k.ps[:, 7, 0:self.n], self.k.ones[:], self.squares[:, b % 2, :], start=b == 0, stop=b == KT - 1)\
            .then_inc(self.k.counted, 1)

    def root(self, act):
        k, n = self.k, self.n
        act.wait_ge(k.counted, KT * (self.c + 1))
        act.activation(self.logs[:], k.ps[:, 7, 0:n], ACT.Ln, bias=k.eps[:, 0:1], scale=1.0 / D).then_inc(k.logged, 1)
        act.wait_ge(k.logged, self.c + 1)
        act.activation(k.rstd[:, 0:n], self.logs[:], ACT.Exp, scale=-0.5).then_inc(k.rooted, 1)


class Operand:

    def __init__(self, k, f, src, gain=None, n=T, normed=None):
        self.k, self.src, self.gain, self.n = k, src, gain, n
        self.blocks = src.shape[1]
        self.hi, self.lo = (f.sb(f"operand_{s}", [P, self.blocks, n], F32R) for s in ("high", "low"))
        self.c_split, self.c_scaled = k.blocks_split, k.blocks_scaled
        k.blocks_split += self.blocks
        if gain is not None:
            self.normed = f.sb("operand_normed", [P, 2, n]) if normed is None else normed
            k.blocks_scaled += self.blocks

    def block(self, b):
        return self.src[:, b, 0:self.n] if self.gain is None else self.normed[:, b % 2, :]

    def high_of(self, act, b):
        act.copy(self.hi[:, b, :], self.block(b)).then_inc(self.k.high, 1)

    def low_of(self, dve, b):
        dve.wait_ge(self.k.high, self.c_split + b + 1)
        dve.tensor_tensor(self.lo[:, b, :], self.block(b), self.hi[:, b, :], ALU.subtract).then_inc(self.k.low, 1)

    def highs(self, act):
        for b in range(self.blocks):
            if self.gain is not None:
                act.wait_ge(self.k.scaled, self.c_scaled + b + 1)
            self.high_of(act, b)

    def lows(self, dve):
        k = self.k

        def scale(b):
            if b >= 2:
                dve.wait_ge(k.low, self.c_split + b - 1)
            dve.scalar_tensor_tensor(self.normed[:, b % 2, :], self.src[:, b, 0:self.n], self.gain[:, b:b + 1],
                                     k.rstd[:, 0:self.n], ALU.mult, ALU.mult).then_inc(k.scaled, 1)

        if self.gain is not None:
            scale(0)
        for b in range(self.blocks):
            if self.gain is not None and b + 1 < self.blocks:
                scale(b + 1)
            self.low_of(dve, b)

    def ready(self, pe, b):
        pe.wait_ge(self.k.low, self.c_split + b + 1)

    def halves(self, b, at=slice(None)):
        return self.hi[:, b, at], self.lo[:, b, at]


def row_stats(k, name, src, n=T):
    with Phase(k, name) as f:
        stats = Stats(k, f, n)
        with k.nc.Block() as block:

            @block.scalar
            def _(act):
                for b in range(KT):
                    stats.square(act, b, src[:, b, 0:n])
                stats.root(act)

            @block.tensor
            def _(pe):
                for b in range(KT):
                    stats.count(pe, b)


def take_in(k, name, mixed, gain, stats=True):
    with Phase(k, name) as f:
        rows = Stats(k, f) if stats else None
        part = f.sb("part", [P, 2, T])
        (parted, taken), c = k.take_sems, KT * k.takes
        k.takes += 1
        with k.nc.Block() as block:

            @block.vector
            def _(dve):
                def scale(b):
                    if b >= 2:
                        dve.wait_ge(taken, c + b - 1)
                    dve.scalar_tensor_tensor(part[:, b % 2, :], mixed[:, b, :], gain[:, b:b + 1], k.rstd[:], ALU.mult,
                                             ALU.mult).then_inc(parted, 1)

                scale(0)
                for b in range(KT):
                    if b + 1 < KT:
                        scale(b + 1)
                    dve.wait_ge(parted, c + b + 1)
                    dve.tensor_tensor(k.xT[:, b, :], k.xT[:, b, :], part[:, b % 2, :], ALU.add).then_inc(taken, 1)

            @block.scalar
            def _(act):
                for b in range(KT if stats else 0):
                    act.wait_ge(taken, c + b + 1)
                    rows.square(act, b, k.xT[:, b, :])
                if stats:
                    rows.root(act)

            @block.tensor
            def _(pe):
                for b in range(KT if stats else 0):
                    rows.count(pe, b)



def memory_kv(k, mem_T, mem_gain):
    nc, ps, g0 = k.nc, k.ps, k.first_panel["mem_kv"]
    gain = k.col_a[:, ROW_A["mem_k_norm_g"]:ROW_A["mem_k_norm_g"] + 1]
    with Phase(k, "mem_kv") as f:
        squares, logs, rstd, raw = (f.sb(s, [P, 2, M]) for s in ("squares", "logs", "rstd", "raw"))
        copied, summed, logged, rooted = (f.sem(s) for s in ("copied", "summed", "logged", "rooted"))
        mem = Operand(k, f, mem_T, mem_gain, M)
        with nc.Block() as block:

            @block.sync
            def _(sp):
                k.load_panels(sp, k.lookahead("mem_kv"))

            @block.tensor
            def _(pe):
                w_hi, w_lo = k.panel(pe, g0, 0, 0, KT, PW)
                for m in range(2):
                    at = slice(m * P, (m + 1) * P)
                    for kt in range(KT):
                        if m == 0:
                            mem.ready(pe, kt)
                        last = product(pe, ps[:, m, 0:M], (w_hi[:, kt, at], w_lo[:, kt, at]), mem.halves(kt), kt == 0, kt == KT - 1)
                last.then_inc(k.panel_used, 1)
                w_hi, w_lo = k.panel(pe, g0, 0, 1, KT, PW)
                for t in range(2):
                    at = slice(t * P, (t + 1) * P)
                    for kt in range(KT):
                        last = product(pe, ps[:, 2 + t, 0:M], mem.halves(kt, at), (w_hi[:, kt, :], w_lo[:, kt, :]), kt == 0, kt == KT - 1)
                last.then_inc(k.panel_used, 1)
                pe.wait_ge(copied, 2)
                for m in range(2):
                    last = pe.matmul(ps[:, 4, m * M:(m + 1) * M], k.head_ones[:], squares[:, m, :], start=True, stop=True)
                last.then_inc(summed, 1)

            @block.scalar
            def _(act):
                mem.highs(act)
                act.wait_ge(k.panel_used, g0 + 1)
                act.copy(raw[:], ps[:, 0:2, 0:M]).then_inc(copied, 1)
                act.activation(squares[:], ps[:, 0:2, 0:M], ACT.Square).then_inc(copied, 1)
                k.split_high(act, g0, 0, 2)
                k.split_high(act, g0, 0, 3)
                act.wait_ge(k.panel_used, g0 + 2)
                act.copy(k.v_mem[:], ps[:, 2:4, 0:M])
                act.wait_ge(summed, 1)
                act.activation(logs[:], ps[:, 4, :].rearrange("p (m t) -> p m t", m=2), ACT.Ln, bias=k.eps[:, 0:1],
                               scale=1.0 / HD).then_inc(logged, 1)
                act.wait_ge(logged, 1)
                act.activation(rstd[:], logs[:], ACT.Exp, scale=-0.5).then_inc(rooted, 1)

            @block.vector
            def _(dve):
                mem.lows(dve)
                k.split_low(dve, g0, 0, 2)
                k.split_low(dve, g0, 0, 3)
                dve.wait_ge(rooted, 1)
                dve.scalar_tensor_tensor(k.k_mem[:], raw[:], gain, rstd[:], ALU.mult, ALU.mult)



def wait_block(eng, k, g0, made, i, b):
    if b % 2 == 0:
        eng.wait_ge(made, 4 * i + b // 2 + 1)
    else:
        eng.wait_ge(k.panel_used, 4 * i + (g0 + b // 2 + 1))


def stream_columns(pe, k, name, x, made, bank_free, need=lambda b: b + 1):
    g0, ps = k.first_panel[name], k.ps
    n = next(p[1] for p in k.phases if p[0] == name)

    def body(i, j):
        w_hi, w_lo = k.panel(pe, g0, i, j, KT, PW)
        for m in range(2):
            pe.wait_ge(bank_free, 8 * i + need(2 * j + m))
            at = slice(m * P, (m + 1) * P)
            for kt in range(KT):
                if isinstance(i, int) and i == j == m == 0:
                    x.ready(pe, kt)
                last = product(pe, ps[:, 2 * j + m, :], (w_hi[:, kt, at], w_lo[:, kt, at]), x.halves(kt), kt == 0, kt == KT - 1)
            last.then_inc(k.panel_used if m else made, 1)

    in_fours(pe, n, body)


def rwkv_in(k, slab):
    nc, ps, g0 = k.nc, k.ps, k.first_panel["rw_in"]
    mu, n_mu, n_all = k.col_a[:, ROW_A["rw_mu"]:ROW_A["rw_mu"] + 20], 20, 22
    with Phase(k, "rw_in") as f:
        z, step = f.sb("z", [P, 2, T + 1]), f.sb("step", [P, 2, T])
        x = Operand(k, f, k.xT, k.col_a[:, ROW_A["norm_mix_g"]:ROW_A["norm_mix_g"] + KT])
        made, bank_free, zeroed, stepped, shifted = (f.sem(s) for s in ("made", "bank_free", "zeroed", "stepped", "shifted"))
        with nc.Block() as block:

            @block.sync
            def _(sp):
                k.load_panels(sp, k.lookahead("rw_in"))

            @block.tensor
            def _(pe):
                stream_columns(pe, k, "rw_in", x, made, bank_free)

            @block.scalar
            def _(act):
                act.sem_inc(bank_free, 8)
                x.highs(act)
                for b in range(n_all):
                    wait_block(act, k, g0, made, 0, b)
                    if b % 2:
                        k.split_high(act, g0, 0, b // 2 + 2)
                    if b >= n_mu:
                        act.copy(slab[:, b, :], ps[:, b % 8, :]).then_inc(bank_free, 1)
                        continue
                    if b == 0:
                        act.wait_ge(zeroed, 1)
                    if b >= 2:
                        act.wait_ge(shifted, b - 1)
                    act.copy(z[:, b % 2, 1:T + 1], ps[:, b % 8, :]).then_inc(bank_free, 1)

            @block.vector
            def _(dve):
                dve.memset(z[:, :, 0:1], 0.0).then_inc(zeroed, 1)
                x.lows(dve)
                for b in range(n_all):
                    if b % 2:
                        k.split_low(dve, g0, 0, b // 2 + 2)
                    if b >= n_mu:
                        continue
                    dve.wait_ge(bank_free, 8 + b + 1)
                    if b >= 2:
                        dve.wait_ge(shifted, b - 1)
                    dve.tensor_tensor(step[:, b % 2, :], z[:, b % 2, 0:T], z[:, b % 2, 1:T + 1],
                                      ALU.subtract).then_inc(stepped, 1)
                    dve.wait_ge(stepped, b + 1)
                    dve.scalar_tensor_tensor(slab[:, b, :], step[:, b % 2, :], mu[:, b:b + 1], z[:, b % 2, 1:T + 1],
                                             ALU.mult, ALU.add).then_inc(shifted, 1)


def add_projection(k, name, x, kts, out=None, stats=True, split=False):
    nc, ps, g0 = k.nc, k.ps, k.first_panel[name]
    chunks, blocks = [], 0
    for n in kts:
        chunks.append((blocks, n))
        blocks += n
    res, pairs, n_chunks = (k.xT if out is None else out), KT // 2, len(kts)
    with Phase(k, name) as f:
        (made, taken), c_made, c_taken = k.projection_sems, pairs * k.projections, KT * k.projections
        k.projections += 1
        x = Operand(k, f, x) if split else x
        rows = Stats(k, f) if stats else None
        with nc.Block() as block:

            @block.sync
            def _(sp):
                k.load_panels(sp, k.lookahead(name))

            @block.tensor
            def _(pe):
                for i in range(pairs):
                    bank = 2 * (i % 3)
                    if i == 3:
                        pe.wait_ge(taken, c_taken + 2)
                    for c, (k0, n) in enumerate(chunks):
                        g = n_chunks * i + c
                        w_hi, w_lo = k.panel(pe, g0, g // 4, g % 4, n, PW)
                        for m in range(2):
                            at = slice(m * P, (m + 1) * P)
                            for kt in range(n):
                                if split and i == m == 0:
                                    x.ready(pe, k0 + kt)
                                last = product(pe, ps[:, bank + m, :], (w_hi[:, kt, at], w_lo[:, kt, at]), x.halves(k0 + kt),
                                               k0 + kt == 0, k0 + kt == blocks - 1)
                            if m:
                                last.then_inc(k.panel_used, 1)
                            elif c == n_chunks - 1:
                                last.then_inc(made, 1)
                        if stats and i and c == 0:
                            for b in (2 * i - 2, 2 * i - 1):
                                rows.count(pe, b)
                if stats:
                    for b in (KT - 2, KT - 1):
                        rows.count(pe, b)

            @block.scalar
            def _(act):
                if split:
                    x.highs(act)
                for i in range(pairs):
                    for c in range(n_chunks):
                        k.split_high(act, g0, 0, n_chunks * i + c + 2)
                    if stats:
                        for b in (2 * i, 2 * i + 1):
                            act.wait_ge(taken, c_taken + b + 1)
                            rows.square(act, b, res[:, b, :])
                if stats:
                    rows.root(act)

            @block.vector
            def _(dve):
                if split:
                    x.lows(dve)
                for i in range(pairs):
                    for c in range(n_chunks):
                        k.split_low(dve, g0, 0, n_chunks * i + c + 2)
                    for b in (2 * i, 2 * i + 1):
                        if b % 2 == 0:
                            dve.wait_ge(made, c_made + i + 1)
                        else:
                            dve.wait_ge(k.panel_used, g0 + n_chunks * (i + 1))
                        bank = ps[:, 2 * (i % 3) + b % 2, :]
                        if out is None:
                            dve.tensor_tensor(k.xT[:, b, :], bank, k.xT[:, b, :], ALU.add).then_inc(taken, 1)
                        else:
                            dve.tensor_copy(out[:, b, :], bank).then_inc(taken, 1)


class Hidden:

    def __init__(self, f, blocks):
        self.hi, self.lo = (f.sb(f"hidden_{s}", [P, blocks, T], F32R) for s in ("high", "low"))

    def halves(self, b):
        return self.hi[:, b, :], self.lo[:, b, :]


def squared_relu_ffn(k):
    nc, ps, blocks = k.nc, k.ps, 16
    with Phase(k, "ffn") as f:
        hidden = Hidden(f, blocks)
        x = Operand(k, f, k.xT, k.col_a[:, ROW_A["norm_ffn_g"]:ROW_A["norm_ffn_g"] + KT])
        for half in range(2):
            squared_relu_in(k, half, x, hidden, blocks)
            add_projection(k, f"ff2{half}", hidden, (8, 8), stats=half == 1)


def squared_relu_in(k, half, x, hidden, blocks):
    nc, ps, name = k.nc, k.ps, f"ff1{half}"
    g0 = k.first_panel[name]
    with Phase(k, name) as f:
        relu = f.sb("relu", [P, 4, T])
        made, bank_free, squared, high, low = (f.sem(s) for s in ("made", "bank_free", "squared", "high", "low"))
        with nc.Block() as block:

            @block.sync
            def _(sp):
                k.load_panels(sp, k.lookahead(name))

            @block.tensor
            def _(pe):
                stream_columns(pe, k, name, x, made, bank_free)

            @block.scalar
            def _(act):
                act.sem_inc(bank_free, 8)
                if half == 0:
                    x.highs(act)

                def high_of(b):
                    act.wait_ge(squared, b + 1)
                    act.copy(hidden.hi[:, b, :], relu[:, b % 4, :]).then_inc(high, 1)

                for b in range(blocks):
                    wait_block(act, k, g0, made, 0, b)
                    if b % 2:
                        k.split_high(act, g0, 0, b // 2 + 2)
                    if b >= 4:
                        act.wait_ge(low, b - 3)
                    act.activation(relu[:, b % 4, :], ps[:, b % 8, :], ACT.Relu).then_inc(bank_free, 1)
                    if b:
                        high_of(b - 1)
                high_of(blocks - 1)

            @block.vector
            def _(dve):
                if half == 0:
                    x.lows(dve)

                def low_of(b):
                    dve.wait_ge(high, b + 1)
                    dve.tensor_tensor(hidden.lo[:, b, :], relu[:, b % 4, :], hidden.hi[:, b, :], ALU.subtract).then_inc(low, 1)

                for b in range(blocks):
                    if b % 2:
                        k.split_low(dve, g0, 0, b // 2 + 2)
                    dve.wait_ge(bank_free, 8 + b + 1)
                    dve.tensor_tensor(relu[:, b % 4, :], relu[:, b % 4, :], relu[:, b % 4, :], ALU.mult).then_inc(squared, 1)
                    if b:
                        low_of(b - 1)
                low_of(blocks - 1)


def swiglu_in(k, layer, gain, hidden):
    nc, ps, name = k.nc, k.ps, f"gate_up{layer}"
    n, g0 = 2 * HID // PW, k.first_panel[name]
    with Phase(k, name) as f:
        gate = f.sb("gate", [P, 4, T])
        x = Operand(k, f, k.xT, gain, normed=gate[:, 0:2, :])
        made, bank_free, gated, high, low = (f.sem(s) for s in ("made", "bank_free", "gated", "high", "low"))
        with nc.Block() as block:

            @block.sync
            def _(sp):
                k.load_panels(sp, k.lookahead(name))

            @block.tensor
            def _(pe):
                stream_columns(pe, k, name, x, made, bank_free, need=lambda b: 4 * (b // 4) + 2 + 2 * (b % 2))

            def hidden_block(half, i, j, m):
                at = 4 * i + (j - 1 + m)
                return half[:, at, :] if isinstance(i, int) else half[:, bass.ds(at, 1), :].rearrange("p a t -> p (a t)")

            @block.scalar
            def _(act):
                act.sem_inc(low, 4)
                x.highs(act)

                def body(i, j):
                    if j % 2 == 0:
                        for m in range(2):
                            wait_block(act, k, g0, made, i, 2 * j + m)
                            act.wait_ge(low, 4 * i + j + m + 1)
                            act.activation(gate[:, j + m, :], ps[:, 2 * j + m, :], ACT.Silu).then_inc(gated, 1)
                        k.split_high(act, g0, i, j + 2)
                    else:
                        k.split_high(act, g0, i, j + 2)
                        for m in range(2):
                            act.wait_ge(bank_free, 8 * i + 8 + 4 * (j // 2) + 2 * m + 2)
                            act.copy(hidden_block(hidden.hi, i, j, m), gate[:, j - 1 + m, :]).then_inc(high, 1)

                in_fours(act, n, body)

            @block.vector
            def _(dve):
                dve.sem_inc(bank_free, 8)
                x.lows(dve)

                def body(i, j):
                    k.split_low(dve, g0, i, j + 2)
                    if j % 2 == 0:
                        return
                    for m in range(2):
                        wait_block(dve, k, g0, made, i, 2 * j + m)
                        dve.wait_ge(gated, 4 * i + j - 1 + m + 1)
                        here = gate[:, j - 1 + m, :]
                        dve.tensor_tensor(here, here, ps[:, 2 * j + m, :], ALU.mult).then_inc(bank_free, 2)
                    for m in range(2):
                        dve.wait_ge(high, 4 * i + j - 1 + m + 1)
                        dve.tensor_tensor(hidden_block(hidden.lo, i, j, m), gate[:, j - 1 + m, :], hidden_block(hidden.hi, i, j, m),
                                          ALU.subtract).then_inc(low, 1)

                in_fours(dve, n, body)



class Steps:

    def __init__(self, f, name, steps):
        self.sem, self.n, self.at = f.sem(name), len(steps), {s: i for i, s in enumerate(steps)}
        self.next = 0

    def begin(self, eng):
        eng.sem_inc(self.sem, self.n)

    def did(self, name, ins):
        if self.at[name] != self.next % self.n:
            raise ValueError(f"step {name} out of order")
        self.next += 1
        ins.then_inc(self.sem, 1)

    def wait(self, eng, name, rnd, back=0):
        eng.wait_ge(self.sem, self.n * rnd + (self.n * (1 - back) + self.at[name] + 1))


SLAB_R, SLAB_K, SLAB_V, SLAB_WA, SLAB_G, SLAB_Q = 0, 6, 12, 18, 19, 20


def decay_and_rate(k, slab, lw, rate):
    nc, ps, ins = k.nc, k.ps, k.ins
    with Phase(k, "lora") as f:
        low = f.sb("weights", [P, MIX])
        landed, squashed, made, done = f.sem("landed"), f.sem("squashed"), f.sem("made"), f.sem("done")
        w0, a0 = (k.col_a[:, ROW_A[n]:ROW_A[n] + PAIRS] for n in ("rw_w0", "rw_a0"))
        with nc.Block() as block:

            @block.sync
            def _(sp):
                sp.dma_start(low[0:HD, :], ins["rw_w2"][0]).then_inc(landed, 16)
                sp.dma_start(low[HD:P, :], ins["rw_a2"][0]).then_inc(landed, 16)

            @block.scalar
            def _(act):
                act.activation(slab[0:HD, SLAB_WA, :], slab[0:HD, SLAB_WA, :], ACT.Tanh).then_inc(squashed, 1)
                for p in range(PAIRS):
                    act.wait_ge(made, 2 * p + 1)
                    act.activation(lw[:, p, :], ps[:, 2 * (p % 4), :], ACT.Sigmoid, bias=w0[:, p:p + 1]).then_inc(done, 1)
                    act.wait_ge(made, 2 * p + 2)
                    act.activation(rate[:, p, :], ps[:, 2 * (p % 4) + 1, :], ACT.Sigmoid, bias=a0[:, p:p + 1]).then_inc(done, 1)
                act.activation(slab[:, SLAB_G, :], slab[:, SLAB_G, :], ACT.Sigmoid)

            @block.tensor
            def _(pe):
                pe.wait_ge(landed, 32)
                pe.wait_ge(squashed, 1)
                for p in range(PAIRS):
                    for half in range(2):
                        if p >= 4:
                            pe.wait_ge(done, 2 * (p - 4) + half + 1)
                        rows = slice(half * HD, (half + 1) * HD)
                        pe.matmul(ps[:, 2 * (p % 4) + half, :], low[rows, p * P:(p + 1) * P], slab[rows, SLAB_WA, :],
                                  start=True, stop=True).then_inc(made, 1)


LEVELS = range(1, 6)
PREP_ACT = ["k_squared", "v_still", "kk_log", "kk_root", "e_pos", "e_neg", "e_prev", "pass"]
PREP_DVE = ["cum", "k_part", "k_new", "kk_clip", "kk", "rk", "ah", "bonus", "rh_kept"]
PREP_POOL = ["mid", "mid_prev", "ends", "passes", "b", "bh", "kh", "rh"]
PREP_PE = ["kk_sum", "rk_sum"]


def main_steps():
    both = range(2)
    act = [f"tok{q}" for q in range(TT)] + [f"ab{e}" for e in both]
    dve = [f"{n}{e}" for e in both for n in ("inv_T", "rb")] + [f"{n}{e}" for e in both for n in ("ak", "rk")]
    pool = [f"{n}{e}" for e in both for n in ("inv", "inv_eye", "inv_T_eye", "below1_")]
    pe = [f"turn{q}" for q in range(TT)] + [f"a1_{e}" for e in both] + [f"a2_{e}" for e in both]
    for lv in LEVELS:
        pe += [f"x{e}_{lv}" for e in both] + [f"tm{e}_{lv}" for e in both]
        act += [f"x{e}_{lv}" for e in both]
        dve += [f"{n}{e}_{lv}" for e in both for n in (("t", "m") if lv < 5 else ("m",))]
        pool += [f"below{lv + 1}_{e}" for e in both if lv < 5]
    pe += [f"{n}{e}" for n in ("av", "wu") for e in both] + ["out"]
    act += [f"{n}{e}" for n in ("a_side", "av", "wu") for e in both] + ["h", "y"]
    dve += ["g", "q"]
    return act, dve, pool, pe


def scan_chunks(k, slab, lw, rate, passes, mix):
    nc, ps = k.nc, k.ps
    cols = {n: k.col_a[:, ROW_A[n]:ROW_A[n] + PAIRS] for n in ("rw_k_k", "rw_k_a", "rw_r_k")}
    with Phase(k, "scan") as f:
        sq, rn, kk, kn, cum, mid, v_st, e_pos = (mix[:, i, :] for i in range(8))
        prev = slab[:, SLAB_WA, :]
        rk_sum, ah, kh = sq, kk, kn
        bh, rh = f.sb("bh", [P, T]), f.sb("rh", [P, T])
        tok = f.sb("tok", [P, TT, 4, P])
        ends = f.sb("ends", [P, NCH - 1])

        def two(name):
            return [f.sb(f"{name}{e}", [P, TT, P]) for e in range(2)]

        ab, below, inv, inv_T, x, ak_T, rb_T, rk_T = (two(s) for s in ("ab", "below", "inv", "inv_T", "x", "ak", "rb", "rkT"))
        a_av, w_u = below, x
        act_s, dve_s, pool_s, pe_s = (Steps(f, n, s) for n, s in zip(
            ("act_done", "vector_done", "pool_done", "tensor_done"), main_steps()))
        act_p, dve_p, pool_p, pe_p = (Steps(f, n, s) for n, s in zip(
            ("act_prepared", "vector_prepared", "pool_prepared", "tensor_prepared"),
            (PREP_ACT, PREP_DVE, PREP_POOL, PREP_PE)))

        def blk(t, i):
            return t[:, i, :] if isinstance(i, int) else t[:, bass.ds(i, 1), :].rearrange("p a t -> p (a t)")

        def col(t, i):
            return t[:, i:i + 1] if isinstance(i, int) else t[:, bass.ds(i, 1)]

        def per_chunk(t):
            return t.rearrange("p (c t) -> p c t", c=NCH)

        def tiles(t):
            return t.rearrange("p (q t) -> p q t", q=TT)

        def on_tiles(mask):
            return mask[:].unsqueeze(1).broadcast_to([P, TT, P])

        def pair_of(bank, which):
            return ps[:, bank:bank + 2, :].rearrange("p b (q w t) -> p (b q) w t", q=2, w=2)[:, :, which, :]

        def four(bank):
            return ps[:, bank, :].rearrange("p (q t) -> p q t", q=TT)

        def by_parity(t):
            return t.rearrange("p (q c k) -> p c q k", c=2, k=HD)

        def halves(bank):
            return ps[:, bank:bank + 2, 0:TT * HD].rearrange("p c (q k) -> p c q k", q=TT)

        mids = per_chunk(cum)[:, :, CH // 2 - 1:CH // 2]

        with nc.Block() as block:

            @block.scalar
            def _(act):
                act_s.begin(act)
                act_p.begin(act)

                def prep(p, slot):
                    if slot == 1:
                        pe_p.wait(act, "rk_sum", p, 1)
                        act_p.did("k_squared", act.activation(sq, blk(slab, SLAB_K + p), ACT.Square, scale=col(cols["rw_k_k"], p)))
                        pe_s.wait(act, "turn3", p, 1)
                        dve_p.wait(act, "bonus", p, 1)
                        act_p.did("v_still", act.copy(v_st[:], blk(slab, SLAB_V + p)))
                    if slot == 2:
                        dve_p.wait(act, "kk_clip", p)
                        act_p.did("kk_log", act.activation(rn, rn, ACT.Ln, scale=KK_SCALE))
                        act_p.wait(act, "kk_log", p)
                        act_p.did("kk_root", act.activation(rn, rn, ACT.Exp, scale=-0.5, bias=k.eps[:, 2:3]))
                    if slot == 3:
                        pool_p.wait(act, "mid", p)
                        dve_p.wait(act, "rh_kept", p, 1)
                        act_p.did("e_pos", act.activation(e_pos, mid, ACT.Exp, scale=-LOG_DECAY))
                        pool_p.wait(act, "mid_prev", p)
                        act_p.wait(act, "e_pos", p)
                        act_p.did("e_neg", act.activation(mid, mid, ACT.Exp, scale=LOG_DECAY))
                        act_p.did("e_prev", act.activation(prev, prev, ACT.Exp, scale=-LOG_DECAY))
                        pool_p.wait(act, "passes", p)
                        act_p.did("pass", act.activation(blk(passes, p), ends[:], ACT.Exp, scale=-LOG_DECAY))

                def main(p, prep_next):
                    for q in range(TT):
                        pe_s.wait(act, f"turn{q}", p)
                        if q == 0:
                            pe_s.wait(act, "out", p, 1)
                        act_s.did(f"tok{q}", act.copy(tok[:, q, :, :], four((6, 4, 5, 6)[q])))
                    for e in range(2):
                        pe_s.wait(act, f"a1_{e}", p)
                        pool_s.wait(act, f"below5_{e}", p, 1)
                        act_s.did(f"ab{e}", act.copy(ab[e][:], four(3 * e)))
                    for lv in LEVELS:
                        for e in range(2):
                            pe_s.wait(act, f"x{e}_{lv}", p)
                            act_s.did(f"x{e}_{lv}", act.copy(x[e][:], four(3 * e)))
                        if prep_next and lv < 5:
                            prep(p + 1, lv)
                    for e in range(2):
                        act_s.wait(act, "tok3", p)
                        act_s.did(f"a_side{e}", act.copy(a_av[e][:, :, 0:HD], tok[:, :, 0, e * HD:(e + 1) * HD]))
                    for e in range(2):
                        pe_s.wait(act, f"av{e}", p)
                        act_s.did(f"av{e}", act.copy(a_av[e][:, :, HD:P], ps[:, 3 * e, 0:TT * HD].rearrange("p (q v) -> p q v", q=TT)))
                    for e in range(2):
                        pe_s.wait(act, f"wu{e}", p)
                        act_s.did(f"wu{e}", act.copy(w_u[e][:], four(3 * e + 1)))
                    pe_s.wait(act, "out", p)
                    act_s.did("h", act.copy(by_parity(blk(rate, p)), halves(4)))
                    act_s.did("y", act.copy(blk(slab, SLAB_K + p), ps[:, 3, :]))

                for slot in range(1, 5):
                    prep(0, slot)
                with act.Fori(0, PAIRS - 1) as p:
                    main(p, True)
                main(PAIRS - 1, False)

            @block.vector
            def _(dve):
                dve_s.begin(dve)
                dve_p.begin(dve)

                def prep(p, slot):
                    if slot == 1:
                        pool_p.wait(dve, "passes", p, 1)
                        dve_p.did("cum", dve.tensor_tensor_scan(cum, k.restart[:], blk(lw, p), 0.0, ALU.mult, ALU.add))
                        pe_s.wait(dve, "a2_1", p, 1)
                        pool_p.wait(dve, "kh", p, 1)
                        dve_p.wait(dve, "rk", p, 1)
                        dve_p.did("k_part", dve.scalar_tensor_tensor(kn, blk(rate, p), 1.0, blk(slab, SLAB_K + p), ALU.subtract, ALU.mult))
                        dve_p.wait(dve, "k_part", p)
                        dve_p.did("k_new", dve.scalar_tensor_tensor(kn, kn, col(cols["rw_k_a"], p), blk(slab, SLAB_K + p), ALU.mult, ALU.add))
                    if slot == 2:
                        pe_p.wait(dve, "kk_sum", p)
                        dve_p.wait(dve, "kk", p, 1)
                        dve_p.did("kk_clip", dve.tensor_scalar(rn, ps[:, 7, :], 1e-24, None, ALU.max))
                    if slot == 3:
                        act_p.wait(dve, "kk_root", p)
                        pe_s.wait(dve, "a2_1", p, 1)
                        pool_p.wait(dve, "b", p, 1)
                        dve_p.wait(dve, "ah", p, 1)
                        dve_p.did("kk", dve.scalar_tensor_tensor(kk, blk(slab, SLAB_K + p), col(cols["rw_k_k"], p), rn, ALU.mult, ALU.mult))
                        pe_p.wait(dve, "rk_sum", p, 1)
                        dve_p.wait(dve, "k_new", p)
                        dve_p.did("rk", dve.scalar_tensor_tensor(rk_sum[:], blk(slab, SLAB_R + p), col(cols["rw_r_k"], p), kn, ALU.mult, ALU.mult))
                    if slot == 4:
                        act_p.wait(dve, "e_prev", p)
                        dve_p.wait(dve, "kk", p)
                        pool_p.wait(dve, "b", p)
                        dve_p.did("ah", dve.scalar_tensor_tensor(ah[:], kk, -1.0, prev, ALU.mult, ALU.mult))
                        pe_p.wait(dve, "rk_sum", p)
                        act_p.wait(dve, "v_still", p)
                        dve_p.did("bonus", dve.tensor_tensor(blk(slab, SLAB_V + p), ps[:, 7, :], v_st[:], ALU.mult))
                        pool_p.wait(dve, "rh", p)
                        dve_p.wait(dve, "rk", p)
                        dve_p.did("rh_kept", dve.tensor_tensor(blk(slab, SLAB_R + p), blk(slab, SLAB_R + p), e_pos, ALU.mult))

                def main(p, prep_next):
                    for e in range(2):
                        pe_s.wait(dve, f"a1_{e}", p)
                        dve_s.did(f"inv_T{e}", dve.tensor_tensor(inv_T[e][:], pair_of(3 * e + 1, 0), on_tiles(k.level0_T), ALU.mult))
                        pe_s.wait(dve, "out", p, 1)
                        dve_s.did(f"rb{e}", dve.tensor_tensor(rb_T[e][:], pair_of(3 * e + 1, 1), on_tiles(k.upto_T), ALU.mult))
                    for e in range(2):
                        pe_s.wait(dve, f"a2_{e}", p)
                        dve_s.did(f"ak{e}", dve.tensor_tensor(ak_T[e][:], pair_of(3 * e + 1, 0), on_tiles(k.before_T), ALU.mult))
                        dve_s.did(f"rk{e}", dve.tensor_tensor(rk_T[e][:], pair_of(3 * e + 1, 1), on_tiles(k.upto_T), ALU.mult))
                    for lv in LEVELS:
                        for e in range(2):
                            pe_s.wait(dve, f"tm{e}_{lv}", p)
                            if lv == 1:
                                pool_s.wait(dve, f"inv_T_eye{e}", p)
                            if lv < 5:
                                dve_s.did(f"t{e}_{lv}", dve.tensor_tensor(inv[e][:], four(3 * e + 1), inv[e][:], ALU.add))
                            if lv > 1:
                                dve_s.wait(dve, f"m{e}_{lv - 1}", p)
                            dve_s.did(f"m{e}_{lv}", dve.tensor_tensor(inv_T[e][:], four(3 * e + 2), inv_T[e][:], ALU.add))
                        if prep_next and lv < 5:
                            prep(p + 1, lv)
                    pe_s.wait(dve, "out", p)
                    eye = k.eye64[:].unsqueeze(1).unsqueeze(1).broadcast_to([P, 2, TT, HD])
                    dve_s.did("g", dve.tensor_tensor(by_parity(blk(lw, p)), halves(0), eye, ALU.add))
                    dve_p.wait(dve, "rh_kept", p)
                    dve_s.did("q", dve.tensor_tensor(blk(slab, SLAB_R + p), ps[:, 2, :], blk(slab, SLAB_R + p), ALU.add))

                for slot in range(1, 5):
                    prep(0, slot)
                with dve.Fori(0, PAIRS - 1) as p:
                    main(p, True)
                main(PAIRS - 1, False)

            @block.gpsimd
            def _(pool):
                pool_s.begin(pool)
                pool_p.begin(pool)

                def prep(p, slot):
                    if slot == 2:
                        dve_p.wait(pool, "cum", p)
                        pool_p.wait(pool, "bh", p, 1)
                        pool_p.wait(pool, "kh", p, 1)
                        pool_p.did("mid", pool.tensor_tensor(per_chunk(mid), per_chunk(cum), mids.broadcast_to([P, NCH, CH]), ALU.subtract))
                        pool_p.wait(pool, "mid", p)
                        dve_p.wait(pool, "ah", p, 1)
                        pool_p.did("mid_prev", pool.tensor_tensor(prev, mid, blk(lw, p), ALU.subtract))
                        act_p.wait(pool, "pass", p, 1)
                        pool_p.did("ends", pool.tensor_tensor(ends[:].unsqueeze(2), per_chunk(cum)[:, 0:NCH - 1, CH - 1:CH], mids[:, 0:NCH - 1], ALU.subtract))
                        pool_p.wait(pool, "ends", p)
                        pool_p.did("passes", pool.tensor_tensor(ends[:].unsqueeze(2), ends[:].unsqueeze(2), mids[:, 1:NCH], ALU.add))
                    if slot == 3:
                        dve_p.wait(pool, "kk", p)
                        pe_s.wait(pool, "a2_1", p, 1)
                        pool_p.did("b", pool.tensor_tensor(bh[:], kk, blk(rate, p), ALU.mult))
                        act_p.wait(pool, "e_neg", p)
                        pool_p.wait(pool, "b", p)
                        pool_p.did("bh", pool.tensor_tensor(bh[:], bh[:], mid, ALU.mult))
                        dve_p.wait(pool, "rk", p)
                        pool_p.did("kh", pool.tensor_tensor(kh[:], kn, mid, ALU.mult))
                    if slot == 4:
                        act_p.wait(pool, "e_pos", p)
                        pool_p.did("rh", pool.tensor_tensor(rh[:], blk(slab, SLAB_R + p), e_pos, ALU.mult))

                def main(p, prep_next):
                    for e in range(2):
                        act_s.wait(pool, f"ab{e}", p)
                        pool_s.did(f"inv{e}", pool.tensor_tensor(inv[e][:], ab[e][:], on_tiles(k.level[:, 0, :]), ALU.mult))
                        pool_s.wait(pool, f"inv{e}", p)
                        pool_s.did(f"inv_eye{e}", pool.tensor_tensor(inv[e][:], inv[e][:], on_tiles(k.ident), ALU.add))
                        dve_s.wait(pool, f"inv_T{e}", p)
                        pool_s.did(f"inv_T_eye{e}", pool.tensor_tensor(inv_T[e][:], inv_T[e][:], on_tiles(k.ident), ALU.add))
                        pe_s.wait(pool, f"wu{e}", p, 1)
                        pool_s.did(f"below1_{e}", pool.tensor_tensor(below[e][:], ab[e][:], on_tiles(k.level[:, 1, :]), ALU.mult))
                    for lv in range(1, 5):
                        for e in range(2):
                            pe_s.wait(pool, f"x{e}_{lv}", p)
                            pool_s.did(f"below{lv + 1}_{e}", pool.tensor_tensor(below[e][:], ab[e][:], on_tiles(k.level[:, lv + 1, :]), ALU.mult))
                        if prep_next:
                            prep(p + 1, lv)

                for slot in range(1, 5):
                    prep(0, slot)
                with pool.Fori(0, PAIRS - 1) as p:
                    main(p, True)
                main(PAIRS - 1, False)

            @block.tensor
            def _(pe):
                pe_s.begin(pe)
                pe_p.begin(pe)

                def mm(out, lhsT, rhs, start=True, stop=True):
                    return pe.matmul(out, lhsT, rhs, start=start, stop=stop)

                def prep(p, slot):
                    if slot == 1:
                        act_p.wait(pe, "k_squared", p)
                        dve_p.wait(pe, "bonus", p, 1)
                        pe_p.did("kk_sum", mm(ps[:, 7, :], k.head_ones[:], sq))
                    if slot == 4:
                        dve_p.wait(pe, "kk_clip", p)
                        dve_p.wait(pe, "rk", p)
                        pe_p.did("rk_sum", mm(ps[:, 7, :], k.head_ones[:], rk_sum[:]))

                def main(p, prep_next):
                    dve_p.wait(pe, "ah", p)
                    pool_p.wait(pe, "rh", p)
                    act_p.wait(pe, "v_still", p)
                    act_s.wait(pe, "tok3", p, 1)
                    for q in range(TT):
                        if q == 1:
                            act_s.wait(pe, "h", p, 1)
                            dve_s.wait(pe, "g", p, 1)
                        if q == 3:
                            act_s.wait(pe, "tok0", p)
                        for n, src in enumerate((ah, bh, kh, v_st)):
                            last = pe.transpose(ps[:, (6, 4, 5, 6)[q], n * P:(n + 1) * P], src[:, q * P:(q + 1) * P], k.ident[:])
                        pe_s.did(f"turn{q}", last)
                    act_s.wait(pe, "y", p, 1)
                    dve_s.wait(pe, "q", p, 1)
                    for e in range(2):
                        rows = slice(e * HD, (e + 1) * HD)
                        if e == 1:
                            act_s.wait(pe, "tok3", p)
                        for q in range(TT):
                            at = slice(q * P, (q + 1) * P)
                            mm(ps[:, 3 * e, at], ah[rows, at], bh[rows, at])
                        for q in range(TT):
                            at, bank, c = slice(q * P, (q + 1) * P), 3 * e + 1 + q // 2, (q % 2) * 2 * P
                            mm(ps[:, bank, c:c + P], bh[rows, at], ah[rows, at])
                            last = mm(ps[:, bank, c + P:c + 2 * P], bh[rows, at], rh[rows, at])
                        pe_s.did(f"a1_{e}", last)
                    for e in range(2):
                        rows = slice(e * HD, (e + 1) * HD)
                        dve_s.wait(pe, f"rb{e}", p)
                        for q in range(TT):
                            at, bank, c = slice(q * P, (q + 1) * P), 3 * e + 1 + q // 2, (q % 2) * 2 * P
                            mm(ps[:, bank, c:c + P], kh[rows, at], ah[rows, at])
                            last = mm(ps[:, bank, c + P:c + 2 * P], kh[rows, at], rh[rows, at])
                        pe_s.did(f"a2_{e}", last)
                    for lv in LEVELS:
                        for e in range(2):
                            pool_s.wait(pe, f"below{lv}_{e}", p)
                            if lv == 1:
                                act_s.wait(pe, f"ab{e}", p)
                            else:
                                act_s.wait(pe, f"x{e}_{lv - 1}", p)
                                dve_s.wait(pe, f"m{e}_{lv - 1}", p)
                            for q in range(TT):
                                last = mm(ps[:, 3 * e, q * P:(q + 1) * P], below[e][:, q, :], inv_T[e][:, q, :])
                            pe_s.did(f"x{e}_{lv}", last)
                        for e in range(2):
                            act_s.wait(pe, f"x{e}_{lv}", p)
                            if lv == 1:
                                dve_s.wait(pe, f"rk{e}", p)
                            for q in range(TT):
                                at = slice(q * P, (q + 1) * P)
                                if lv < 5:
                                    mm(ps[:, 3 * e + 1, at], x[e][:, q, :], inv[e][:, q, :])
                                last = mm(ps[:, 3 * e + 2, at], inv[e][:, q, :], x[e][:, q, :])
                            pe_s.did(f"tm{e}_{lv}", last)
                        if prep_next and lv < 5:
                            prep(p + 1, lv)
                    for e in range(2):
                        for q in range(TT):
                            last = mm(ps[:, 3 * e, q * HD:(q + 1) * HD], ak_T[e][:, q, :], tok[:, q, 3, e * HD:(e + 1) * HD])
                        pe_s.did(f"av{e}", last)
                    for e in range(2):
                        act_s.wait(pe, f"av{e}", p)
                        dve_s.wait(pe, f"m{e}_5", p)
                        for q in range(TT):
                            last = mm(ps[:, 3 * e + 1, q * P:(q + 1) * P], inv_T[e][:, q, :], a_av[e][:, q, :])
                        pe_s.did(f"wu{e}", last)
                    for e in range(2):
                        act_s.wait(pe, f"wu{e}", p)
                        if e == 0:
                            act_s.wait(pe, "wu1", p)
                        rows, w, u = slice(e * HD, (e + 1) * HD), slice(0, HD), slice(HD, P)
                        for q in range(TT):
                            at = slice(q * P, (q + 1) * P)
                            mm(ps[rows, 2, at], w_u[e][:, q, w], rb_T[e][:, q, :])
                            mm(ps[rows, 3, at], w_u[e][:, q, u], rb_T[e][:, q, :], stop=False)
                            mm(ps[rows, 3, at], tok[:, q, 3, rows], rk_T[e][:, q, :], start=False)
                            for c in range(2):
                                cs, to = slice(c * CH, (c + 1) * CH), slice(q * HD, (q + 1) * HD)
                                mm(ps[rows, c, to], w_u[e][cs, q, w], tok[cs, q, 1, rows])
                                mm(ps[rows, 4 + c, to], tok[cs, q, 1, rows], w_u[e][cs, q, u], stop=False)
                                last = mm(ps[rows, 4 + c, to], tok[cs, q, 2, rows], tok[cs, q, 3, rows], start=False)
                    pe_s.did("out", last)

                for slot in range(1, 5):
                    prep(0, slot)
                with pe.Fori(0, PAIRS - 1) as p:
                    main(p, True)
                main(PAIRS - 1, False)


def scan_states(k, slab, lw, rate, passes):
    nc, ps = k.nc, k.ps
    with Phase(k, "states") as f:
        state = f.sb("state", [P, NCH - 1, PAIRS, HD])
        moved, grown, passed, read, added = (f.sem(s) for s in ("moved", "grown", "passed", "read", "added"))

        def chunk(t, n, pairs=slice(0, PAIRS)):
            return t[:, pairs, n * CH:(n + 1) * CH]

        with nc.Block() as block:

            @block.tensor
            def _(pe):
                def outputs(n):
                    for p in range(PAIRS):
                        for e in range(2):
                            rows = slice(e * HD, (e + 1) * HD)
                            last = pe.matmul(ps[rows, 2 + p, (n + 1) * CH:(n + 2) * CH], state[rows, n, p, :],
                                             slab[rows, SLAB_R + p, (n + 1) * CH:(n + 2) * CH], start=True, stop=True)
                    last.then_inc(read, 1)

                for n in range(NCH - 2):
                    pe.wait_ge(passed, n + 1)
                    if n >= 2:
                        pe.wait_ge(grown, n - 1)
                    for p in range(PAIRS):
                        for e in range(2):
                            rows = slice(e * HD, (e + 1) * HD)
                            last = pe.matmul(ps[rows, n % 2, p * HD:(p + 1) * HD], lw[rows, p, (n + 1) * CH:(n + 2) * CH],
                                             state[rows, n, p, :], start=True, stop=True)
                    last.then_inc(moved, 1)
                    outputs(n)
                pe.wait_ge(passed, NCH - 1)
                outputs(NCH - 2)

            @block.vector
            def _(dve):
                def by_pass(n):
                    return passes[:, :, n:n + 1].broadcast_to([P, PAIRS, HD])

                dve.tensor_tensor(state[:, 0], chunk(rate, 0), by_pass(0), ALU.mult).then_inc(passed, 1)
                for n in range(1, NCH - 1):
                    dve.wait_ge(moved, n)
                    dve.tensor_tensor(state[:, n], ps[:, (n - 1) % 2, 0:PAIRS * HD].rearrange("p (h v) -> p h v", h=PAIRS),
                                      chunk(rate, n), ALU.add).then_inc(grown, 1)
                    dve.wait_ge(grown, n)
                    dve.tensor_tensor(state[:, n], state[:, n], by_pass(n), ALU.mult).then_inc(passed, 1)
                dve.wait_ge(read, NCH - 1)
                for p in range(PAIRS):
                    y = slab[:, SLAB_K + p, CH:T]
                    dve.tensor_tensor(y, ps[:, 2 + p, CH:T], y, ALU.add)


def rwkv_out(k, slab, mix):
    nc, ps, ins = k.nc, k.ps, k.ins
    gain, shift = (k.col_a[:, ROW_A[n]:ROW_A[n] + PAIRS] for n in ("rw_lnx_g", "rw_lnx_b"))
    with Phase(k, "rwkv_out") as f:
        g2, mean_of = f.sb("g2", [P, MIX]), f.sb("mean_of", [P, P])
        logs, rstd, out = f.sb("logs", [P, 2, T]), f.sb("rstd", [P, 2, T]), mix
        landed, meant, averaged, centred, squared, spread, logged, rooted, scaled, shifted, gated = (f.sem(s) for s in (
            "landed", "meant", "averaged", "centred", "squared", "spread", "logged", "rooted", "scaled", "shifted", "gated"))
        with nc.Block() as block:

            @block.sync
            def _(sp):
                sp.dma_start(g2[:], ins["rw_g2"][0]).then_inc(landed, 16)

            @block.tensor
            def _(pe):
                pe.wait_ge(landed, 16)
                pe.wait_ge(meant, 1)

                def mean(p):
                    if p >= 2:
                        pe.wait_ge(centred, p - 1)
                    pe.matmul(ps[:, p % 2, :], mean_of[:], slab[:, SLAB_K + p, :], start=True, stop=True).then_inc(averaged, 1)

                mean(0)
                for p in range(PAIRS):
                    if p + 1 < PAIRS:
                        mean(p + 1)
                    pe.wait_ge(squared, p + 1)
                    if p >= 2:
                        pe.wait_ge(logged, p - 1)
                    pe.matmul(ps[:, 2 + p % 2, :], mean_of[:], out[:, p, :], start=True, stop=True).then_inc(spread, 1)
                    if p >= 2:
                        pe.wait_ge(gated, p - 1)
                    pe.matmul(ps[:, 4 + p % 2, :], g2[:, p * P:(p + 1) * P], slab[:, SLAB_G, :], start=True, stop=True)\
                        .then_inc(spread, 1)

            @block.vector
            def _(dve):
                dve.tensor_scalar(mean_of[:], k.head_ones[:], 1.0 / HD, None, ALU.mult).then_inc(meant, 1)

                def centre(p):
                    dve.wait_ge(averaged, p + 1)
                    y = slab[:, SLAB_K + p, :]
                    dve.tensor_tensor(y, y, ps[:, p % 2, :], ALU.subtract).then_inc(centred, 1)

                centre(0)
                for p in range(PAIRS):
                    if p + 1 < PAIRS:
                        centre(p + 1)
                    y = slab[:, SLAB_K + p, :]
                    dve.wait_ge(rooted, p + 1)
                    dve.scalar_tensor_tensor(y, y, gain[:, p:p + 1], rstd[:, p % 2, :], ALU.mult, ALU.mult).then_inc(scaled, 1)
                    dve.wait_ge(scaled, p + 1)
                    dve.scalar_tensor_tensor(y, y, shift[:, p:p + 1], slab[:, SLAB_V + p, :], ALU.add, ALU.add).then_inc(shifted, 1)
                    dve.wait_ge(shifted, p + 1)
                    dve.wait_ge(spread, 2 * p + 2)
                    dve.tensor_tensor(out[:, p, :], y, ps[:, 4 + p % 2, :], ALU.mult).then_inc(gated, 1)

            @block.scalar
            def _(act):
                for p in range(PAIRS):
                    act.wait_ge(centred, p + 1)
                    act.activation(out[:, p, :], slab[:, SLAB_K + p, :], ACT.Square).then_inc(squared, 1)
                    act.wait_ge(spread, 2 * p + 1)
                    if p >= 2:
                        act.wait_ge(rooted, p - 1)
                    act.activation(logs[:, p % 2, :], ps[:, 2 + p % 2, :], ACT.Ln, bias=k.eps[:, 1:2]).then_inc(logged, 1)
                    act.wait_ge(logged, p + 1)
                    if p >= 2:
                        act.wait_ge(scaled, p - 1)
                    act.activation(rstd[:, p % 2, :], logs[:, p % 2, :], ACT.Exp, scale=-0.5).then_inc(rooted, 1)


def memory_attention(k, slab, mix):
    nc, ps = k.nc, k.ps
    gain = k.col_a[:, ROW_A["mem_q_norm_g"]:ROW_A["mem_q_norm_g"] + 1]
    heads, scale = 4, HD ** -0.5
    with Phase(k, "mem_attn") as f:
        q, squares, logs, rstd = (f.sb(s, [P, 2, T]) for s in ("q", "squares", "logs", "rstd"))
        probs = f.sb("probs", [P, 2, TT, M])
        probs_T = f.sb("probs_T", [P, 2, 2, T])
        top, total, inv = (f.sb(s, [P, heads, TT]) for s in ("top", "total", "inv"))
        squared, summed, logged, rooted, normed = (f.sem(s) for s in ("squared", "summed", "logged", "rooted", "normed"))
        scored, topped, negated, exped, inverted, scaled, turned, copied, mixed, kept = (f.sem(s) for s in (
            "scored", "topped", "negated", "exped", "inverted", "scaled", "turned", "copied", "mixed", "kept"))
        with nc.Block() as block:

            @block.tensor
            def _(pe):
                pe.wait_ge(squared, 1)
                for m in range(2):
                    last = pe.matmul(ps[:, m, :], k.head_ones[:], squares[:, m, :], start=True, stop=True)
                last.then_inc(summed, 1)
                pe.wait_ge(normed, 1)

                def scores(h):
                    rows = slice((h % 2) * HD, (h % 2 + 1) * HD)
                    if h:
                        pe.wait_ge(exped, TT * h)
                    for t in range(TT):
                        last = pe.matmul(ps[:, 2 + t // 2, (t % 2) * M:(t % 2 + 1) * M], q[rows, h // 2, t * P:(t + 1) * P],
                                         k.k_mem[rows, h // 2, :], start=True, stop=True)
                    last.then_inc(scored, 1)

                scores(0)
                for h in range(heads):
                    if h + 1 < heads:
                        scores(h + 1)
                    pe.wait_ge(scaled, h + 1)
                    if h:
                        pe.wait_ge(copied, h)
                    for m in range(2):
                        for t in range(TT):
                            last = pe.transpose(ps[:, 4 + m, t * P:(t + 1) * P], probs[:, h % 2, t, m * P:(m + 1) * P], k.ident[:])
                    last.then_inc(turned, 1)
                    pe.wait_ge(copied, h + 1)
                    if h >= 2:
                        pe.wait_ge(kept, h - 1)
                    rows = slice((h % 2) * HD, (h % 2 + 1) * HD)
                    for m in range(2):
                        last = pe.matmul(ps[rows, 6 + h % 2, :], k.v_mem[:, m, h * HD:(h + 1) * HD], probs_T[:, h % 2, m, :],
                                         start=m == 0, stop=m == 1)
                    last.then_inc(mixed, 1)

            @block.scalar
            def _(act):
                act.activation(squares[:], slab[:, SLAB_Q:SLAB_Q + 2, :], ACT.Square).then_inc(squared, 1)
                act.wait_ge(summed, 1)
                act.activation(logs[:], ps[:, 0:2, :], ACT.Ln, bias=k.eps[:, 0:1], scale=1.0 / HD).then_inc(logged, 1)
                act.wait_ge(logged, 1)
                act.activation(rstd[:], logs[:], ACT.Exp, scale=-0.5).then_inc(rooted, 1)
                for h in range(heads):
                    act.wait_ge(negated, h + 1)
                    if h >= 2:
                        act.wait_ge(turned, h - 1)
                    for t in range(TT):
                        act.activation(probs[:, h % 2, t, :], ps[:, 2 + t // 2, (t % 2) * M:(t % 2 + 1) * M], ACT.Exp,
                                       bias=top[:, h, t:t + 1], scale=scale, accum_out=total[:, h, t:t + 1]).then_inc(exped, 1)
                    act.wait_ge(turned, h + 1)
                    if h >= 2:
                        act.wait_ge(mixed, h - 1)
                    act.copy(probs_T[:, h % 2], ps[:, 4:6, :]).then_inc(copied, 1)

            @block.vector
            def _(dve):
                dve.wait_ge(rooted, 1)
                dve.scalar_tensor_tensor(q[:], slab[:, SLAB_Q:SLAB_Q + 2, :], gain, rstd[:], ALU.mult, ALU.mult).then_inc(normed, 1)

                def tops(h):
                    dve.wait_ge(scored, h + 1)
                    dve.tensor_reduce(top[:, h, :], ps[:, 2:4, :].rearrange("p b (t m) -> p (b t) m", t=2), AX.X, ALU.max)\
                        .then_inc(topped, 1)
                    dve.wait_ge(topped, h + 1)
                    dve.tensor_scalar(top[:, h, :], top[:, h, :], -scale, None, ALU.mult).then_inc(negated, 1)

                tops(0)
                for h in range(heads):
                    dve.wait_ge(exped, TT * (h + 1))
                    dve.reciprocal(inv[:, h, :], total[:, h, :]).then_inc(inverted, 1)
                    if h + 1 < heads:
                        tops(h + 1)
                    dve.wait_ge(mixed, h + 1)
                    rows = slice((h % 2) * HD, (h % 2 + 1) * HD)
                    dve.tensor_copy(mix[rows, PAIRS + h // 2, :], ps[rows, 6 + h % 2, :]).then_inc(kept, 1)

            @block.gpsimd
            def _(pool):
                for h in range(heads):
                    pool.wait_ge(inverted, h + 1)
                    pool.tensor_tensor(probs[:, h % 2], probs[:, h % 2], inv[:, h, :].unsqueeze(2).broadcast_to([P, TT, M]),
                                       ALU.mult).then_inc(scaled, 1)


def rwkv_block(k):
    with Phase(k, "first") as f:
        mix = f.sb("mix", [P, KT, T])
        with Phase(k, "rwkv") as g:
            slab, lw, rate = g.sb("slab", [P, 22, T]), g.sb("lw", [P, PAIRS, T]), g.sb("rate", [P, PAIRS, T])
            passes = g.sb("passes", [P, PAIRS, NCH - 1])
            rwkv_in(k, slab)
            decay_and_rate(k, slab, lw, rate)
            scan_chunks(k, slab, lw, rate, passes, mix)
            scan_states(k, slab, lw, rate, passes)
            rwkv_out(k, slab, mix)
            memory_attention(k, slab, mix)
        add_projection(k, "w_out", mix, (KT,), split=True)
    squared_relu_ffn(k)



FOX_H, NSA_H, GROUPS = 8, 8, 2
NCMP = T // 16 - 1
FORGET_W = P
ATTN_WIDTHS = [PW] * 11 + [FORGET_W, 24]


class Attention:

    def __init__(self, f):
        self.fq, self.fk = f.sb("fq", [P, 4, T]), f.sb("fk", [P, 4, T])
        self.fv = f.sb("fv", [P, TT, FOX_H * HD])
        self.nq = f.sb("nq", [P, 4, T])
        self.cmp_in = f.sb("cmp_in", [P, 2, T])
        self.ks, self.kw = f.sb("ks", [P, GROUPS, T]), f.sb("kw", [P, GROUPS, T])
        self.vs, self.vw = f.sb("vs", [P, TT, P]), f.sb("vw", [P, TT, P])
        self.kc, self.vc = f.sb("kc", [P, GROUPS, 32]), f.sb("vc", [32, GROUPS, HD])
        self.u = f.sb("forget_in", [FOX_H, T])
        self.gates = f.sb("gates", [P, TT, 24])

    def add_tables(self, f):
        self.forget = f.sb("forget", [P, FOX_H, T])
        self.alibi = f.sb("alibi", [P, NSA_H, T])
        self.cmp_dist = f.sb("cmp_dist", [P, TT, 32])
        self.future = f.sb("future", [P, P])


def attn_project(k, a, gain):
    nc, ps, ins, g0 = k.nc, k.ps, k.ins, k.first_panel["attn_in"]
    n_pairs, n_all = 11, 24
    with Phase(k, "attn_in") as f:
        b_f, ks_raw, kw_raw = f.sb("b_f", [FOX_H, 1]), f.sb("ks_raw", [P, T]), f.sb("kw_raw", [P, T])
        landed, first, copied, doubled = f.sem("landed"), f.sem("first"), f.sem("copied"), f.sem("doubled")
        x = Operand(k, f, k.xT, gain)
        features = {0: (a.fq, 0, -0.125), 1: (a.fq, 2, -0.125), 2: (a.fk, 0, 1.0), 3: (a.fk, 2, 1.0),
                    6: (a.nq, 0, -0.125), 7: (a.nq, 2, -0.125), 8: (a.cmp_in, 0, 1.0)}
        with nc.Block() as block:

            @block.sync
            def _(sp):
                with nc.allow_non_contiguous_dma(reason="eight numbers"):
                    sp.dma_start(b_f[:], ins["fox_b_f_2"].rearrange("l h -> h l")).then_inc(landed, 16)
                k.load_panels(sp, k.lookahead("attn_in"))
                sp.wait_ge(copied, 21)
                for g in range(GROUPS):
                    for half in range(2):
                        for src, dst in ((ks_raw, a.ks), (kw_raw, a.kw)):
                            sp.dma_start(dst[half * HD:(half + 1) * HD, g, :], src[g * HD:(g + 1) * HD, :]).then_inc(doubled, 16)
                sp.wait_ge(doubled, 16 * 4 * GROUPS)

            @block.tensor
            def _(pe):
                def start(b, n):
                    w = k.panel(pe, g0, n // 4, n % 4, KT, ATTN_WIDTHS[n])
                    if b >= 8:
                        pe.wait_ge(copied, b - 7)
                    return w

                def columns(b, n, m):
                    w_hi, w_lo = start(b, n)
                    at = slice(m * P, (m + 1) * P)
                    for kt in range(KT):
                        if b == 0:
                            x.ready(pe, kt)
                        last = product(pe, ps[:, b % 8, :], (w_hi[:, kt, at], w_lo[:, kt, at]), x.halves(kt), kt == 0, kt == KT - 1)
                    return last

                def tokens(b, n, c0, cols, tiles):
                    w_hi, w_lo = start(b, n)
                    for i, t in enumerate(tiles):
                        for kt in range(KT):
                            last = product(pe, ps[:, b % 8, i * cols:(i + 1) * cols], x.halves(kt, slice(t * P, (t + 1) * P)),
                                           (w_hi[:, kt, c0:c0 + cols], w_lo[:, kt, c0:c0 + cols]), kt == 0, kt == KT - 1)
                    return last

                for n in range(n_pairs):
                    for m in range(2):
                        b = 2 * n + m
                        if n in features or (n > 8 and m == 0):
                            last = columns(b, n, m)
                        elif n in (4, 5):
                            last = tokens(b, n, 0, PW, (2 * m, 2 * m + 1))
                        else:
                            last = tokens(b, n, P, P, range(TT))
                        last.then_inc(k.panel_used if m else first, 1)
                columns(22, 11, 0).then_inc(k.panel_used, 1)
                tokens(23, 12, 0, 24, range(TT)).then_inc(k.panel_used, 1)

            @block.vector
            def _(dve):
                x.lows(dve)
                for n in range(len(ATTN_WIDTHS)):
                    k.split_low(dve, g0, 0, n + 2)

            @block.scalar
            def _(act):
                x.highs(act)
                for b in range(n_all):
                    n, m, bank = b // 2, b % 2, ps[:, b % 8, :]
                    if b >= 2 * n_pairs:
                        act.wait_ge(k.panel_used, g0 + n_pairs + b - 2 * n_pairs + 1)
                    elif m:
                        act.wait_ge(k.panel_used, g0 + n + 1)
                    else:
                        act.wait_ge(first, n + 1)
                    if b >= 2 * n_pairs or m:
                        k.split_high(act, g0, 0, (n_pairs + b - 2 * n_pairs if b >= 2 * n_pairs else n) + 2)
                    if b == 22:
                        act.wait_ge(landed, 16)
                        made = act.activation(a.u[:], bank[0:FOX_H], ACT.Identity, bias=b_f[:])
                    elif b == 23:
                        made = act.activation(a.gates[:], bank[:, 0:TT * 24].rearrange("p (t c) -> p t c", t=TT), ACT.Sigmoid)
                    elif n in features:
                        tile, at, scale = features[n]
                        made = act.mul(tile[:, at + m, :], bank, scale)
                    elif n in (4, 5):
                        made = act.copy(a.fv[:, 2 * m:2 * m + 2, (n - 4) * PW:(n - 3) * PW],
                                        bank.rearrange("p (t c) -> p t c", t=2))
                    elif m == 0:
                        made = act.copy((ks_raw if n == 9 else kw_raw)[:], bank)
                    else:
                        made = act.copy((a.vs if n == 9 else a.vw)[:], bank.rearrange("p (t c) -> p t c", t=TT))
                    made.then_inc(copied, 1)


def attn_prepare(k, a, heads):
    nc, ps, ins = k.nc, k.ps, k.ins
    with Phase(k, "attn_pre") as f:
        w1, w2 = f.sb("w1", [P, 2, 32, HD]), f.sb("w2", [P, 2, HD])
        hidden = f.sb("hidden", [P, 2, 32])
        soft, neg = f.sb("soft", [FOX_H, T]), f.sb("neg", [FOX_H, T])
        room = heads[:].rearrange("p b t -> p (b t)")
        flat = room[:, 0:64 * NCMP].rearrange("p (v i n) -> p v i n", v=2, i=32)
        pick = room[0:FOX_H, 4 * T:6 * T].rearrange("h (g c) -> h g c", g=FOX_H)
        dist, steep = heads[:, 6, :], heads[0:FOX_H, 7, :]
        ones = k.ones[0:FOX_H, 0:1].broadcast_to([FOX_H, T])
        landed, filled, cut, opened, negated, softened, summed, spread, kept, blocked, mapped, bent, made, zeroed = (
            f.sem(s) for s in ("landed", "filled", "cut", "opened", "negated", "softened", "summed", "spread", "kept",
                               "blocked", "mapped", "bent", "made", "zeroed"))
        with nc.Block() as block:

            @block.sync
            def _(sp):
                for half in range(2):
                    rows = slice(half * HD, (half + 1) * HD)
                    for kv in range(2):
                        sp.dma_start(w1[rows, kv], ins["nsa_cmp_w1_2"][0, kv].rearrange("(i d) h -> d i h", d=HD)).then_inc(landed, 16)
                        sp.dma_start(w2[rows, kv, :], ins["nsa_cmp_w2_2"][0, kv]).then_inc(landed, 16)

            @block.gpsimd
            def _(pool):
                pool.memset(pick[:], 0.0).then_inc(filled, 1)
                pool.iota(dist[:], [[-1, T]], base=T - P, channel_multiplier=1, allow_small_or_imprecise_dtypes=True).then_inc(filled, 1)
                pool.iota(a.cmp_dist[:], [[P, TT], [-16, 32]], base=-31, channel_multiplier=1,
                          allow_small_or_imprecise_dtypes=True).then_inc(filled, 1)
                pool.memset(a.future[:], 0.0).then_inc(filled, 1)
                pool.wait_ge(filled, 4)
                pool.affine_select(out=pick[:], in_=pick[:], pattern=[[-1, FOX_H], [0, P]], compare_op=ALU.not_equal, fill=-1.0,
                                   base=0, channel_multiplier=1).then_inc(cut, 1)
                pool.affine_select(out=dist[:], in_=dist[:], pattern=[[-1, T]], compare_op=ALU.is_ge, fill=BIG, base=T - P,
                                   channel_multiplier=1).then_inc(cut, 1)
                pool.affine_select(out=a.cmp_dist[:], in_=a.cmp_dist[:], pattern=[[P, TT], [-16, 32]], compare_op=ALU.is_ge,
                                   fill=BIG, base=-31, channel_multiplier=1).then_inc(cut, 1)
                pool.affine_select(out=a.future[:], in_=a.future[:], pattern=[[-1, P]], compare_op=ALU.is_ge, fill=BIG, base=0,
                                   channel_multiplier=1).then_inc(cut, 1)

            @block.scalar
            def _(act):
                act.activation(soft[:], a.u[:], ACT.Abs).then_inc(opened, 1)
                act.wait_ge(opened, 1)
                act.activation(soft[:], soft[:], ACT.Exp, scale=-1.0).then_inc(opened, 1)
                act.wait_ge(opened, 2)
                act.activation(soft[:], soft[:], ACT.Ln, bias=k.eps[0:FOX_H, 3:4]).then_inc(opened, 1)
                for h in range(FOX_H):
                    act.wait_ge(spread, h + 1)
                    act.copy(a.forget[:, h, :], ps[:, h % 4, :]).then_inc(kept, 1)
                act.wait_ge(mapped, 1)
                act.wait_ge(zeroed, 1)
                act.activation(hidden[:, :, 0:NCMP], ps[:, 4, :].rearrange("p (v n) -> p v n", v=2)[:, :, 0:NCMP],
                               ACT.Gelu_apprx_tanh).then_inc(bent, 1)
                act.wait_ge(made, 1)
                act.copy(a.kc[:], ps[:, 5:8:2, 0:32])
                act.copy(a.vc[:], ps[0:32, 5:8:2, HD:2 * HD])

            @block.vector
            def _(dve):
                dve.memset(hidden[:], 0.0).then_inc(zeroed, 1)
                dve.tensor_scalar(neg[:], a.u[:], -1.0, 0.0, ALU.mult, ALU.max).then_inc(negated, 1)
                dve.wait_ge(opened, 3)
                dve.wait_ge(negated, 1)
                dve.tensor_tensor(neg[:], neg[:], soft[:], ALU.add).then_inc(softened, 1)
                dve.wait_ge(softened, 1)
                dve.tensor_tensor_scan(steep[:], ones, neg[:], 0.0, ALU.mult, ALU.add).then_inc(summed, 1)
                for kv in range(2):
                    by_16 = a.cmp_in[:, kv, :].rearrange("p (n i) -> p i n", i=16)
                    for half in range(2):
                        at = slice(16 * half, 16 * half + 16)
                        dve.tensor_tensor(flat[:, kv, at, :], by_16[:, :, half:half + NCMP],
                                          k.pe_T[:, kv, at].unsqueeze(2).broadcast_to([P, 16, NCMP]), ALU.add).then_inc(blocked, 1)
                dve.wait_ge(cut, 2)
                for h in range(NSA_H):
                    dve.tensor_scalar(a.alibi[:, h, :], dist[:], 2.0 ** -(h + 1), None, ALU.mult)

            @block.tensor
            def _(pe):
                pe.wait_ge(summed, 1)
                pe.wait_ge(cut, 1)
                for h in range(FOX_H):
                    if h >= 4:
                        pe.wait_ge(kept, h - 3)
                    pe.matmul(ps[:, h % 4, :], pick[:, h, :], steep[:], start=True, stop=True).then_inc(spread, 1)
                pe.wait_ge(blocked, 4)
                pe.wait_ge(landed, 16 * 8)
                for kv in range(2):
                    for g in range(GROUPS):
                        rows = slice(g * HD, (g + 1) * HD)
                        for i in range(32):
                            last = pe.matmul(ps[rows, 4, kv * 256:kv * 256 + NCMP], w1[rows, kv, i, :], flat[rows, kv, i, :],
                                             start=i == 0, stop=i == 31)
                last.then_inc(mapped, 1)
                pe.wait_ge(bent, 1)
                for g in range(GROUPS):
                    rows, bank = slice(g * HD, (g + 1) * HD), 5 + 2 * g
                    for half in range(2):
                        pe.matmul(ps[half * HD:(half + 1) * HD, bank, 0:32], w2[rows, 0, :], hidden[rows, 0, :], start=True, stop=True)
                    last = pe.matmul(ps[0:32, bank, HD:2 * HD], hidden[rows, 1, :], w2[rows, 1, :], start=True, stop=True)
                last.then_inc(made, 1)


def attention(k, a, heads):
    nc, ps = k.nc, k.ps
    units = [("fox", h) for h in range(FOX_H)]
    for h in range(NSA_H):
        units += [("slc", h), ("win", h), ("cmp", h)]
    n_units = len(units)
    s_at = {3: (0, 0), 2: (1, 0), 0: (1, 384), 1: (2, 0)}
    z_at = {3: 0, 2: 512, 0: 896, 1: 1024}
    t_at = {0: (3, 0), 1: (4, 0), 3: (4, 384), 2: (5, 0)}
    w_at = {0: 0, 1: 512, 3: 896, 2: 1024}
    with Phase(k, "attn") as f:
        z, w_T = f.sb("z", [P, 2, 1280]), f.sb("w_T", [P, 2, 1280])
        top, total, weight = (f.sb(s, [P, 2, TT]) for s in ("top", "total", "weight"))
        scored, lowered, exped, weighted, scaled, turned, copied_a, copied_v, mixed, kept, floored, inverted, clamped = (
            f.sem(s) for s in ("scored", "lowered", "exped", "weighted", "scaled", "turned", "copied_a", "copied_v", "mixed",
                               "kept", "floored", "inverted", "clamped"))

        def rows_of_head(h):
            return slice((h % 2) * HD, (h % 2 + 1) * HD)

        def head_no(u):
            kind, h = units[u]
            return h if kind == "fox" else FOX_H + h

        def last_of_head(u):
            return u + 1 == n_units or head_no(u + 1) != head_no(u)

        cmp_units = [sum(x[0] == "cmp" for x in units[:u + 1]) for u in range(n_units)]

        with nc.Block() as block:

            @block.tensor
            def _(pe):
                def scores(u):
                    kind, h = units[u]
                    rows = rows_of_head(h)
                    if u:
                        pe.wait_ge(lowered, u)
                    q, keys = {"fox": (a.fq, a.fk[rows, h // 2, :]), "slc": (a.nq, a.ks[rows, h // 4, :]),
                               "win": (a.nq, a.kw[rows, h // 4, :]), "cmp": (a.nq, a.kc[rows, h // 4, :])}[kind]
                    for t in range(TT):
                        q_t = q[rows, h // 2, t * P:(t + 1) * P]
                        if kind == "cmp":
                            last = pe.matmul(ps[:, 0, t * 32:(t + 1) * 32], q_t, keys, start=True, stop=True)
                            continue
                        bank, c = s_at[t]
                        n = (t + 1) * P
                        last = pe.matmul(ps[:, bank, c:c + n], q_t, keys[:, 0:n], start=True, stop=kind != "fox")
                        if kind == "fox":
                            last = pe.matmul(ps[:, bank, c + n - P:c + n], k.ident[:], a.future[:], start=False, stop=True)
                    last.then_inc(scored, 1)

                def turn(u):
                    pe.wait_ge(scaled, u + 1)
                    if u:
                        pe.wait_ge(copied_a, u - cmp_units[u - 1])
                        pe.wait_ge(copied_v, u)
                    if units[u][0] == "cmp":
                        for t in range(TT):
                            last = pe.transpose(ps[0:32, 3, t * P:(t + 1) * P], z[:, u % 2, t * 32:(t + 1) * 32], k.ident[:])
                    else:
                        for j in range(TT):
                            bank, c = t_at[j]
                            for t in range(j, TT):
                                at = z_at[t] + j * P
                                last = pe.transpose(ps[:, bank, c + (t - j) * P:c + (t - j + 1) * P], z[:, u % 2, at:at + P], k.ident[:])
                    last.then_inc(turned, 1)

                def mix(u):
                    kind, h = units[u]
                    pe.wait_ge(copied_a, u + 1 - cmp_units[u])
                    pe.wait_ge(copied_v, u + 1)
                    n, rows = head_no(u), rows_of_head(h)
                    first, final = u == 0 or head_no(u - 1) != n, last_of_head(u)
                    if first and n >= 2:
                        pe.wait_ge(kept, n - 1)
                    out, vcol = ps[rows, 6 + n % 2, :], slice((h // 4) * HD, (h // 4 + 1) * HD)
                    if kind == "cmp":
                        last = pe.matmul(out, a.vc[:, h // 4, :], w_T[0:32, u % 2, 0:T], start=first, stop=final)
                    else:
                        for j in range(TT):
                            v = a.fv[:, j, h * HD:(h + 1) * HD] if kind == "fox" else (a.vs if kind == "slc" else a.vw)[:, j, vcol]
                            last = pe.matmul(out[:, j * P:T], v, w_T[:, u % 2, w_at[j]:w_at[j] + T - j * P], start=first and j == 0,
                                             stop=final and j == TT - 1)
                    last.then_inc(mixed, 1)

                scores(0)
                for u in range(n_units):
                    if u + 1 < n_units:
                        scores(u + 1)
                    turn(u)
                    if u:
                        mix(u - 1)
                mix(n_units - 1)

            @block.vector
            def _(dve):
                def lower(u):
                    kind, h = units[u]
                    dve.wait_ge(scored, u + 1)
                    if u >= 2:
                        dve.wait_ge(turned, u - 1)
                    if kind == "cmp":
                        zc = z[:, u % 2, 0:TT * 32].rearrange("p (t n) -> p t n", t=TT)
                        dve.scalar_tensor_tensor(zc, a.cmp_dist[:], 2.0 ** -(h + 1), ps[:, 0, 0:TT * 32].rearrange("p (t n) -> p t n", t=TT),
                                                 ALU.mult, ALU.add).then_inc(floored, 1)
                        dve.wait_ge(floored, 2 * cmp_units[u] - 1)
                        dve.tensor_reduce(top[:, u % 2, :], zc, AX.X, ALU.min).then_inc(floored, 1)
                        dve.wait_ge(floored, 2 * cmp_units[u])
                        dve.tensor_scalar(top[:, u % 2, :], top[:, u % 2, :], 1e26, None, ALU.min).then_inc(lowered, 1)
                        return
                    for t in range(TT):
                        bank, c = s_at[t]
                        n = (t + 1) * P
                        bias = a.forget[:, h, 0:n] if kind == "fox" else a.alibi[:, h, T - n:T]
                        last = dve.tensor_tensor_reduce(z[:, u % 2, z_at[t]:z_at[t] + n], ps[:, bank, c:c + n], bias, 1.0, 3e38,
                                                        ALU.add, ALU.min, top[:, u % 2, t:t + 1])
                    last.then_inc(lowered, 1)

                def weigh(u):
                    kind, h = units[u]
                    dve.wait_ge(exped, u + 1)
                    if u >= 2:
                        dve.wait_ge(scaled, u - 1)
                    if kind == "cmp":
                        dve.tensor_scalar(total[:, u % 2, :], total[:, u % 2, :], 1e-30, None, ALU.max).then_inc(clamped, 1)
                        dve.wait_ge(clamped, cmp_units[u])
                    if kind == "fox":
                        dve.reciprocal(weight[:, u % 2, :], total[:, u % 2, :]).then_inc(weighted, 1)
                        return
                    dve.reciprocal(weight[:, u % 2, :], total[:, u % 2, :]).then_inc(inverted, 1)
                    dve.wait_ge(inverted, u - FOX_H + 1)
                    gate = a.gates[:, :, 3 * h + ("cmp", "slc", "win").index(kind)]
                    dve.tensor_tensor(weight[:, u % 2, :], weight[:, u % 2, :], gate, ALU.mult).then_inc(weighted, 1)

                def copy(u):
                    dve.wait_ge(turned, u + 1)
                    if u >= 2:
                        dve.wait_ge(mixed, u - 1)
                    if units[u][0] == "cmp":
                        dve.tensor_copy(w_T[0:32, u % 2, 0:T], ps[0:32, 3, :]).then_inc(copied_v, 1)
                    else:
                        dve.tensor_copy(w_T[:, u % 2, 0:T], ps[:, 3, :]).then_inc(copied_v, 1)

                lower(0)
                for u in range(n_units):
                    weigh(u)
                    if u + 1 < n_units:
                        lower(u + 1)
                    copy(u)

            @block.scalar
            def _(act):
                def exps(u):
                    act.wait_ge(lowered, u + 1)
                    if u >= 2:
                        act.wait_ge(weighted, u - 1)
                    for t in range(TT):
                        at, n = (t * 32, 32) if units[u][0] == "cmp" else (z_at[t], (t + 1) * P)
                        last = act.activation(z[:, u % 2, at:at + n], z[:, u % 2, at:at + n], ACT.Exp, bias=top[:, u % 2, t:t + 1],
                                              scale=-1.0, accum_out=total[:, u % 2, t:t + 1])
                    last.then_inc(exped, 1)

                def copy(u):
                    if units[u][0] == "cmp":
                        return
                    act.wait_ge(turned, u + 1)
                    if u >= 2:
                        act.wait_ge(mixed, u - 1)
                    act.copy(w_T[:, u % 2, T:1280], ps[:, 4:6, :].rearrange("p b c -> p (b c)")[:, 0:768]).then_inc(copied_a, 1)

                def keep(u):
                    act.wait_ge(mixed, u + 1)
                    n, rows = head_no(u), rows_of_head(units[u][1])
                    act.copy(heads[rows, n // 2, :], ps[rows, 6 + n % 2, :]).then_inc(kept, 1)

                exps(0)
                for u in range(n_units):
                    if u + 1 < n_units:
                        exps(u + 1)
                    copy(u)
                    if u and last_of_head(u - 1):
                        keep(u - 1)
                keep(n_units - 1)

            @block.gpsimd
            def _(pool):
                for u in range(n_units):
                    pool.wait_ge(weighted, u + 1)
                    for t in range(TT):
                        at, n = (t * 32, 32) if units[u][0] == "cmp" else (z_at[t], (t + 1) * P)
                        last = pool.tensor_scalar(z[:, u % 2, at:at + n], z[:, u % 2, at:at + n], weight[:, u % 2, t:t + 1], None, ALU.mult)
                    last.then_inc(scaled, 1)



POOL_WINDOWS = (2, 4, 8, 16)


def pool_mixer(k, out, norm_gain):
    nc, ps, g0 = k.nc, k.ps, k.first_panel["pool"]
    gain, groups, banks = k.col_b[:, ROW_B["pool_scale_2"]:ROW_B["pool_scale_2"] + KT], len(POOL_WINDOWS), 6
    with Phase(k, "pool") as f:
        h, sums, pooled, diff = (f.sb(s, [P, KT, T]) for s in ("h", "sums", "pooled", "diff"))
        count, inv = f.sb("count", [P, 16]), f.sb("inv", [P, 16])
        one = k.ones[:, 0:1].broadcast_to([P, T])
        x, rows = Operand(k, f, pooled), Stats(k, f)
        counted, inverted, gained, normed, summed, apart, pooled_s, first, scaled = (f.sem(s) for s in (
            "counted", "inverted", "gained", "normed", "summed", "apart", "pooled", "first", "scaled"))
        with nc.Block() as block:

            @block.sync
            def _(sp):
                k.load_panels(sp, k.lookahead("pool"))

            @block.gpsimd
            def _(pool):
                pool.iota(count[:], [[1, 16]], base=1, channel_multiplier=0, allow_small_or_imprecise_dtypes=True).then_inc(counted, 1)
                for b in range(KT):
                    pool.wait_ge(gained, b + 1)
                    pool.tensor_tensor(h[:, b, :], h[:, b, :], k.rstd[:], ALU.mult).then_inc(normed, 1)

            @block.vector
            def _(dve):
                dve.wait_ge(counted, 1)
                dve.reciprocal(inv[:], count[:]).then_inc(inverted, 1)
                dve.wait_ge(inverted, 1)
                for b in range(KT):
                    w = POOL_WINDOWS[b // 2]
                    dve.wait_ge(normed, b + 1)
                    dve.tensor_tensor_scan(sums[:, b, :], one, h[:, b, :], 0.0, ALU.mult, ALU.add).then_inc(summed, 1)
                    dve.wait_ge(summed, b + 1)
                    dve.tensor_tensor(diff[:, b, w:T], sums[:, b, w:T], sums[:, b, 0:T - w], ALU.subtract)
                    dve.tensor_tensor(diff[:, b, 0:w], sums[:, b, 0:w], inv[:, 0:w], ALU.mult).then_inc(apart, 1)
                    dve.wait_ge(apart, b + 1)
                    dve.tensor_tensor(pooled[:, b, 0:w], diff[:, b, 0:w], h[:, b, 0:w], ALU.subtract)
                    dve.scalar_tensor_tensor(pooled[:, b, w:T], diff[:, b, w:T], 1.0 / w, h[:, b, w:T], ALU.mult, ALU.subtract)\
                        .then_inc(pooled_s, 1)
                    if b:
                        x.low_of(dve, b - 1)
                x.low_of(dve, KT - 1)
                for g in range(groups):
                    k.split_low(dve, g0, 0, g + 2)

            @block.tensor
            def _(pe):
                for g in range(groups):
                    w_hi, w_lo = k.panel(pe, g0, 0, g, 2, PW)
                    for m in range(2):
                        b, at = 2 * g + m, slice(m * P, (m + 1) * P)
                        if b >= banks:
                            pe.wait_ge(scaled, b - banks + 1)
                        for kt in range(2):
                            x.ready(pe, 2 * g + kt)
                            last = product(pe, ps[:, b % banks, :], (w_hi[:, kt, at], w_lo[:, kt, at]), x.halves(2 * g + kt), kt == 0, kt == 1)
                        last.then_inc(k.panel_used if m else first, 1)
                    for b in (2 * g - 2, 2 * g - 1) if g else ():
                        rows.count(pe, b)
                for b in (KT - 2, KT - 1):
                    rows.count(pe, b)

            @block.scalar
            def _(act):
                for b in range(KT):
                    act.mul(h[:, b, :], k.xT[:, b, :], norm_gain[:, b:b + 1]).then_inc(gained, 1)
                for b in range(KT):
                    act.wait_ge(pooled_s, b + 1)
                    x.high_of(act, b)
                for b in range(KT):
                    if b % 2:
                        act.wait_ge(k.panel_used, g0 + b // 2 + 1)
                        k.split_high(act, g0, 0, b // 2 + 2)
                    else:
                        act.wait_ge(first, b // 2 + 1)
                    act.mul(out[:, b, :], ps[:, b % banks, :], gain[:, b:b + 1]).then_inc(scaled, 1)
                    act.wait_ge(scaled, b + 1)
                    rows.square(act, b, out[:, b, :])
                rows.root(act)


def second_block(k):
    def gain(layer, n):
        at = ROW_B["norm_g_2"] + (4 * layer + n) * KT
        return k.col_b[:, at:at + KT]

    for layer in range(2):
        with Phase(k, f"mixer{layer}") as f:
            mixed = f.sb("mixed", [P, KT, T])
            if layer == 0:
                with Phase(k, "attn_all") as g:
                    a = Attention(g)
                    attn_project(k, a, gain(layer, 0))
                    a.add_tables(g)
                    attn_prepare(k, a, mixed)
                    attention(k, a, mixed)
                add_projection(k, "attn_out", mixed, (KT,), out=mixed, split=True)
            else:
                pool_mixer(k, mixed, gain(layer, 0))
            take_in(k, f"mixer{layer}_out", mixed, gain(layer, 1))
        with Phase(k, f"glu{layer}") as f:
            hidden = Hidden(f, HK)
            swiglu_in(k, layer, gain(layer, 2), hidden)
            mixed = f.sb("out", [P, KT, T])
            add_projection(k, f"down{layer}", hidden, DOWN_CHUNKS, out=mixed)
            take_in(k, f"glu{layer}_out", mixed, gain(layer, 3), stats=layer == 0)


def store(k):
    nc, ps = k.nc, k.ps
    with Phase(k, "store") as f:
        y = f.sb("y", [P, TT, D])
        turned, copied, stored = f.sem("turned"), f.sem("copied"), f.sem("stored")
        with nc.Block() as block:

            @block.tensor
            def _(pe):
                for t in range(TT):
                    for kt in range(KT):
                        last = pe.transpose(ps[:, 2 * t + kt // 4, (kt % 4) * P:(kt % 4 + 1) * P], k.xT[:, kt, t * P:(t + 1) * P], k.ident[:])
                    last.then_inc(turned, 1)

            @block.scalar
            def _(act):
                for t in range(TT):
                    act.wait_ge(turned, t + 1)
                    act.copy(y[:, t, 0:BANK], ps[:, 2 * t, :]).then_inc(copied, 1)

            @block.vector
            def _(dve):
                for t in range(TT):
                    dve.wait_ge(turned, t + 1)
                    dve.tensor_copy(y[:, t, BANK:D], ps[:, 2 * t + 1, :]).then_inc(stored, 1)

            @block.sync
            def _(sp):
                done = k.output_stored
                for t in range(TT):
                    sp.wait_ge(copied, t + 1)
                    sp.wait_ge(stored, t + 1)
                    sp.dma_start(k.out[0, t * P:(t + 1) * P, :], y[:, t, :]).then_inc(done, 16)
                sp.wait_ge(done, 16 * TT)


def build(nc, ins, out):
    with ExitStack() as ctx:
        k = Kernel(nc, ctx, ins, out)
        k.output_stored = ctx.enter_context(nc.semaphore("output_stored"))
        with Phase(k, "memory") as f:
            mem_T = f.sb("mem_T", [P, KT, M])
            setup(k, mem_T)
            row_stats(k, "mem_stats", mem_T, M)
            memory_kv(k, mem_T, k.col_a[:, ROW_A["mem_norm_g"]:ROW_A["mem_norm_g"] + KT])
        row_stats(k, "x_stats", k.xT)
        rwkv_block(k)
        second_block(k)
        store(k)


_UNUSED = ("df_in", "df_q_norm_g", "df_k_norm_g", "df_lq1", "df_lk1", "df_lq2", "df_lk2", "df_subln_g")


def kernel(**inputs):
    import numpy as np
    import concourse.bacc as bacc
    from concourse.bass_utils import run_bass_kernel_spmd

    nc = bacc.Bacc("TRN2", target_bir_lowering=False, num_devices=1)
    arrays, ins = {}, {}
    for name, value in inputs.items():
        if name in _UNUSED:
            continue
        arrays[f"in_{name}"] = np.ascontiguousarray(value)
        ins[name] = nc.dram_tensor(f"in_{name}", arrays[f"in_{name}"].shape, F32, kind="ExternalInput").ap()
    out = nc.dram_tensor("out_x", (1, T, D), F32, kind="ExternalOutput").ap()
    build(nc, ins, out)
    result = run_bass_kernel_spmd(nc, [arrays], core_ids=[0])
    return result.results[0]["out_x"]
```

```python
from contextlib import ExitStack

import concourse.bass as bass
from concourse import mybir

F32 = mybir.dt.float32
F32R = mybir.dt.float32r
ALU = mybir.AluOpType
ACT = mybir.ActivationFunctionType
AX = mybir.AxisListType

P = 128
T = 512
D = 1024
KT = D // P
TT = T // P
M = 256
HD = 64
MIX = 768
PAIRS = MIX // P
LOG_DECAY = 0.6065306597126334
CH = 64
NCH = T // CH
RING = 2
AHEAD = 2 * RING
PW = 256
HID = 2816
HK = HID // P
DOWN_CHUNKS = (6, 6, 5, 5)
BANK = 512
BIG = 1e30
RMS_EPS = 1e-6
GN_EPS = 64e-5
KK_SCALE = 2.0 ** 24
KK_BIAS = 12.0 * 0.6931471805599453

VEC_A = (("norm_mix_g", 8), ("norm_ffn_g", 8), ("mem_norm_g", 8), ("rw_mu", 20), ("rw_w0", 6), ("rw_a0", 6),
         ("rw_k_k", 6), ("rw_k_a", 6), ("rw_r_k", 6), ("rw_lnx_g", 6), ("rw_lnx_b", 6),
         ("mem_q_norm_g", 1), ("mem_k_norm_g", 1))
VEC_B = (("norm_g_2", 64), ("pool_scale_2", 8))


def rows_of(table):
    at, out = 0, {}
    for name, n in table:
        out[name] = at
        at += n
    return out, at


ROW_A, N_A = rows_of(VEC_A)
ROW_B, N_B = rows_of(VEC_B)

FQ, FK, FV, FF, NQ, KC, VC, KS, VS, KW, VW, NG = 0, 512, 1024, 1536, 1544, 2056, 2184, 2312, 2440, 2568, 2696, 2824


class Kernel:

    def __init__(self, nc, ctx, ins, out):
        self.nc, self.ins, self.out = nc, ins, out
        self.n_blocks = 0

        def sb(name, shape):
            return ctx.enter_context(nc.sbuf_tensor(name, shape, F32))

        self.ring = sb("weight_ring", [P, RING, KT * PW])
        self.xT = sb("residual_T", [P, KT, T])
        self.w_hi = ctx.enter_context(nc.sbuf_tensor("weight_high", [P, RING, KT * PW], F32R))
        self.w_lo = ctx.enter_context(nc.sbuf_tensor("weight_low", [P, RING, KT * PW], F32R))
        self.rstd = sb("rstd", [P, T])
        self.ident = sb("identity", [P, P])
        self.ones = sb("ones", [P, P])
        self.head_ones = sb("head_ones", [P, P])
        self.eps = sb("eps_columns", [P, 4])
        self.col_a = sb("columns_a", [P, N_A])
        self.col_b = sb("columns_b", [P, N_B])
        self.pe_T = sb("position_T", [P, 2, 32])
        self.ps = ctx.enter_context(nc.psum_tensor("psum", [P, 8, BANK], F32))
        self.panel_landed = [ctx.enter_context(nc.semaphore(f"panel_landed_{s}")) for s in range(RING)]
        self.panel_high, self.panel_low, self.panel_used = (
            ctx.enter_context(nc.semaphore(f"panel_{s}")) for s in ("high", "low", "used"))
        self.squared, self.counted, self.logged, self.rooted, self.scaled, self.high, self.low = (
            ctx.enter_context(nc.semaphore(f"rows_{s}"))
            for s in ("squared", "counted", "logged", "rooted", "scaled", "high", "low"))
        self.take_sems, self.projection_sems = ([ctx.enter_context(nc.semaphore(f"{phase}_{s}")) for s in names] for phase, names in (
            ("take_in", ("parted", "taken")), ("projection", ("made", "taken"))))
        self.takes, self.projections = 0, 0
        self.added = ctx.enter_context(nc.semaphore("rows_added"))
        self.squares_counted = self.squares_added = 0
        self.stats_made, self.blocks_scaled, self.blocks_split = 0, 0, 0
        self.plan_panels()
        self.loaded, self.two_part = 0, []
        self.second_landed = ctx.enter_context(nc.semaphore("panel_second_landed"))

    def add_first_block(self, f):
        self.eye64 = f.sb("eye64", [P, HD])
        self.level = f.sb("level_masks", [P, 6, P])
        self.level0_T = f.sb("level0_mask_T", [P, P])
        self.upto_T = f.sb("upto_mask_T", [P, P])
        self.before_T = f.sb("before_mask_T", [P, P])
        self.restart = f.sb("restart", [P, T])
        self.k_mem = f.sb("k_mem_T", [P, 2, M])
        self.v_mem = f.sb("v_mem", [P, 2, M])

    def plan_panels(self):
        ins, self.phases, self.first_panel = self.ins, [], {}

        def tall(w):
            return w.rearrange("(k p) m -> p k m", p=P)

        def columns(w, c0=0):
            view = tall(w)
            return lambda i: (view[:, :, bass.ds(c0 + PW * i, PW)], view.shape[1], PW)

        def listed(parts):
            return lambda i: parts[i]

        def chunked(w, chunks):
            view, parts, k0 = tall(w), [], 0
            for n in chunks:
                parts.append((k0, n))
                k0 += n
            return lambda i, j: (view[:, parts[j][0]:parts[j][0] + parts[j][1], bass.ds(PW * i, PW)], parts[j][1], PW)

        def halved(w, half):
            view = tall(w)
            return listed([(view[:, 16 * half + 8 * c:16 * half + 8 * c + 8, PW * i:PW * (i + 1)], KT, PW)
                           for i in range(4) for c in range(2)])

        def add(name, n, view, kind="columns"):
            self.first_panel[name] = sum(x[1] for x in self.phases)
            self.phases.append((name, n, view, kind))

        add("mem_kv", 2, columns(ins["w_mem_kv"]))
        add("rw_in", 11, columns(ins["rw_in"][0]))
        add("w_out", 4, columns(ins["w_out"][0]))
        for half in range(2):
            add(f"ff1{half}", 8, columns(ins["w_ff1"][0], 8 * PW * half))
            add(f"ff2{half}", 8, halved(ins["w_ff2"][0], half), "listed")
        w = tall(ins["attn_w_in_2"][0])
        cuts = [(FQ, 256), (FQ + 256, 256), (FK, 256), (FK + 256, 256), (FV, 256), (FV + 256, 256), (NQ, 256),
                (NQ + 256, 256), (KC, 256)]
        parts = [(w[:, :, c:c + n], KT, n) for c, n in cuts]
        twos = w[:, :, KS:KS + 4 * P].rearrange("p k (b w c) -> p k b w c", b=2, w=2)
        parts += [(twos[:, :, :, i, :], KT, PW) for i in range(2)]
        parts += [(w[:, :, c:c + P], KT, P) for c in (FF, NG + 24 - P)]
        add("attn_in", len(parts), listed(parts), "listed")
        add("attn_out", 4, columns(ins["attn_w_out_2"][0]))
        for layer in range(2):
            gate, up = tall(ins["ffn_w_gate_2"][layer]), tall(ins["ffn_w_up_2"][layer])

            def gate_up(i, j, gate=gate, up=up):
                return ((gate, up)[j % 2][:, :, bass.ds(2 * PW * i + PW * (j // 2), PW)], KT, PW)

            add(f"gate_up{layer}", 2 * HID // PW, gate_up, "chunks")
            add(f"down{layer}", 16, chunked(ins["ffn_w_down_2"][layer], DOWN_CHUNKS), "chunks")
            if layer == 0:
                pool = [(ins["pool_w_2"][0, g].rearrange("(k p) m -> p k m", p=P), 2, PW) for g in range(4)]
                add("pool", 4, listed(pool), "listed")
        self.n_panels = sum(x[1] for x in self.phases)

    def panel_columns(self, g):
        for name, n, view, kind in self.phases:
            at = g - self.first_panel[name]
            if 0 <= at < n:
                _, kt, width = view(at // 4, at % 4) if kind == "chunks" else view(at)
                return kt * width
        return 0

    def load_panels(self, sp, until):
        until = min(until, self.n_panels)
        start = 0
        for name, n, view, kind in self.phases:
            lo, hi = max(self.loaded, start), min(until, start + n)
            g0, start = start, start + n

            def load(i, j, g0=g0, view=view, kind=kind):
                slot, g = (g0 + j) % RING, g0 + j
                src, kt, width = view(i, j) if kind == "chunks" else view(4 * i + j)
                if not isinstance(i, int) or g + 4 * i >= RING:
                    sp.wait_ge(self.panel_low, 4 * i + (g - RING + 1))
                dst = self.ring[:, slot, 0:kt * width].rearrange("p (k m) -> p k m", k=kt)
                if len(src.shape) == 4:
                    self.two_part.append(g + 4 * i)
                    sp.dma_start(dst[:, :, P:PW], src[:, :, 1, :]).then_inc(self.second_landed, 16)
                    dst, src = dst[:, :, 0:P], src[:, :, 0, :]
                sp.dma_start(dst, src).then_inc(self.panel_landed[slot], 16)

            at = lo - g0
            while at < hi - g0:
                fours = (hi - g0 - at) // 4
                if at % 4 == 0 and fours >= 2 and kind != "listed" and g0 + at >= RING:
                    with sp.Fori(at // 4, at // 4 + fours) as i:
                        for j in range(4):
                            load(i, j)
                    at += 4 * fours
                else:
                    load(at // 4, at % 4)
                    at += 1
        self.loaded = max(self.loaded, until)

    def split_high(self, act, g0, i, j):
        g = g0 + j
        if isinstance(i, int) and g + 4 * i >= self.n_panels:
            return
        slot, n = g % RING, self.panel_columns(g + 4 * i if isinstance(i, int) else g)
        if not isinstance(i, int) or g + 4 * i >= RING:
            act.wait_ge(self.panel_used, 4 * i + (g - RING + 1))
        act.wait_ge(self.panel_landed[slot], 32 * i + 16 * (g // RING + 1))
        if isinstance(i, int) and g + 4 * i in self.two_part:
            act.wait_ge(self.second_landed, 16 * (self.two_part.index(g + 4 * i) + 1))
        act.copy(self.w_hi[:, slot, 0:n], self.ring[:, slot, 0:n]).then_inc(self.panel_high, 1)

    def split_low(self, dve, g0, i, j):
        g = g0 + j
        if isinstance(i, int) and g + 4 * i >= self.n_panels:
            return
        slot, n = g % RING, self.panel_columns(g + 4 * i if isinstance(i, int) else g)
        dve.wait_ge(self.panel_high, 4 * i + (g + 1))
        dve.tensor_tensor(self.w_lo[:, slot, 0:n], self.ring[:, slot, 0:n], self.w_hi[:, slot, 0:n],
                          ALU.subtract).then_inc(self.panel_low, 1)

    def panel(self, pe, g0, i, j, kt, width):
        slot = (g0 + j) % RING
        pe.wait_ge(self.panel_low, 4 * i + (g0 + j + 1))
        return [w[:, slot, 0:kt * width].rearrange("p (k m) -> p k m", k=kt) for w in (self.w_hi, self.w_lo)]

    def lookahead(self, name):
        n = next(x[1] for x in self.phases if x[0] == name)
        return self.first_panel[name] + n + AHEAD


def product(pe, out, w, x, start, stop):
    (w_hi, w_lo), (x_hi, x_lo) = w, x
    pe.matmul(out, w_hi, x_hi, start=start, stop=False)
    pe.matmul(out, w_hi, x_lo, start=False, stop=False)
    return pe.matmul(out, w_lo, x_hi, start=False, stop=stop)


class Phase:

    def __init__(self, k, name):
        self.k, self.name, self.ctx = k, name, ExitStack()

    def __enter__(self):
        self.ctx.__enter__()
        return self

    def __exit__(self, *a):
        return self.ctx.__exit__(*a)

    def sem(self, name):
        return self.ctx.enter_context(self.k.nc.semaphore(f"{self.name}_{name}"))

    def sb(self, name, shape, dtype=F32):
        return self.ctx.enter_context(self.k.nc.sbuf_tensor(f"{self.name}_{name}", shape, dtype))


def in_fours(eng, n, body):
    fours = (n - 2) // 4
    done = 0
    if fours >= 3:
        for j in range(4):
            body(0, j)
        with eng.Fori(1, fours) as i:
            for j in range(4):
                body(i, j)
        done = 4 * fours
    for at in range(done, n):
        body(at // 4, at % 4)



def setup(k, mem_T):
    nc, ps, ins = k.nc, k.ps, k.ins
    with Phase(k, "setup") as f:
        x_in, mem_in = f.sb("x", [P, TT, D]), f.sb("mem", [P, 2, D])
        vec_a, vec_b, pe_in = f.sb("vec_a", [N_A, P]), f.sb("vec_b", [N_B, P]), f.sb("pe", [32, 2, P])
        x_landed, vec_landed, mem_landed = f.sem("x_landed"), f.sem("vec_landed"), f.sem("mem_landed")
        filled, cut = f.sem("filled"), f.sem("cut")
        x_turned, x_copied, mem_turned, mem_copied = (f.sem(n) for n in ("x_turned", "x_copied", "mem_turned", "mem_copied"))
        vec_turned = f.sem("vec_turned")
        with nc.Block() as block:

            @block.sync
            def _(sp):
                for t in range(TT):
                    sp.dma_start(x_in[:, t, :], ins["x"][0, t * P:(t + 1) * P, :]).then_inc(x_landed, 16)
                for t in range(2):
                    sp.dma_start(mem_in[:, t, :], ins["mem"][0, t * P:(t + 1) * P, :]).then_inc(mem_landed, 16)
                k.load_panels(sp, AHEAD)

            @block.gpsimd
            def _(pool):
                for n, (tile, value) in enumerate(((k.ident, 0.0), (k.head_ones, 1.0), (k.eye64, 0.0), (k.level, 1.0),
                                                   (k.level0_T, 0.0), (k.upto_T, 1.0), (k.before_T, 1.0),
                                                   (k.restart, 1.0), (k.ones, 1.0))):
                    pool.memset(tile[:], value).then_inc(filled, 1)
                pool.wait_ge(filled, 9)

                def select(n, view, pattern, base, channel, op, fill):
                    if n:
                        pool.wait_ge(cut, n)
                    pool.affine_select(out=view, in_=view, pattern=pattern, compare_op=op, fill=fill, base=base,
                                       channel_multiplier=channel).then_inc(cut, 1)

                cuts = [(k.ident[:], [[-1, P]], 0, 1, ALU.not_equal, 1.0),
                        (k.eye64[:], [[-1, HD]], 0, 1, ALU.not_equal, 1.0),
                        (k.eye64[:], [[-1, HD]], -HD, 1, ALU.not_equal, 1.0)]
                halves = k.head_ones[:].rearrange("p (h c) -> p h c", h=2)
                cuts += [(halves, [[-HD, 2], [0, HD]], 0, 1, ALU.is_ge, 0.0),
                         (halves, [[HD, 2], [0, HD]], HD - 1, -1, ALU.is_ge, 0.0)]
                for lv in range(6):
                    s = 1 << lv
                    cells = k.level[:, lv, :].rearrange("p (b h s) -> p b h s", h=2, s=s)
                    cuts += [(cells, [[-2 * s, P // (2 * s)], [-P * 2, 2], [0, s]], -s, 1, ALU.is_ge, 0.0),
                             (cells, [[2 * s, P // (2 * s)], [0, 2], [0, s]], 2 * s - 1, -1, ALU.is_ge, 0.0)]
                cells = k.level0_T[:].rearrange("p (b h) -> p b h", h=2)
                cuts += [(cells[:, :, 1], [[-2, P // 2]], 0, 1, ALU.not_equal, 1.0)]
                for tile, strict in ((k.upto_T, 0), (k.before_T, 1)):
                    cells = tile[:].rearrange("p (c t) -> p c t", c=2)
                    cuts += [(cells, [[CH, 2], [1, CH]], -strict, -1, ALU.is_ge, 0.0),
                             (cells, [[-CH, 2], [0, CH]], 0, 1, ALU.is_ge, 0.0)]
                cells = k.restart[:].rearrange("p (c t) -> p c t", c=NCH)
                cuts += [(cells, [[0, NCH], [1, CH]], 0, 0, ALU.not_equal, 0.0)]
                for n, c in enumerate(cuts):
                    select(n, *c)

            @block.scalar
            def _(act):
                load_log_exp(act)
                for table, tile, row in ((VEC_A, vec_a, ROW_A), (VEC_B, vec_b, ROW_B)):
                    for name, n in table:
                        a = ins[name]
                        for half in range(2 if n == 1 else 1):
                            if n == 1:
                                flat, dst = a, tile[row[name]:row[name] + 1, half * HD:(half + 1) * HD]
                            else:
                                order = {1: "(r c) -> r c", 2: "l (r c) -> (l r) c", 3: "l n (r c) -> (l n r) c"}
                                if name == "rw_r_k":
                                    flat = a.rearrange("l (r h) c -> (l r) (h c)", h=2)
                                else:
                                    flat = a.rearrange(order[len(a.shape)], c=P)
                                dst = tile[row[name]:row[name] + n, :]
                            act.dma_start(dst, flat).then_inc(vec_landed, 16)
                for kv in range(2):
                    for half in range(2):
                        act.dma_start(pe_in[:, kv, half * HD:(half + 1) * HD],
                                      ins["nsa_cmp_pe_2"][0, kv]).then_inc(vec_landed, 16)
                for kt in range(KT):
                    act.wait_ge(x_turned, kt + 1)
                    act.copy(k.xT[:, kt, :], ps[:, kt % 4, :]).then_inc(x_copied, 1)
                for g in range(RING):
                    k.split_high(act, 0, 0, g)

            @block.vector
            def _(dve):
                for n, value in enumerate((RMS_EPS, GN_EPS, KK_BIAS, 1.0)):
                    dve.memset(k.eps[:, n:n + 1], value)
                for j in range(4):
                    dve.wait_ge(mem_turned, j + 1)
                    dve.tensor_copy(mem_T[:, 2 * j:2 * j + 2, :],
                                    ps[:, 4 + j % 2, :].rearrange("p (k m) -> p k m", k=2)).then_inc(mem_copied, 1)
                dve.wait_ge(vec_turned, 1)
                dve.tensor_copy(k.col_a[:], ps[:, 6, 0:N_A])
                dve.tensor_copy(k.col_b[:], ps[:, 6, P:P + N_B])
                dve.tensor_copy(k.pe_T[:], ps[:, 6, 2 * P:2 * P + 64].rearrange("p (v i) -> p v i", v=2))
                for g in range(RING):
                    k.split_low(dve, 0, 0, g)

            @block.tensor
            def _(pe):
                pe.wait_ge(cut, 1)
                pe.wait_ge(x_landed, 16 * TT)
                for kt in range(KT):
                    if kt >= 4:
                        pe.wait_ge(x_copied, kt - 3)
                    for t in range(TT):
                        last = pe.transpose(ps[:, kt % 4, t * P:(t + 1) * P], x_in[:, t, kt * P:(kt + 1) * P], k.ident[:])
                    last.then_inc(x_turned, 1)
                pe.wait_ge(mem_landed, 32)
                for j in range(4):
                    if j >= 2:
                        pe.wait_ge(mem_copied, j - 1)
                    for kt in (2 * j, 2 * j + 1):
                        for t in range(2):
                            c = (kt % 2) * M + t * P
                            last = pe.transpose(ps[:, 4 + j % 2, c:c + P], mem_in[:, t, kt * P:(kt + 1) * P], k.ident[:])
                    last.then_inc(mem_turned, 1)
                pe.wait_ge(vec_landed, 16 * (len(VEC_A) + len(VEC_B) + 2 + 4))
                pe.transpose(ps[:, 6, 0:N_A], vec_a[:], k.ident[0:N_A, 0:N_A])
                pe.transpose(ps[:, 6, P:P + N_B], vec_b[:], k.ident[0:N_B, 0:N_B])
                for kv in range(2):
                    last = pe.transpose(ps[:, 6, 2 * P + 32 * kv:2 * P + 32 * kv + 32], pe_in[:, kv, :], k.ident[0:32, 0:32])
                last.then_inc(vec_turned, 1)



def load_log_exp(act):
    act.preload_act_table_set("natural_log_exp_and_others")


class Stats:

    def __init__(self, k, f, n=T, adds=False):
        self.k, self.n, self.c, self.c_counted, self.c_added = k, n, k.stats_made, k.squares_counted, k.squares_added
        k.stats_made += 1
        self.parts = 3 if adds else KT
        k.squares_counted += self.parts
        self.adds = KT - self.parts
        k.squares_added += self.adds
        self.squares, self.logs = f.sb("squares", [P, 2, n]), f.sb("logs", [P, n])
        self.sum = f.sb("square_sum", [P, n]) if adds else None

    def part(self, b):
        return self.sum[:] if self.adds and b == 0 else self.squares[:, b % 2, :]

    def square(self, act, b, src):
        if self.adds and b >= 3:
            act.wait_ge(self.k.added, self.c_added + b - 2)
        elif not self.adds and b >= 2:
            act.wait_ge(self.k.counted, self.c_counted + b - 1)
        act.activation(self.part(b), src, ACT.Square).then_inc(self.k.squared, 1)

    def add(self, dve, b):
        if not 1 <= b <= self.adds:
            return
        dve.wait_ge(self.k.squared, KT * self.c + b + 1)
        if b >= 2:
            dve.wait_ge(self.k.added, self.c_added + b - 1)
        dve.tensor_tensor(self.sum[:], self.sum[:], self.part(b), ALU.add).then_inc(self.k.added, 1)

    def count(self, pe, b):
        if 0 < b <= self.adds:
            return
        if self.adds and b == 0:
            pe.wait_ge(self.k.added, self.c_added + self.adds)
        pe.wait_ge(self.k.squared, KT * self.c + b + 1)
        pe.matmul(self.k.ps[:, 7, 0:self.n], self.k.ones[:], self.part(b), start=b == 0, stop=b == KT - 1)\
            .then_inc(self.k.counted, 1)

    def root(self, act):
        k, n = self.k, self.n
        act.wait_ge(k.counted, self.c_counted + self.parts)
        act.activation(self.logs[:], k.ps[:, 7, 0:n], ACT.Ln, bias=k.eps[:, 0:1], scale=1.0 / D).then_inc(k.logged, 1)
        act.wait_ge(k.logged, self.c + 1)
        act.activation(k.rstd[:, 0:n], self.logs[:], ACT.Exp, scale=-0.5).then_inc(k.rooted, 1)


class Operand:

    def __init__(self, k, f, src, gain=None, n=T, normed=None):
        self.k, self.src, self.gain, self.n = k, src, gain, n
        self.blocks = src.shape[1]
        self.hi, self.lo = (f.sb(f"operand_{s}", [P, self.blocks, n], F32R) for s in ("high", "low"))
        self.c_split, self.c_scaled = k.blocks_split, k.blocks_scaled
        k.blocks_split += self.blocks
        if gain is not None:
            self.normed = f.sb("operand_normed", [P, 2, n]) if normed is None else normed
            k.blocks_scaled += self.blocks

    def block(self, b):
        return self.src[:, b, 0:self.n] if self.gain is None else self.normed[:, b % 2, :]

    def high_of(self, act, b):
        act.copy(self.hi[:, b, :], self.block(b)).then_inc(self.k.high, 1)

    def low_of(self, dve, b):
        dve.wait_ge(self.k.high, self.c_split + b + 1)
        dve.tensor_tensor(self.lo[:, b, :], self.block(b), self.hi[:, b, :], ALU.subtract).then_inc(self.k.low, 1)

    def highs(self, act):
        for b in range(self.blocks):
            if self.gain is not None:
                act.wait_ge(self.k.scaled, self.c_scaled + b + 1)
            self.high_of(act, b)

    def lows(self, dve):
        k = self.k

        def scale(b):
            if b >= 2:
                dve.wait_ge(k.low, self.c_split + b - 1)
            dve.scalar_tensor_tensor(self.normed[:, b % 2, :], self.src[:, b, 0:self.n], self.gain[:, b:b + 1],
                                     k.rstd[:, 0:self.n], ALU.mult, ALU.mult).then_inc(k.scaled, 1)

        if self.gain is not None:
            scale(0)
        for b in range(self.blocks):
            if self.gain is not None and b + 1 < self.blocks:
                scale(b + 1)
            self.low_of(dve, b)

    def ready(self, pe, b):
        pe.wait_ge(self.k.low, self.c_split + b + 1)

    def halves(self, b, at=slice(None)):
        return self.hi[:, b, at], self.lo[:, b, at]


def row_stats(k, name, src, n=T):
    with Phase(k, name) as f:
        stats = Stats(k, f, n)
        with k.nc.Block() as block:

            @block.scalar
            def _(act):
                for b in range(KT):
                    stats.square(act, b, src[:, b, 0:n])
                stats.root(act)

            @block.tensor
            def _(pe):
                for b in range(KT):
                    stats.count(pe, b)


def take_in(k, name, mixed, gain, stats=True):
    with Phase(k, name) as f:
        rows = Stats(k, f) if stats else None
        part = f.sb("part", [P, 2, T])
        (parted, taken), c = k.take_sems, KT * k.takes
        k.takes += 1
        with k.nc.Block() as block:

            @block.vector
            def _(dve):
                def scale(b):
                    if b >= 2:
                        dve.wait_ge(taken, c + b - 1)
                    dve.scalar_tensor_tensor(part[:, b % 2, :], mixed[:, b, :], gain[:, b:b + 1], k.rstd[:], ALU.mult,
                                             ALU.mult).then_inc(parted, 1)

                scale(0)
                for b in range(KT):
                    if b + 1 < KT:
                        scale(b + 1)
                    dve.wait_ge(parted, c + b + 1)
                    dve.tensor_tensor(k.xT[:, b, :], k.xT[:, b, :], part[:, b % 2, :], ALU.add).then_inc(taken, 1)

            @block.scalar
            def _(act):
                for b in range(KT if stats else 0):
                    act.wait_ge(taken, c + b + 1)
                    rows.square(act, b, k.xT[:, b, :])
                if stats:
                    rows.root(act)

            @block.tensor
            def _(pe):
                for b in range(KT if stats else 0):
                    rows.count(pe, b)



def memory_kv(k, mem_T, mem_gain):
    nc, ps, g0 = k.nc, k.ps, k.first_panel["mem_kv"]
    gain = k.col_a[:, ROW_A["mem_k_norm_g"]:ROW_A["mem_k_norm_g"] + 1]
    with Phase(k, "mem_kv") as f:
        squares, logs, rstd, raw = (f.sb(s, [P, 2, M]) for s in ("squares", "logs", "rstd", "raw"))
        copied, summed, logged, rooted = (f.sem(s) for s in ("copied", "summed", "logged", "rooted"))
        mem = Operand(k, f, mem_T, mem_gain, M)
        with nc.Block() as block:

            @block.sync
            def _(sp):
                k.load_panels(sp, k.lookahead("mem_kv"))

            @block.tensor
            def _(pe):
                w_hi, w_lo = k.panel(pe, g0, 0, 0, KT, PW)
                for m in range(2):
                    at = slice(m * P, (m + 1) * P)
                    for kt in range(KT):
                        if m == 0:
                            mem.ready(pe, kt)
                        last = product(pe, ps[:, m, 0:M], (w_hi[:, kt, at], w_lo[:, kt, at]), mem.halves(kt), kt == 0, kt == KT - 1)
                last.then_inc(k.panel_used, 1)
                w_hi, w_lo = k.panel(pe, g0, 0, 1, KT, PW)
                for t in range(2):
                    at = slice(t * P, (t + 1) * P)
                    for kt in range(KT):
                        last = product(pe, ps[:, 2 + t, 0:M], mem.halves(kt, at), (w_hi[:, kt, :], w_lo[:, kt, :]), kt == 0, kt == KT - 1)
                last.then_inc(k.panel_used, 1)
                pe.wait_ge(copied, 2)
                for m in range(2):
                    last = pe.matmul(ps[:, 4, m * M:(m + 1) * M], k.head_ones[:], squares[:, m, :], start=True, stop=True)
                last.then_inc(summed, 1)

            @block.scalar
            def _(act):
                mem.highs(act)
                act.wait_ge(k.panel_used, g0 + 1)
                act.copy(raw[:], ps[:, 0:2, 0:M]).then_inc(copied, 1)
                act.activation(squares[:], ps[:, 0:2, 0:M], ACT.Square).then_inc(copied, 1)
                k.split_high(act, g0, 0, 2)
                k.split_high(act, g0, 0, 3)
                act.wait_ge(k.panel_used, g0 + 2)
                act.copy(k.v_mem[:], ps[:, 2:4, 0:M])
                act.wait_ge(summed, 1)
                act.activation(logs[:], ps[:, 4, :].rearrange("p (m t) -> p m t", m=2), ACT.Ln, bias=k.eps[:, 0:1],
                               scale=1.0 / HD).then_inc(logged, 1)
                act.wait_ge(logged, 1)
                act.activation(rstd[:], logs[:], ACT.Exp, scale=-0.5).then_inc(rooted, 1)

            @block.vector
            def _(dve):
                mem.lows(dve)
                k.split_low(dve, g0, 0, 2)
                k.split_low(dve, g0, 0, 3)
                dve.wait_ge(rooted, 1)
                dve.scalar_tensor_tensor(k.k_mem[:], raw[:], gain, rstd[:], ALU.mult, ALU.mult)



def wait_block(eng, k, g0, made, i, b):
    if b % 2 == 0:
        eng.wait_ge(made, 4 * i + b // 2 + 1)
    else:
        eng.wait_ge(k.panel_used, 4 * i + (g0 + b // 2 + 1))


def stream_columns(pe, k, name, x, made, bank_free, need=lambda b: b + 1):
    g0, ps = k.first_panel[name], k.ps
    n = next(p[1] for p in k.phases if p[0] == name)

    def body(i, j):
        w_hi, w_lo = k.panel(pe, g0, i, j, KT, PW)
        for m in range(2):
            pe.wait_ge(bank_free, 8 * i + need(2 * j + m))
            at = slice(m * P, (m + 1) * P)
            for kt in range(KT):
                if isinstance(i, int) and i == j == m == 0:
                    x.ready(pe, kt)
                last = product(pe, ps[:, 2 * j + m, :], (w_hi[:, kt, at], w_lo[:, kt, at]), x.halves(kt), kt == 0, kt == KT - 1)
            last.then_inc(k.panel_used if m else made, 1)

    in_fours(pe, n, body)


def rwkv_in(k, slab, low, low_landed):
    nc, ps, ins, g0 = k.nc, k.ps, k.ins, k.first_panel["rw_in"]
    mu, n_mu, n_all = k.col_a[:, ROW_A["rw_mu"]:ROW_A["rw_mu"] + 20], 20, 22
    with Phase(k, "rw_in") as f:
        z, step = f.sb("z", [P, 2, T + 1]), f.sb("step", [P, 2, T])
        x = Operand(k, f, k.xT, k.col_a[:, ROW_A["norm_mix_g"]:ROW_A["norm_mix_g"] + KT])
        made, bank_free, zeroed, stepped, shifted = (f.sem(s) for s in ("made", "bank_free", "zeroed", "stepped", "shifted"))
        with nc.Block() as block:

            @block.sync
            def _(sp):
                k.load_panels(sp, k.lookahead("rw_in"))
                for half, name in enumerate(("rw_w2", "rw_a2")):
                    sp.dma_start(low[half * HD:(half + 1) * HD, half, :], ins[name][0]).then_inc(low_landed, 16)

            @block.tensor
            def _(pe):
                stream_columns(pe, k, "rw_in", x, made, bank_free)

            @block.scalar
            def _(act):
                act.sem_inc(bank_free, 8)
                x.highs(act)
                for b in range(n_all):
                    wait_block(act, k, g0, made, 0, b)
                    if b % 2:
                        k.split_high(act, g0, 0, b // 2 + 2)
                    if b >= n_mu:
                        act.copy(slab[:, b, :], ps[:, b % 8, :]).then_inc(bank_free, 1)
                        continue
                    if b == 0:
                        act.wait_ge(zeroed, 1)
                    if b >= 2:
                        act.wait_ge(shifted, b - 1)
                    act.copy(z[:, b % 2, 1:T + 1], ps[:, b % 8, :]).then_inc(bank_free, 1)

            @block.vector
            def _(dve):
                dve.memset(z[:, :, 0:1], 0.0).then_inc(zeroed, 1)
                for half in range(2):
                    dve.memset(low[(1 - half) * HD:(2 - half) * HD, half, :], 0.0)
                x.lows(dve)
                for b in range(n_all):
                    if b % 2:
                        k.split_low(dve, g0, 0, b // 2 + 2)
                    if b >= n_mu:
                        continue
                    dve.wait_ge(bank_free, 8 + b + 1)
                    if b >= 2:
                        dve.wait_ge(shifted, b - 1)
                    dve.tensor_tensor(step[:, b % 2, :], z[:, b % 2, 0:T], z[:, b % 2, 1:T + 1],
                                      ALU.subtract).then_inc(stepped, 1)
                    dve.wait_ge(stepped, b + 1)
                    dve.scalar_tensor_tensor(slab[:, b, :], step[:, b % 2, :], mu[:, b:b + 1], z[:, b % 2, 1:T + 1],
                                             ALU.mult, ALU.add).then_inc(shifted, 1)


def add_projection(k, name, x, kts, out=None, stats=True, split=False):
    nc, ps, g0 = k.nc, k.ps, k.first_panel[name]
    chunks, blocks = [], 0
    for n in kts:
        chunks.append((blocks, n))
        blocks += n
    res, pairs, n_chunks = (k.xT if out is None else out), KT // 2, len(kts)
    with Phase(k, name) as f:
        (made, taken), c_made, c_taken = k.projection_sems, pairs * k.projections, KT * k.projections
        k.projections += 1
        x = Operand(k, f, x) if split else x
        rows = Stats(k, f, adds=True) if stats else None
        with nc.Block() as block:

            @block.sync
            def _(sp):
                k.load_panels(sp, k.lookahead(name))

            @block.tensor
            def _(pe):
                for i in range(pairs):
                    bank = 2 * (i % 3)
                    if i == 3:
                        pe.wait_ge(taken, c_taken + 2)
                    for c, (k0, n) in enumerate(chunks):
                        g = n_chunks * i + c
                        w_hi, w_lo = k.panel(pe, g0, g // 4, g % 4, n, PW)
                        for m in range(2):
                            at = slice(m * P, (m + 1) * P)
                            for kt in range(n):
                                if split and i == m == 0:
                                    x.ready(pe, k0 + kt)
                                last = product(pe, ps[:, bank + m, :], (w_hi[:, kt, at], w_lo[:, kt, at]), x.halves(k0 + kt),
                                               k0 + kt == 0, k0 + kt == blocks - 1)
                            if m:
                                last.then_inc(k.panel_used, 1)
                            elif c == n_chunks - 1:
                                last.then_inc(made, 1)
                if stats:
                    for b in range(KT):
                        rows.count(pe, b)

            @block.scalar
            def _(act):
                if split:
                    x.highs(act)
                for i in range(pairs):
                    for c in range(n_chunks):
                        k.split_high(act, g0, 0, n_chunks * i + c + 2)
                    if stats:
                        for b in (2 * i, 2 * i + 1):
                            act.wait_ge(taken, c_taken + b + 1)
                            rows.square(act, b, res[:, b, :])
                if stats:
                    rows.root(act)

            @block.vector
            def _(dve):
                if split:
                    x.lows(dve)
                for i in range(pairs):
                    for c in range(n_chunks):
                        k.split_low(dve, g0, 0, n_chunks * i + c + 2)
                    for b in (2 * i, 2 * i + 1):
                        if b % 2 == 0:
                            dve.wait_ge(made, c_made + i + 1)
                        else:
                            dve.wait_ge(k.panel_used, g0 + n_chunks * (i + 1))
                        bank = ps[:, 2 * (i % 3) + b % 2, :]
                        if out is None:
                            dve.tensor_tensor(k.xT[:, b, :], bank, k.xT[:, b, :], ALU.add).then_inc(taken, 1)
                        else:
                            dve.tensor_copy(out[:, b, :], bank).then_inc(taken, 1)
                    if stats:
                        for b in (2 * i, 2 * i + 1):
                            rows.add(dve, b)


class Hidden:

    def __init__(self, f, blocks):
        self.hi, self.lo = (f.sb(f"hidden_{s}", [P, blocks, T], F32R) for s in ("high", "low"))

    def halves(self, b):
        return self.hi[:, b, :], self.lo[:, b, :]


def squared_relu_ffn(k):
    nc, ps, blocks = k.nc, k.ps, 16
    with Phase(k, "ffn") as f:
        hidden = Hidden(f, blocks)
        x = Operand(k, f, k.xT, k.col_a[:, ROW_A["norm_ffn_g"]:ROW_A["norm_ffn_g"] + KT])
        for half in range(2):
            squared_relu_in(k, half, x, hidden, blocks)
            add_projection(k, f"ff2{half}", hidden, (8, 8), stats=half == 1)


def squared_relu_in(k, half, x, hidden, blocks):
    nc, ps, name = k.nc, k.ps, f"ff1{half}"
    g0 = k.first_panel[name]
    with Phase(k, name) as f:
        relu = f.sb("relu", [P, 4, T])
        made, bank_free, squared, high, low = (f.sem(s) for s in ("made", "bank_free", "squared", "high", "low"))
        with nc.Block() as block:

            @block.sync
            def _(sp):
                k.load_panels(sp, k.lookahead(name))

            @block.tensor
            def _(pe):
                stream_columns(pe, k, name, x, made, bank_free)

            @block.scalar
            def _(act):
                act.sem_inc(bank_free, 8)
                if half == 0:
                    x.highs(act)

                def high_of(b):
                    act.wait_ge(squared, b + 1)
                    act.copy(hidden.hi[:, b, :], relu[:, b % 4, :]).then_inc(high, 1)

                for b in range(blocks):
                    wait_block(act, k, g0, made, 0, b)
                    if b % 2:
                        k.split_high(act, g0, 0, b // 2 + 2)
                    if b >= 4:
                        act.wait_ge(low, b - 3)
                    act.activation(relu[:, b % 4, :], ps[:, b % 8, :], ACT.Relu).then_inc(bank_free, 1)
                    if b:
                        high_of(b - 1)
                high_of(blocks - 1)

            @block.vector
            def _(dve):
                if half == 0:
                    x.lows(dve)

                def low_of(b):
                    dve.wait_ge(high, b + 1)
                    dve.tensor_tensor(hidden.lo[:, b, :], relu[:, b % 4, :], hidden.hi[:, b, :], ALU.subtract).then_inc(low, 1)

                for b in range(blocks):
                    if b % 2:
                        k.split_low(dve, g0, 0, b // 2 + 2)
                    dve.wait_ge(bank_free, 8 + b + 1)
                    dve.tensor_tensor(relu[:, b % 4, :], relu[:, b % 4, :], relu[:, b % 4, :], ALU.mult).then_inc(squared, 1)
                    if b:
                        low_of(b - 1)
                low_of(blocks - 1)


def swiglu_in(k, layer, gain, hidden):
    nc, ps, name = k.nc, k.ps, f"gate_up{layer}"
    n, g0 = 2 * HID // PW, k.first_panel[name]
    with Phase(k, name) as f:
        gate = f.sb("gate", [P, 4, T])
        x = Operand(k, f, k.xT, gain, normed=gate[:, 0:2, :])
        made, bank_free, gated, high, low = (f.sem(s) for s in ("made", "bank_free", "gated", "high", "low"))
        with nc.Block() as block:

            @block.sync
            def _(sp):
                k.load_panels(sp, k.lookahead(name))

            @block.tensor
            def _(pe):
                stream_columns(pe, k, name, x, made, bank_free, need=lambda b: 4 * (b // 4) + 2 + 2 * (b % 2))

            def hidden_block(half, i, j, m):
                at = 4 * i + (j - 1 + m)
                return half[:, at, :] if isinstance(i, int) else half[:, bass.ds(at, 1), :].rearrange("p a t -> p (a t)")

            @block.scalar
            def _(act):
                act.sem_inc(low, 4)
                x.highs(act)

                def body(i, j):
                    if j % 2 == 0:
                        for m in range(2):
                            wait_block(act, k, g0, made, i, 2 * j + m)
                            act.wait_ge(low, 4 * i + j + m + 1)
                            act.activation(gate[:, j + m, :], ps[:, 2 * j + m, :], ACT.Silu).then_inc(gated, 1)
                        k.split_high(act, g0, i, j + 2)
                    else:
                        k.split_high(act, g0, i, j + 2)
                        for m in range(2):
                            act.wait_ge(bank_free, 8 * i + 8 + 4 * (j // 2) + 2 * m + 2)
                            act.copy(hidden_block(hidden.hi, i, j, m), gate[:, j - 1 + m, :]).then_inc(high, 1)

                in_fours(act, n, body)
                load_log_exp(act)

            @block.vector
            def _(dve):
                dve.sem_inc(bank_free, 8)
                x.lows(dve)

                def body(i, j):
                    k.split_low(dve, g0, i, j + 2)
                    if j % 2 == 0:
                        return
                    for m in range(2):
                        wait_block(dve, k, g0, made, i, 2 * j + m)
                        dve.wait_ge(gated, 4 * i + j - 1 + m + 1)
                        here = gate[:, j - 1 + m, :]
                        dve.tensor_tensor(here, here, ps[:, 2 * j + m, :], ALU.mult).then_inc(bank_free, 2)
                    for m in range(2):
                        dve.wait_ge(high, 4 * i + j - 1 + m + 1)
                        dve.tensor_tensor(hidden_block(hidden.lo, i, j, m), gate[:, j - 1 + m, :], hidden_block(hidden.hi, i, j, m),
                                          ALU.subtract).then_inc(low, 1)

                in_fours(dve, n, body)



class Steps:

    def __init__(self, f, name, steps):
        self.sem, self.n, self.at = f.sem(name), len(steps), {s: i for i, s in enumerate(steps)}
        self.next = 0

    def begin(self, eng):
        eng.sem_inc(self.sem, self.n)

    def did(self, name, ins):
        if self.at[name] != self.next % self.n:
            raise ValueError(f"step {name} out of order")
        self.next += 1
        ins.then_inc(self.sem, 1)

    def wait(self, eng, name, rnd, back=0):
        eng.wait_ge(self.sem, self.n * rnd + (self.n * (1 - back) + self.at[name] + 1))


SLAB_R, SLAB_K, SLAB_V, SLAB_WA, SLAB_G, SLAB_Q = 0, 6, 12, 18, 19, 20


def decay_and_rate(k, slab, lw, rate, low, low_landed):
    nc, ps, ins = k.nc, k.ps, k.ins
    with Phase(k, "lora") as f:
        squashed, made, done = f.sem("squashed"), f.sem("made"), f.sem("done")
        w0, a0 = (k.col_a[:, ROW_A[n]:ROW_A[n] + PAIRS] for n in ("rw_w0", "rw_a0"))
        with nc.Block() as block:

            @block.scalar
            def _(act):
                act.activation(slab[0:HD, SLAB_WA, :], slab[0:HD, SLAB_WA, :], ACT.Tanh).then_inc(squashed, 1)
                for p in range(PAIRS):
                    act.wait_ge(made, 2 * p + 1)
                    act.activation(lw[:, p, :], ps[:, 2 * (p % 4), :], ACT.Sigmoid, bias=w0[:, p:p + 1]).then_inc(done, 1)
                    act.wait_ge(made, 2 * p + 2)
                    act.activation(rate[:, p, :], ps[:, 2 * (p % 4) + 1, :], ACT.Sigmoid, bias=a0[:, p:p + 1]).then_inc(done, 1)
                act.activation(slab[:, SLAB_G, :], slab[:, SLAB_G, :], ACT.Sigmoid)
                load_log_exp(act)

            @block.tensor
            def _(pe):
                pe.wait_ge(low_landed, 32)
                pe.wait_ge(squashed, 1)
                for p in range(PAIRS):
                    for half in range(2):
                        if p >= 4:
                            pe.wait_ge(done, 2 * (p - 4) + half + 1)
                        pe.matmul(ps[:, 2 * (p % 4) + half, :], low[:, half, p * P:(p + 1) * P], slab[:, SLAB_WA, :],
                                  start=True, stop=True).then_inc(made, 1)


LEVELS = range(1, 6)
PREP_ACT = ["k_squared", "v_still", "kk_log", "kk_root", "e_pos", "e_neg", "e_prev", "pass"]
PREP_DVE = ["cum", "k_part", "k_new", "kk_clip", "kk", "rk", "ah", "bonus", "rh_kept"]
PREP_POOL = ["mid", "mid_prev", "ends", "passes", "b", "bh", "kh", "rh"]
PREP_PE = ["kk_sum", "rk_sum"]


def main_steps():
    both = range(2)
    act = [f"tok{q}" for q in range(TT)] + [f"ab{e}" for e in both]
    dve = [f"{n}{e}" for e in both for n in ("inv_T", "rb", "inv", "inv_T_eye")] + [f"{n}{e}" for e in both for n in ("ak", "rk")]
    pool = [f"{n}{e}" for e in both for n in ("below1_", "inv_eye")]
    pe = [f"turn{q}" for q in range(TT)] + [f"a1_{e}" for e in both] + [f"a2_{e}" for e in both]
    for lv in LEVELS:
        pe += [f"x{e}_{lv}" for e in both] + [f"tm{e}_{lv}" for e in both]
        act += [f"x{e}_{lv}" for e in both]
        dve += [f"{n}{e}_{lv}" for e in both for n in (("t", "m") if lv < 5 else ("m",))]
        pool += [f"below{lv + 1}_{e}" for e in both if lv < 5]
    pe += [f"{n}{e}" for n in ("av", "wu") for e in both] + ["out"]
    act += [f"{n}{e}" for n in ("a_side", "av", "wu") for e in both] + ["h", "y"]
    dve += ["g", "q"]
    return act, dve, pool, pe


def scan_chunks(k, slab, lw, rate, passes, mix):
    nc, ps = k.nc, k.ps
    cols = {n: k.col_a[:, ROW_A[n]:ROW_A[n] + PAIRS] for n in ("rw_k_k", "rw_k_a", "rw_r_k")}
    with Phase(k, "scan") as f:
        sq, rn, kk, kn, cum, mid, v_st, e_pos = (mix[:, i, :] for i in range(8))
        prev = slab[:, SLAB_WA, :]
        rk_sum, ah, kh = sq, kk, kn
        bh, rh = f.sb("bh", [P, T]), f.sb("rh", [P, T])
        tok = f.sb("tok", [P, TT, 4, P])
        ends = f.sb("ends", [P, NCH - 1])

        def two(name):
            return [f.sb(f"{name}{e}", [P, TT, P]) for e in range(2)]

        ab, below, inv, inv_T, x, ak_T, rb_T, rk_T = (two(s) for s in ("ab", "below", "inv", "inv_T", "x", "ak", "rb", "rkT"))
        a_av, w_u = below, x
        act_s, dve_s, pool_s, pe_s = (Steps(f, n, s) for n, s in zip(
            ("act_done", "vector_done", "pool_done", "tensor_done"), main_steps()))
        act_p, dve_p, pool_p, pe_p = (Steps(f, n, s) for n, s in zip(
            ("act_prepared", "vector_prepared", "pool_prepared", "tensor_prepared"),
            (PREP_ACT, PREP_DVE, PREP_POOL, PREP_PE)))

        def blk(t, i):
            return t[:, i, :] if isinstance(i, int) else t[:, bass.ds(i, 1), :].rearrange("p a t -> p (a t)")

        def col(t, i):
            return t[:, i:i + 1] if isinstance(i, int) else t[:, bass.ds(i, 1)]

        def per_chunk(t):
            return t.rearrange("p (c t) -> p c t", c=NCH)

        def tiles(t):
            return t.rearrange("p (q t) -> p q t", q=TT)

        def on_tiles(mask):
            return mask[:].unsqueeze(1).broadcast_to([P, TT, P])

        def pair_of(bank, which):
            return ps[:, bank:bank + 2, :].rearrange("p b (q w t) -> p (b q) w t", q=2, w=2)[:, :, which, :]

        def four(bank):
            return ps[:, bank, :].rearrange("p (q t) -> p q t", q=TT)

        def by_parity(t):
            return t.rearrange("p (q c k) -> p c q k", c=2, k=HD)

        def halves(bank):
            return ps[:, bank:bank + 2, 0:TT * HD].rearrange("p c (q k) -> p c q k", q=TT)

        mids = per_chunk(cum)[:, :, CH // 2 - 1:CH // 2]

        with nc.Block() as block:

            @block.scalar
            def _(act):
                act_s.begin(act)
                act_p.begin(act)

                def prep(p, slot):
                    if slot == 1:
                        pe_p.wait(act, "rk_sum", p, 1)
                        act_p.did("k_squared", act.activation(sq, blk(slab, SLAB_K + p), ACT.Square, scale=col(cols["rw_k_k"], p)))
                        pe_s.wait(act, "turn3", p, 1)
                        dve_p.wait(act, "bonus", p, 1)
                        act_p.did("v_still", act.copy(v_st[:], blk(slab, SLAB_V + p)))
                    if slot == 2:
                        dve_p.wait(act, "kk_clip", p)
                        act_p.did("kk_log", act.activation(rn, rn, ACT.Ln, scale=KK_SCALE))
                        act_p.wait(act, "kk_log", p)
                        act_p.did("kk_root", act.activation(rn, rn, ACT.Exp, scale=-0.5, bias=k.eps[:, 2:3]))
                    if slot == 3:
                        pool_p.wait(act, "mid", p)
                        dve_p.wait(act, "rh_kept", p, 1)
                        act_p.did("e_pos", act.activation(e_pos, mid, ACT.Exp, scale=-LOG_DECAY))
                        pool_p.wait(act, "mid_prev", p)
                        act_p.wait(act, "e_pos", p)
                        act_p.did("e_neg", act.activation(mid, mid, ACT.Exp, scale=LOG_DECAY))
                        act_p.did("e_prev", act.activation(prev, prev, ACT.Exp, scale=-LOG_DECAY))
                        pool_p.wait(act, "passes", p)
                        act_p.did("pass", act.activation(blk(passes, p), ends[:], ACT.Exp, scale=-LOG_DECAY))

                def main(p, prep_next):
                    for q in range(TT):
                        pe_s.wait(act, f"turn{q}", p)
                        if q == 0:
                            pe_s.wait(act, "out", p, 1)
                        act_s.did(f"tok{q}", act.copy(tok[:, q, :, :], four((6, 4, 5, 6)[q])))
                    for e in range(2):
                        pe_s.wait(act, f"a1_{e}", p)
                        pool_s.wait(act, f"below5_{e}", p, 1)
                        act_s.did(f"ab{e}", act.copy(ab[e][:], four(3 * e)))
                    for lv in LEVELS:
                        for e in range(2):
                            pe_s.wait(act, f"x{e}_{lv}", p)
                            act_s.did(f"x{e}_{lv}", act.copy(x[e][:], four(3 * e)))
                        if prep_next and lv < 5:
                            prep(p + 1, lv)
                    for e in range(2):
                        act_s.wait(act, "tok3", p)
                        act_s.did(f"a_side{e}", act.copy(a_av[e][:, :, 0:HD], tok[:, :, 0, e * HD:(e + 1) * HD]))
                    for e in range(2):
                        pe_s.wait(act, f"av{e}", p)
                        act_s.did(f"av{e}", act.copy(a_av[e][:, :, HD:P], ps[:, 3 * e, 0:TT * HD].rearrange("p (q v) -> p q v", q=TT)))
                    for e in range(2):
                        pe_s.wait(act, f"wu{e}", p)
                        act_s.did(f"wu{e}", act.copy(w_u[e][:], four(3 * e + 1)))
                    pe_s.wait(act, "out", p)
                    act_s.did("h", act.copy(by_parity(blk(rate, p)), halves(4)))
                    act_s.did("y", act.copy(blk(slab, SLAB_K + p), ps[:, 3, :]))

                for slot in range(1, 5):
                    prep(0, slot)
                with act.Fori(0, PAIRS - 1) as p:
                    main(p, True)
                main(PAIRS - 1, False)

            @block.vector
            def _(dve):
                dve_s.begin(dve)
                dve_p.begin(dve)

                def clip(p):
                    pe_p.wait(dve, "kk_sum", p)
                    dve_p.wait(dve, "kk", p, 1)
                    dve_p.did("kk_clip", dve.tensor_scalar(rn, ps[:, 7, :], 1e-24, None, ALU.max))

                def prep(p, slot):
                    if slot == 1:
                        pool_p.wait(dve, "passes", p, 1)
                        dve_p.did("cum", dve.tensor_tensor_scan(cum, k.restart[:], blk(lw, p), 0.0, ALU.mult, ALU.add))
                        pe_s.wait(dve, "a2_1", p, 1)
                        pool_p.wait(dve, "kh", p, 1)
                        dve_p.wait(dve, "rk", p, 1)
                        dve_p.did("k_part", dve.scalar_tensor_tensor(kn, blk(rate, p), 1.0, blk(slab, SLAB_K + p), ALU.subtract, ALU.mult))
                        dve_p.wait(dve, "k_part", p)
                        dve_p.did("k_new", dve.scalar_tensor_tensor(kn, kn, col(cols["rw_k_a"], p), blk(slab, SLAB_K + p), ALU.mult, ALU.add))
                    if slot == 3:
                        act_p.wait(dve, "kk_root", p)
                        pe_s.wait(dve, "a2_1", p, 1)
                        pool_p.wait(dve, "b", p, 1)
                        dve_p.wait(dve, "ah", p, 1)
                        dve_p.did("kk", dve.scalar_tensor_tensor(kk, blk(slab, SLAB_K + p), col(cols["rw_k_k"], p), rn, ALU.mult, ALU.mult))
                        pe_p.wait(dve, "rk_sum", p, 1)
                        dve_p.wait(dve, "k_new", p)
                        dve_p.did("rk", dve.scalar_tensor_tensor(rk_sum[:], blk(slab, SLAB_R + p), col(cols["rw_r_k"], p), kn, ALU.mult, ALU.mult))
                    if slot == 4:
                        act_p.wait(dve, "e_prev", p)
                        dve_p.wait(dve, "kk", p)
                        pool_p.wait(dve, "b", p)
                        dve_p.did("ah", dve.scalar_tensor_tensor(ah[:], kk, -1.0, prev, ALU.mult, ALU.mult))
                        pe_p.wait(dve, "rk_sum", p)
                        act_p.wait(dve, "v_still", p)
                        dve_p.did("bonus", dve.tensor_tensor(blk(slab, SLAB_V + p), ps[:, 7, :], v_st[:], ALU.mult))
                        pool_p.wait(dve, "rh", p)
                        dve_p.wait(dve, "rk", p)
                        dve_p.did("rh_kept", dve.tensor_tensor(blk(slab, SLAB_R + p), blk(slab, SLAB_R + p), e_pos, ALU.mult))

                def main(p, prep_next):
                    for e in range(2):
                        pe_s.wait(dve, f"a1_{e}", p)
                        dve_s.did(f"inv_T{e}", dve.tensor_tensor(inv_T[e][:], pair_of(3 * e + 1, 0), on_tiles(k.level0_T), ALU.mult))
                        pe_s.wait(dve, "out", p, 1)
                        dve_s.did(f"rb{e}", dve.tensor_tensor(rb_T[e][:], pair_of(3 * e + 1, 1), on_tiles(k.upto_T), ALU.mult))
                        act_s.wait(dve, f"ab{e}", p)
                        dve_s.did(f"inv{e}", dve.tensor_tensor(inv[e][:], ab[e][:], on_tiles(k.level[:, 0, :]), ALU.mult))
                        dve_s.wait(dve, f"inv_T{e}", p)
                        dve_s.did(f"inv_T_eye{e}", dve.tensor_tensor(inv_T[e][:], inv_T[e][:], on_tiles(k.ident), ALU.add))
                    for e in range(2):
                        pe_s.wait(dve, f"a2_{e}", p)
                        dve_s.did(f"ak{e}", dve.tensor_tensor(ak_T[e][:], pair_of(3 * e + 1, 0), on_tiles(k.before_T), ALU.mult))
                        dve_s.did(f"rk{e}", dve.tensor_tensor(rk_T[e][:], pair_of(3 * e + 1, 1), on_tiles(k.upto_T), ALU.mult))
                    for lv in LEVELS:
                        if prep_next and lv == 2:
                            clip(p + 1)
                        for e in range(2):
                            pe_s.wait(dve, f"tm{e}_{lv}", p)
                            if lv < 5:
                                dve_s.did(f"t{e}_{lv}", dve.tensor_tensor(inv[e][:], four(3 * e + 1), inv[e][:], ALU.add))
                            if lv > 1:
                                dve_s.wait(dve, f"m{e}_{lv - 1}", p)
                            dve_s.did(f"m{e}_{lv}", dve.tensor_tensor(inv_T[e][:], four(3 * e + 2), inv_T[e][:], ALU.add))
                        if prep_next and lv < 5:
                            prep(p + 1, lv)
                    pe_s.wait(dve, "out", p)
                    eye = k.eye64[:].unsqueeze(1).unsqueeze(1).broadcast_to([P, 2, TT, HD])
                    dve_s.did("g", dve.tensor_tensor(by_parity(blk(lw, p)), halves(0), eye, ALU.add))
                    dve_p.wait(dve, "rh_kept", p)
                    dve_s.did("q", dve.tensor_tensor(blk(slab, SLAB_R + p), ps[:, 2, :], blk(slab, SLAB_R + p), ALU.add))

                for slot in range(1, 5):
                    if slot == 2:
                        clip(0)
                    prep(0, slot)
                with dve.Fori(0, PAIRS - 1) as p:
                    main(p, True)
                main(PAIRS - 1, False)

            @block.gpsimd
            def _(pool):
                pool_s.begin(pool)
                pool_p.begin(pool)

                def prep(p, slot):
                    if slot == 2:
                        dve_p.wait(pool, "cum", p)
                        pool_p.wait(pool, "bh", p, 1)
                        pool_p.wait(pool, "kh", p, 1)
                        pool_p.did("mid", pool.tensor_tensor(per_chunk(mid), per_chunk(cum), mids.broadcast_to([P, NCH, CH]), ALU.subtract))
                        pool_p.wait(pool, "mid", p)
                        dve_p.wait(pool, "ah", p, 1)
                        pool_p.did("mid_prev", pool.tensor_tensor(prev, mid, blk(lw, p), ALU.subtract))
                        act_p.wait(pool, "pass", p, 1)
                        pool_p.did("ends", pool.tensor_tensor(ends[:].unsqueeze(2), per_chunk(cum)[:, 0:NCH - 1, CH - 1:CH], mids[:, 0:NCH - 1], ALU.subtract))
                        pool_p.wait(pool, "ends", p)
                        pool_p.did("passes", pool.tensor_tensor(ends[:].unsqueeze(2), ends[:].unsqueeze(2), mids[:, 1:NCH], ALU.add))
                    if slot == 3:
                        dve_p.wait(pool, "kk", p)
                        pe_s.wait(pool, "a2_1", p, 1)
                        pool_p.did("b", pool.tensor_tensor(bh[:], kk, blk(rate, p), ALU.mult))
                        act_p.wait(pool, "e_neg", p)
                        pool_p.wait(pool, "b", p)
                        pool_p.did("bh", pool.tensor_tensor(bh[:], bh[:], mid, ALU.mult))
                        dve_p.wait(pool, "rk", p)
                        pool_p.did("kh", pool.tensor_tensor(kh[:], kn, mid, ALU.mult))
                    if slot == 4:
                        act_p.wait(pool, "e_pos", p)
                        pool_p.did("rh", pool.tensor_tensor(rh[:], blk(slab, SLAB_R + p), e_pos, ALU.mult))

                def main(p, prep_next):
                    for e in range(2):
                        act_s.wait(pool, f"ab{e}", p)
                        pe_s.wait(pool, f"wu{e}", p, 1)
                        pool_s.did(f"below1_{e}", pool.tensor_tensor(below[e][:], ab[e][:], on_tiles(k.level[:, 1, :]), ALU.mult))
                        dve_s.wait(pool, f"inv{e}", p)
                        pool_s.did(f"inv_eye{e}", pool.tensor_tensor(inv[e][:], inv[e][:], on_tiles(k.ident), ALU.add))
                    for lv in range(1, 5):
                        for e in range(2):
                            pe_s.wait(pool, f"x{e}_{lv}", p)
                            pool_s.did(f"below{lv + 1}_{e}", pool.tensor_tensor(below[e][:], ab[e][:], on_tiles(k.level[:, lv + 1, :]), ALU.mult))
                        if prep_next:
                            prep(p + 1, lv)

                for slot in range(1, 5):
                    prep(0, slot)
                with pool.Fori(0, PAIRS - 1) as p:
                    main(p, True)
                main(PAIRS - 1, False)

            @block.tensor
            def _(pe):
                pe_s.begin(pe)
                pe_p.begin(pe)

                def mm(out, lhsT, rhs, start=True, stop=True):
                    return pe.matmul(out, lhsT, rhs, start=start, stop=stop)

                def prep(p, slot):
                    if slot == 1:
                        act_p.wait(pe, "k_squared", p)
                        dve_p.wait(pe, "bonus", p, 1)
                        pe_p.did("kk_sum", mm(ps[:, 7, :], k.head_ones[:], sq))
                    if slot == 4:
                        dve_p.wait(pe, "kk_clip", p)
                        dve_p.wait(pe, "rk", p)
                        pe_p.did("rk_sum", mm(ps[:, 7, :], k.head_ones[:], rk_sum[:]))

                def main(p, prep_next):
                    dve_p.wait(pe, "ah", p)
                    pool_p.wait(pe, "rh", p)
                    act_p.wait(pe, "v_still", p)
                    act_s.wait(pe, "tok3", p, 1)
                    for q in range(TT):
                        if q == 1:
                            act_s.wait(pe, "h", p, 1)
                            dve_s.wait(pe, "g", p, 1)
                        if q == 3:
                            act_s.wait(pe, "tok0", p)
                        for n, src in enumerate((ah, bh, kh, v_st)):
                            last = pe.transpose(ps[:, (6, 4, 5, 6)[q], n * P:(n + 1) * P], src[:, q * P:(q + 1) * P], k.ident[:])
                        pe_s.did(f"turn{q}", last)
                    act_s.wait(pe, "y", p, 1)
                    dve_s.wait(pe, "q", p, 1)
                    for e in range(2):
                        rows = slice(e * HD, (e + 1) * HD)
                        if e == 1:
                            act_s.wait(pe, "tok3", p)
                        for q in range(TT):
                            at = slice(q * P, (q + 1) * P)
                            mm(ps[:, 3 * e, at], ah[rows, at], bh[rows, at])
                        for q in range(TT):
                            at, bank, c = slice(q * P, (q + 1) * P), 3 * e + 1 + q // 2, (q % 2) * 2 * P
                            mm(ps[:, bank, c:c + P], bh[rows, at], ah[rows, at])
                            last = mm(ps[:, bank, c + P:c + 2 * P], bh[rows, at], rh[rows, at])
                        pe_s.did(f"a1_{e}", last)
                    for e in range(2):
                        rows = slice(e * HD, (e + 1) * HD)
                        dve_s.wait(pe, f"rb{e}", p)
                        for q in range(TT):
                            at, bank, c = slice(q * P, (q + 1) * P), 3 * e + 1 + q // 2, (q % 2) * 2 * P
                            mm(ps[:, bank, c:c + P], kh[rows, at], ah[rows, at])
                            last = mm(ps[:, bank, c + P:c + 2 * P], kh[rows, at], rh[rows, at])
                        pe_s.did(f"a2_{e}", last)
                    for lv in LEVELS:
                        for e in range(2):
                            pool_s.wait(pe, f"below{lv}_{e}", p)
                            if lv == 1:
                                dve_s.wait(pe, f"inv_T_eye{e}", p)
                            else:
                                act_s.wait(pe, f"x{e}_{lv - 1}", p)
                                dve_s.wait(pe, f"m{e}_{lv - 1}", p)
                            for q in range(TT):
                                last = mm(ps[:, 3 * e, q * P:(q + 1) * P], below[e][:, q, :], inv_T[e][:, q, :])
                            pe_s.did(f"x{e}_{lv}", last)
                        for e in range(2):
                            act_s.wait(pe, f"x{e}_{lv}", p)
                            if lv == 1:
                                pool_s.wait(pe, f"inv_eye{e}", p)
                                dve_s.wait(pe, f"rk{e}", p)
                            for q in range(TT):
                                at = slice(q * P, (q + 1) * P)
                                if lv < 5:
                                    mm(ps[:, 3 * e + 1, at], x[e][:, q, :], inv[e][:, q, :])
                                last = mm(ps[:, 3 * e + 2, at], inv[e][:, q, :], x[e][:, q, :])
                            pe_s.did(f"tm{e}_{lv}", last)
                        if prep_next and lv < 5:
                            prep(p + 1, lv)
                    for e in range(2):
                        for q in range(TT):
                            last = mm(ps[:, 3 * e, q * HD:(q + 1) * HD], ak_T[e][:, q, :], tok[:, q, 3, e * HD:(e + 1) * HD])
                        pe_s.did(f"av{e}", last)
                    for e in range(2):
                        act_s.wait(pe, f"av{e}", p)
                        dve_s.wait(pe, f"m{e}_5", p)
                        for q in range(TT):
                            last = mm(ps[:, 3 * e + 1, q * P:(q + 1) * P], inv_T[e][:, q, :], a_av[e][:, q, :])
                        pe_s.did(f"wu{e}", last)
                    for e in range(2):
                        act_s.wait(pe, f"wu{e}", p)
                        if e == 0:
                            act_s.wait(pe, "wu1", p)
                        rows, w, u = slice(e * HD, (e + 1) * HD), slice(0, HD), slice(HD, P)
                        for q in range(TT):
                            at = slice(q * P, (q + 1) * P)
                            mm(ps[rows, 2, at], w_u[e][:, q, w], rb_T[e][:, q, :])
                            mm(ps[rows, 3, at], w_u[e][:, q, u], rb_T[e][:, q, :], stop=False)
                            mm(ps[rows, 3, at], tok[:, q, 3, rows], rk_T[e][:, q, :], start=False)
                            for c in range(2):
                                cs, to = slice(c * CH, (c + 1) * CH), slice(q * HD, (q + 1) * HD)
                                mm(ps[rows, c, to], w_u[e][cs, q, w], tok[cs, q, 1, rows])
                                mm(ps[rows, 4 + c, to], tok[cs, q, 1, rows], w_u[e][cs, q, u], stop=False)
                                last = mm(ps[rows, 4 + c, to], tok[cs, q, 2, rows], tok[cs, q, 3, rows], start=False)
                    pe_s.did("out", last)

                for slot in range(1, 5):
                    prep(0, slot)
                with pe.Fori(0, PAIRS - 1) as p:
                    main(p, True)
                main(PAIRS - 1, False)


def scan_states(k, slab, lw, rate, passes):
    nc, ps = k.nc, k.ps
    with Phase(k, "states") as f:
        state = f.sb("state", [P, NCH - 1, PAIRS, HD])
        moved, grown, passed, read, added = (f.sem(s) for s in ("moved", "grown", "passed", "read", "added"))

        def chunk(t, n, pairs=slice(0, PAIRS)):
            return t[:, pairs, n * CH:(n + 1) * CH]

        with nc.Block() as block:

            @block.tensor
            def _(pe):
                def outputs(n):
                    for p in range(PAIRS):
                        for e in range(2):
                            rows = slice(e * HD, (e + 1) * HD)
                            last = pe.matmul(ps[rows, 2 + p, (n + 1) * CH:(n + 2) * CH], state[rows, n, p, :],
                                             slab[rows, SLAB_R + p, (n + 1) * CH:(n + 2) * CH], start=True, stop=True)
                    last.then_inc(read, 1)

                for n in range(NCH - 2):
                    pe.wait_ge(passed, n + 1)
                    if n >= 2:
                        pe.wait_ge(grown, n - 1)
                    for p in range(PAIRS):
                        for e in range(2):
                            rows = slice(e * HD, (e + 1) * HD)
                            last = pe.matmul(ps[rows, n % 2, p * HD:(p + 1) * HD], lw[rows, p, (n + 1) * CH:(n + 2) * CH],
                                             state[rows, n, p, :], start=True, stop=True)
                    last.then_inc(moved, 1)
                    outputs(n)
                pe.wait_ge(passed, NCH - 1)
                outputs(NCH - 2)

            @block.vector
            def _(dve):
                def by_pass(n):
                    return passes[:, :, n:n + 1].broadcast_to([P, PAIRS, HD])

                dve.tensor_tensor(state[:, 0], chunk(rate, 0), by_pass(0), ALU.mult).then_inc(passed, 1)
                for n in range(1, NCH - 1):
                    dve.wait_ge(moved, n)
                    dve.tensor_tensor(state[:, n], ps[:, (n - 1) % 2, 0:PAIRS * HD].rearrange("p (h v) -> p h v", h=PAIRS),
                                      chunk(rate, n), ALU.add).then_inc(grown, 1)
                    dve.wait_ge(grown, n)
                    dve.tensor_tensor(state[:, n], state[:, n], by_pass(n), ALU.mult).then_inc(passed, 1)
                dve.wait_ge(read, NCH - 1)
                for p in range(PAIRS):
                    y = slab[:, SLAB_K + p, CH:T]
                    dve.tensor_tensor(y, ps[:, 2 + p, CH:T], y, ALU.add)


def rwkv_out(k, slab, mix):
    nc, ps, ins = k.nc, k.ps, k.ins
    gain, shift = (k.col_a[:, ROW_A[n]:ROW_A[n] + PAIRS] for n in ("rw_lnx_g", "rw_lnx_b"))
    with Phase(k, "rwkv_out") as f:
        g2, mean_of = f.sb("g2", [P, MIX]), f.sb("mean_of", [P, P])
        logs, rstd, out = f.sb("logs", [P, 2, T]), f.sb("rstd", [P, 2, T]), mix
        landed, meant, averaged, centred, squared, spread, logged, rooted, scaled, shifted, gated = (f.sem(s) for s in (
            "landed", "meant", "averaged", "centred", "squared", "spread", "logged", "rooted", "scaled", "shifted", "gated"))
        with nc.Block() as block:

            @block.sync
            def _(sp):
                sp.dma_start(g2[:], ins["rw_g2"][0]).then_inc(landed, 16)

            @block.tensor
            def _(pe):
                pe.wait_ge(landed, 16)
                pe.wait_ge(meant, 1)

                def mean(p):
                    if p >= 2:
                        pe.wait_ge(centred, p - 1)
                    pe.matmul(ps[:, p % 2, :], mean_of[:], slab[:, SLAB_K + p, :], start=True, stop=True).then_inc(averaged, 1)

                mean(0)
                for p in range(PAIRS):
                    if p + 1 < PAIRS:
                        mean(p + 1)
                    pe.wait_ge(squared, p + 1)
                    if p >= 2:
                        pe.wait_ge(logged, p - 1)
                    pe.matmul(ps[:, 2 + p % 2, :], mean_of[:], out[:, p, :], start=True, stop=True).then_inc(spread, 1)
                    if p >= 2:
                        pe.wait_ge(gated, p - 1)
                    pe.matmul(ps[:, 4 + p % 2, :], g2[:, p * P:(p + 1) * P], slab[:, SLAB_G, :], start=True, stop=True)\
                        .then_inc(spread, 1)

            @block.vector
            def _(dve):
                dve.tensor_scalar(mean_of[:], k.head_ones[:], 1.0 / HD, None, ALU.mult).then_inc(meant, 1)

                def centre(p):
                    dve.wait_ge(averaged, p + 1)
                    y = slab[:, SLAB_K + p, :]
                    dve.tensor_tensor(y, y, ps[:, p % 2, :], ALU.subtract).then_inc(centred, 1)

                centre(0)
                for p in range(PAIRS):
                    if p + 1 < PAIRS:
                        centre(p + 1)
                    y = slab[:, SLAB_K + p, :]
                    dve.wait_ge(rooted, p + 1)
                    dve.scalar_tensor_tensor(y, y, gain[:, p:p + 1], rstd[:, p % 2, :], ALU.mult, ALU.mult).then_inc(scaled, 1)
                    dve.wait_ge(scaled, p + 1)
                    dve.scalar_tensor_tensor(y, y, shift[:, p:p + 1], slab[:, SLAB_V + p, :], ALU.add, ALU.add).then_inc(shifted, 1)
                    dve.wait_ge(shifted, p + 1)
                    dve.wait_ge(spread, 2 * p + 2)
                    dve.tensor_tensor(out[:, p, :], y, ps[:, 4 + p % 2, :], ALU.mult).then_inc(gated, 1)

            @block.scalar
            def _(act):
                for p in range(PAIRS):
                    act.wait_ge(centred, p + 1)
                    act.activation(out[:, p, :], slab[:, SLAB_K + p, :], ACT.Square).then_inc(squared, 1)
                    act.wait_ge(spread, 2 * p + 1)
                    if p >= 2:
                        act.wait_ge(rooted, p - 1)
                    act.activation(logs[:, p % 2, :], ps[:, 2 + p % 2, :], ACT.Ln, bias=k.eps[:, 1:2]).then_inc(logged, 1)
                    act.wait_ge(logged, p + 1)
                    if p >= 2:
                        act.wait_ge(scaled, p - 1)
                    act.activation(rstd[:, p % 2, :], logs[:, p % 2, :], ACT.Exp, scale=-0.5).then_inc(rooted, 1)


def memory_attention(k, slab, mix):
    nc, ps = k.nc, k.ps
    gain = k.col_a[:, ROW_A["mem_q_norm_g"]:ROW_A["mem_q_norm_g"] + 1]
    heads, scale = 4, HD ** -0.5
    with Phase(k, "mem_attn") as f:
        q, squares, logs, rstd = (f.sb(s, [P, 2, T]) for s in ("q", "squares", "logs", "rstd"))
        probs = f.sb("probs", [P, 2, TT, M])
        probs_T = f.sb("probs_T", [P, 2, 2, T])
        top, total, inv = (f.sb(s, [P, heads, TT]) for s in ("top", "total", "inv"))
        squared, summed, logged, rooted, normed = (f.sem(s) for s in ("squared", "summed", "logged", "rooted", "normed"))
        scored, topped, negated, exped, inverted, scaled, turned, copied, mixed, kept = (f.sem(s) for s in (
            "scored", "topped", "negated", "exped", "inverted", "scaled", "turned", "copied", "mixed", "kept"))
        with nc.Block() as block:

            @block.tensor
            def _(pe):
                pe.wait_ge(squared, 1)
                for m in range(2):
                    last = pe.matmul(ps[:, m, :], k.head_ones[:], squares[:, m, :], start=True, stop=True)
                last.then_inc(summed, 1)
                pe.wait_ge(normed, 1)

                def scores(h):
                    rows = slice((h % 2) * HD, (h % 2 + 1) * HD)
                    if h:
                        pe.wait_ge(exped, TT * h)
                    for t in range(TT):
                        last = pe.matmul(ps[:, 2 + t // 2, (t % 2) * M:(t % 2 + 1) * M], q[rows, h // 2, t * P:(t + 1) * P],
                                         k.k_mem[rows, h // 2, :], start=True, stop=True)
                    last.then_inc(scored, 1)

                scores(0)
                for h in range(heads):
                    if h + 1 < heads:
                        scores(h + 1)
                    pe.wait_ge(scaled, h + 1)
                    if h:
                        pe.wait_ge(copied, h)
                    for m in range(2):
                        for t in range(TT):
                            last = pe.transpose(ps[:, 4 + m, t * P:(t + 1) * P], probs[:, h % 2, t, m * P:(m + 1) * P], k.ident[:])
                    last.then_inc(turned, 1)
                    pe.wait_ge(copied, h + 1)
                    if h >= 2:
                        pe.wait_ge(kept, h - 1)
                    rows = slice((h % 2) * HD, (h % 2 + 1) * HD)
                    for m in range(2):
                        last = pe.matmul(ps[rows, 6 + h % 2, :], k.v_mem[:, m, h * HD:(h + 1) * HD], probs_T[:, h % 2, m, :],
                                         start=m == 0, stop=m == 1)
                    last.then_inc(mixed, 1)

            @block.scalar
            def _(act):
                act.activation(squares[:], slab[:, SLAB_Q:SLAB_Q + 2, :], ACT.Square).then_inc(squared, 1)
                act.wait_ge(summed, 1)
                act.activation(logs[:], ps[:, 0:2, :], ACT.Ln, bias=k.eps[:, 0:1], scale=1.0 / HD).then_inc(logged, 1)
                act.wait_ge(logged, 1)
                act.activation(rstd[:], logs[:], ACT.Exp, scale=-0.5).then_inc(rooted, 1)
                for h in range(heads):
                    act.wait_ge(negated, h + 1)
                    if h >= 2:
                        act.wait_ge(turned, h - 1)
                    for t in range(TT):
                        act.activation(probs[:, h % 2, t, :], ps[:, 2 + t // 2, (t % 2) * M:(t % 2 + 1) * M], ACT.Exp,
                                       bias=top[:, h, t:t + 1], scale=scale, accum_out=total[:, h, t:t + 1]).then_inc(exped, 1)
                    act.wait_ge(turned, h + 1)
                    if h >= 2:
                        act.wait_ge(mixed, h - 1)
                    act.copy(probs_T[:, h % 2], ps[:, 4:6, :]).then_inc(copied, 1)

            @block.vector
            def _(dve):
                dve.wait_ge(rooted, 1)
                dve.scalar_tensor_tensor(q[:], slab[:, SLAB_Q:SLAB_Q + 2, :], gain, rstd[:], ALU.mult, ALU.mult).then_inc(normed, 1)

                def tops(h):
                    dve.wait_ge(scored, h + 1)
                    dve.tensor_reduce(top[:, h, :], ps[:, 2:4, :].rearrange("p b (t m) -> p (b t) m", t=2), AX.X, ALU.max)\
                        .then_inc(topped, 1)
                    dve.wait_ge(topped, h + 1)
                    dve.tensor_scalar(top[:, h, :], top[:, h, :], -scale, None, ALU.mult).then_inc(negated, 1)

                tops(0)
                for h in range(heads):
                    dve.wait_ge(exped, TT * (h + 1))
                    dve.reciprocal(inv[:, h, :], total[:, h, :]).then_inc(inverted, 1)
                    if h + 1 < heads:
                        tops(h + 1)
                    dve.wait_ge(mixed, h + 1)
                    rows = slice((h % 2) * HD, (h % 2 + 1) * HD)
                    dve.tensor_copy(mix[rows, PAIRS + h // 2, :], ps[rows, 6 + h % 2, :]).then_inc(kept, 1)

            @block.gpsimd
            def _(pool):
                for h in range(heads):
                    pool.wait_ge(inverted, h + 1)
                    pool.tensor_tensor(probs[:, h % 2], probs[:, h % 2], inv[:, h, :].unsqueeze(2).broadcast_to([P, TT, M]),
                                       ALU.mult).then_inc(scaled, 1)


def rwkv_block(k):
    with Phase(k, "first") as f:
        mix = f.sb("mix", [P, KT, T])
        with Phase(k, "rwkv") as g:
            slab, lw, rate = g.sb("slab", [P, 22, T]), g.sb("lw", [P, PAIRS, T]), g.sb("rate", [P, PAIRS, T])
            passes = g.sb("passes", [P, PAIRS, NCH - 1])
            low, low_landed = mix[:, 0:3, :].rearrange("p b t -> p (b t)").rearrange("p (h m) -> p h m", h=2), g.sem("low_landed")
            rwkv_in(k, slab, low, low_landed)
            decay_and_rate(k, slab, lw, rate, low, low_landed)
            scan_chunks(k, slab, lw, rate, passes, mix)
            scan_states(k, slab, lw, rate, passes)
            rwkv_out(k, slab, mix)
            memory_attention(k, slab, mix)
        add_projection(k, "w_out", mix, (KT,), split=True)
    squared_relu_ffn(k)



FOX_H, NSA_H, GROUPS = 8, 8, 2
NCMP = T // 16 - 1
ATTN_WIDTHS = [PW] * 11 + [P, P]


def slope(h):
    return 2.0 ** -(h + 1)


class Attention:

    def __init__(self, f):
        self.fq, self.fk = f.sb("fq", [P, FOX_H, T]), f.sb("fk", [P, FOX_H // 2, T])
        self.fv = f.sb("fv", [P, TT, FOX_H * HD])
        self.nq = f.sb("nq", [P, NSA_H, T])
        self.ks, self.kw = f.sb("ks", [P, GROUPS, T]), f.sb("kw", [P, GROUPS, T])
        self.vs, self.vw = f.sb("vs", [P, TT, P]), f.sb("vw", [P, TT, P])
        self.kc, self.vc = f.sb("kc", [P, GROUPS, 32]), f.sb("vc", [32, GROUPS, HD])
        self.gates = f.sb("gates", [P, TT, 24])

    def add_early(self, f):
        self.cmp_in = f.sb("cmp_in", [P, 2, T])
        self.u, self.gates_T = f.sb("forget_in", [FOX_H, T]), f.sb("gates_T", [32, T])

    def add_tables(self, f):
        self.forget = f.sb("forget", [P, FOX_H, T])
        self.dist = f.sb("dist", [P, T])
        self.cmp_dist = f.sb("cmp_dist", [P, TT, 32])
        self.future = f.sb("future", [P, P])


def attn_project(k, a, gain, compress, heads):
    nc, ps, ins, g0 = k.nc, k.ps, k.ins, k.first_panel["attn_in"]
    n_pairs, n_all = 11, 24
    with Phase(k, "attn_in") as f:
        b_f, ks_raw, kw_raw = f.sb("b_f", [FOX_H, 1]), heads[:, 6, :], heads[:, 7, :]
        landed, first, copied, filled = (f.sem(s) for s in ("landed", "first", "copied", "filled"))
        doubled = compress[3]
        nq_scale = f.sb("nq_scale", [P, NSA_H // 2])
        x = Operand(k, f, k.xT, gain, normed=heads[:, 0:2, :])
        features = {0: (a.fq, 0, -0.125), 1: (a.fq, 2, -0.125), 2: (a.fk, 0, 1.0), 3: (a.fk, 2, 1.0),
                    6: (a.nq, 0, None), 7: (a.nq, 2, None), 8: (a.cmp_in, 0, 1.0)}
        by_token = (4, 5, 10)
        with nc.Block() as block:

            @block.sync
            def _(sp):
                with nc.allow_non_contiguous_dma(reason="eight numbers"):
                    sp.dma_start(b_f[:], ins["fox_b_f_2"].rearrange("l h -> h l")).then_inc(landed, 16)
                w1, w2, compress_landed, _ = compress
                for half in range(2):
                    rows = slice(half * HD, (half + 1) * HD)
                    for kv in range(2):
                        sp.dma_start(w1[rows, kv], ins["nsa_cmp_w1_2"][0, kv].rearrange("(i d) h -> d i h", d=HD)).then_inc(compress_landed, 16)
                        sp.dma_start(w2[rows, kv, :], ins["nsa_cmp_w2_2"][0, kv]).then_inc(compress_landed, 16)
                k.load_panels(sp, k.lookahead("attn_in"))
                sp.wait_ge(copied, 20)
                for g in range(GROUPS):
                    for half in range(2):
                        for src, dst in ((ks_raw, a.ks), (kw_raw, a.kw)):
                            sp.dma_start(dst[half * HD:(half + 1) * HD, g, :], src[g * HD:(g + 1) * HD, :]).then_inc(doubled, 16)

            @block.tensor
            def _(pe):
                def start(b, n):
                    w = k.panel(pe, g0, n // 4, n % 4, KT, ATTN_WIDTHS[n])
                    if b >= 8:
                        pe.wait_ge(copied, b - 7)
                    return w

                def columns(b, n, m):
                    w_hi, w_lo = start(b, n)
                    at = slice(m * P, (m + 1) * P)
                    for kt in range(KT):
                        if b == 0:
                            x.ready(pe, kt)
                        last = product(pe, ps[:, b % 8, :], (w_hi[:, kt, at], w_lo[:, kt, at]), x.halves(kt), kt == 0, kt == KT - 1)
                    return last

                def tokens(b, n, c0, cols, tiles):
                    w_hi, w_lo = start(b, n)
                    for i, t in enumerate(tiles):
                        for kt in range(KT):
                            last = product(pe, ps[:, b % 8, i * cols:(i + 1) * cols], x.halves(kt, slice(t * P, (t + 1) * P)),
                                           (w_hi[:, kt, c0:c0 + cols], w_lo[:, kt, c0:c0 + cols]), kt == 0, kt == KT - 1)
                    return last

                for n in range(n_pairs):
                    for m in range(2):
                        b = 2 * n + m
                        last = tokens(b, n, 0, PW, (2 * m, 2 * m + 1)) if n in by_token else columns(b, n, m)
                        last.then_inc(k.panel_used if m else first, 1)
                for b, n in ((22, 11), (23, 12)):
                    columns(b, n, 0).then_inc(k.panel_used, 1)

            @block.gpsimd
            def _(pool):
                for q in (a.fq, a.nq):
                    by_half = q[:].rearrange("p (i e) t -> p i e t", e=2)
                    for e in range(2):
                        pool.memset(by_half[(1 - e) * HD:(2 - e) * HD, :, e, :], 0.0)

            @block.vector
            def _(dve):
                for h in range(NSA_H):
                    made = dve.memset(nq_scale[(h % 2) * HD:(h % 2 + 1) * HD, h // 2:h // 2 + 1], -0.125 / slope(h))
                made.then_inc(filled, 1)
                x.lows(dve)
                for n in range(len(ATTN_WIDTHS)):
                    k.split_low(dve, g0, 0, n + 2)

            @block.scalar
            def _(act):
                x.highs(act)
                for b in range(n_all):
                    n, m, bank = b // 2, b % 2, ps[:, b % 8, :]
                    if b >= 2 * n_pairs:
                        act.wait_ge(k.panel_used, g0 + n_pairs + b - 2 * n_pairs + 1)
                    elif m:
                        act.wait_ge(k.panel_used, g0 + n + 1)
                    else:
                        act.wait_ge(first, n + 1)
                    if b >= 2 * n_pairs or m:
                        k.split_high(act, g0, 0, (n_pairs + b - 2 * n_pairs if b >= 2 * n_pairs else n) + 2)
                    if b == 22:
                        act.wait_ge(landed, 16)
                        made = act.activation(a.u[:], bank[0:FOX_H], ACT.Identity, bias=b_f[:])
                    elif b == 23:
                        made = act.activation(a.gates_T[:], bank[3 * 32:P], ACT.Sigmoid)
                        load_log_exp(act)
                    elif n in features:
                        tile, at, scale = features[n]
                        if scale is None:
                            act.wait_ge(filled, 1)
                            scale = nq_scale[:, at + m:at + m + 1]
                        if n in (2, 3, 8):
                            made = act.mul(tile[:, at + m, :], bank, scale)
                        else:
                            for e in range(2):
                                rows = slice(e * HD, (e + 1) * HD)
                                made = act.mul(tile[rows, 2 * (at + m) + e, :], bank[rows], scale if isinstance(scale, float) else scale[rows])
                    elif n in (4, 5):
                        made = act.copy(a.fv[:, 2 * m:2 * m + 2, (n - 4) * PW:(n - 3) * PW],
                                        bank.rearrange("p (t c) -> p t c", t=2))
                    elif n == 9:
                        made = act.copy(kw_raw if m else ks_raw, bank)
                    else:
                        for tile, c in ((a.vs, 0), (a.vw, P)):
                            made = act.copy(tile[:, 2 * m:2 * m + 2, :], bank.rearrange("p (t c) -> p t c", t=2)[:, :, c:c + P])
                    made.then_inc(copied, 1)


def attn_prepare(k, a, heads, compress):
    nc, ps, ins = k.nc, k.ps, k.ins
    with Phase(k, "attn_pre") as f:
        w1, w2, landed, doubled = compress
        hidden = f.sb("hidden", [P, 2, 32])
        soft, neg = f.sb("soft", [FOX_H, T]), f.sb("neg", [FOX_H, T])
        room = heads[:].rearrange("p b t -> p (b t)")
        flat = room[:, 0:64 * NCMP].rearrange("p (v i n) -> p v i n", v=2, i=32)
        pick = room[0:FOX_H, 4 * T:6 * T].rearrange("h (g c) -> h g c", g=FOX_H)
        dist, steep = a.dist, heads[0:FOX_H, 7, :]
        ones = k.ones[0:FOX_H, 0:1].broadcast_to([FOX_H, T])
        filled, cut, opened, negated, softened, summed, spread, kept, blocked, mapped, bent, made, zeroed, gated = (
            f.sem(s) for s in ("filled", "cut", "opened", "negated", "softened", "summed", "spread", "kept",
                               "blocked", "mapped", "bent", "made", "zeroed", "gated"))
        with nc.Block() as block:

            @block.gpsimd
            def _(pool):
                pool.memset(pick[:], 0.0).then_inc(filled, 1)
                pool.iota(dist[:], [[-1, T]], base=T - P, channel_multiplier=1, allow_small_or_imprecise_dtypes=True).then_inc(filled, 1)
                pool.iota(a.cmp_dist[:], [[P, TT], [-16, 32]], base=-31, channel_multiplier=1,
                          allow_small_or_imprecise_dtypes=True).then_inc(filled, 1)
                pool.memset(a.future[:], 0.0).then_inc(filled, 1)
                pool.wait_ge(filled, 4)
                pool.affine_select(out=pick[:], in_=pick[:], pattern=[[-1, FOX_H], [0, P]], compare_op=ALU.not_equal, fill=-1.0,
                                   base=0, channel_multiplier=1).then_inc(cut, 1)
                pool.affine_select(out=dist[:], in_=dist[:], pattern=[[-1, T]], compare_op=ALU.is_ge, fill=BIG, base=T - P,
                                   channel_multiplier=1).then_inc(cut, 1)
                pool.affine_select(out=a.cmp_dist[:], in_=a.cmp_dist[:], pattern=[[P, TT], [-16, 32]], compare_op=ALU.is_ge,
                                   fill=BIG, base=-31, channel_multiplier=1).then_inc(cut, 1)
                pool.affine_select(out=a.future[:], in_=a.future[:], pattern=[[-1, P]], compare_op=ALU.is_ge, fill=BIG, base=0,
                                   channel_multiplier=1).then_inc(cut, 1)

            @block.scalar
            def _(act):
                act.activation(soft[:], a.u[:], ACT.Abs).then_inc(opened, 1)
                act.wait_ge(opened, 1)
                act.activation(soft[:], soft[:], ACT.Exp, scale=-1.0).then_inc(opened, 1)
                act.wait_ge(opened, 2)
                act.activation(soft[:], soft[:], ACT.Ln, bias=k.eps[0:FOX_H, 3:4]).then_inc(opened, 1)
                act.wait_ge(gated, 1)
                act.copy(a.gates[:], ps[:, 6, 0:TT * 32].rearrange("p (t c) -> p t c", t=TT)[:, :, 8:32])
                act.wait_ge(mapped, 1)
                act.wait_ge(zeroed, 1)
                act.activation(hidden[:, :, 0:NCMP], ps[:, 4, :].rearrange("p (v n) -> p v n", v=2)[:, :, 0:NCMP],
                               ACT.Gelu_apprx_tanh).then_inc(bent, 1)
                load_log_exp(act)
                for h in range(FOX_H):
                    act.wait_ge(spread, h + 1)
                    act.copy(a.forget[:, h, :], ps[:, h % 4, :]).then_inc(kept, 1)
                act.wait_ge(made, 1)
                act.copy(a.kc[:], ps[:, 5:8:2, 0:32])
                act.copy(a.vc[:], ps[0:32, 5:8:2, HD:2 * HD])

            @block.vector
            def _(dve):
                dve.memset(hidden[:], 0.0).then_inc(zeroed, 1)
                for kv in range(2):
                    by_16 = a.cmp_in[:, kv, :].rearrange("p (n i) -> p i n", i=16)
                    for half in range(2):
                        at = slice(16 * half, 16 * half + 16)
                        dve.tensor_tensor(flat[:, kv, at, :], by_16[:, :, half:half + NCMP],
                                          k.pe_T[:, kv, at].unsqueeze(2).broadcast_to([P, 16, NCMP]), ALU.add).then_inc(blocked, 1)
                dve.tensor_scalar(neg[:], a.u[:], -1.0, 0.0, ALU.mult, ALU.max).then_inc(negated, 1)
                dve.wait_ge(opened, 3)
                dve.wait_ge(negated, 1)
                dve.tensor_tensor(neg[:], neg[:], soft[:], ALU.add).then_inc(softened, 1)
                dve.wait_ge(softened, 1)
                dve.wait_ge(doubled, 16 * 4 * GROUPS)
                dve.tensor_tensor_scan(steep[:], ones, neg[:], 0.0, ALU.mult, ALU.add).then_inc(summed, 1)

            @block.tensor
            def _(pe):
                for t in range(TT):
                    last = pe.transpose(ps[:, 6, t * 32:(t + 1) * 32], a.gates_T[:, t * P:(t + 1) * P], k.ident[0:32, 0:32])
                last.then_inc(gated, 1)
                pe.wait_ge(blocked, 4)
                pe.wait_ge(landed, 16 * 8)
                for kv in range(2):
                    for g in range(GROUPS):
                        rows = slice(g * HD, (g + 1) * HD)
                        for i in range(32):
                            last = pe.matmul(ps[rows, 4, kv * 256:kv * 256 + NCMP], w1[rows, kv, i, :], flat[rows, kv, i, :],
                                             start=i == 0, stop=i == 31)
                last.then_inc(mapped, 1)
                pe.wait_ge(summed, 1)
                pe.wait_ge(cut, 1)
                for h in range(FOX_H):
                    if h >= 4:
                        pe.wait_ge(kept, h - 3)
                    pe.matmul(ps[:, h % 4, :], pick[:, h, :], steep[:], start=True, stop=True).then_inc(spread, 1)
                pe.wait_ge(bent, 1)
                for g in range(GROUPS):
                    rows, bank = slice(g * HD, (g + 1) * HD), 5 + 2 * g
                    for half in range(2):
                        pe.matmul(ps[half * HD:(half + 1) * HD, bank, 0:32], w2[rows, 0, :], hidden[rows, 0, :], start=True, stop=True)
                    last = pe.matmul(ps[0:32, bank, HD:2 * HD], hidden[rows, 1, :], w2[rows, 1, :], start=True, stop=True)
                last.then_inc(made, 1)


def attention(k, a, heads):
    nc, ps = k.nc, k.ps
    steps = [("cmp", i) for i in range(NSA_H // 2)] + [("fox", i) for i in range(FOX_H // 2)]
    steps += [(kind, i) for i in range(NSA_H // 2) for kind in ("slc", "win")]
    n_steps, slots = len(steps), 6
    tiles = (3, 2, 1, 0)
    s_at = [{3: (0, 0), 2: (1, 0), 0: (1, 384), 1: (2, 0)}, {3: (3, 0), 2: (4, 0), 0: (4, 384), 1: (2, 256)}]
    z_at = {3: 0, 2: 512, 0: 896, 1: 1024}
    w_at = {0: 0, 1: 512, 3: 896, 2: 1024}
    piece_parts = [[(0, 0, 0)], [(0, 1, 0), (0, 3, 384)], [(0, 2, 0), (1, 2, 256)], [(1, 0, 0)], [(1, 1, 0), (1, 3, 384)]]
    by_act = (0, 2)
    pieces, done, first_piece = [], {"act": 0, "dve": 0}, []
    for s, (kind, _) in enumerate(steps):
        first_piece.append(len(pieces))
        for i in range(2 if kind == "cmp" else len(piece_parts)):
            eng = ("act", "dve")[i] if kind == "cmp" else "act" if i in by_act else "dve"
            done[eng] += 1
            pieces.append((s, i, eng, done[eng]))
    out_bank, turn_bank = 7, 5
    cmp_before = [sum(x[0] == "cmp" for x in steps[:s]) for s in range(n_steps + 1)]

    def pieces_of(s):
        return range(first_piece[s], first_piece[s + 1] if s + 1 < n_steps else len(pieces))

    def first_of_head(s):
        return steps[s][0] != "win"

    def last_of_head(s):
        return steps[s][0] != "slc"

    def block_of(s):
        return steps[s][1] + (0 if steps[s][0] == "fox" else FOX_H // 2)

    heads_before = [sum(last_of_head(x) for x in range(s)) for s in range(n_steps + 1)]

    with Phase(k, "attn") as f:
        z, w_T = f.sb("z", [P, slots, 1280]), f.sb("w_T", [P, 2, 1280])
        top, total, weight = (f.sb(s, [P, slots, TT]) for s in ("top", "total", "weight"))
        scored, lowered, exped, weighted, scaled, scaled_a, scaled_v, turned, mixed, kept, floored, inverted, clamped, crossed = (
            f.sem(s) for s in ("scored", "lowered", "exped", "weighted", "scaled", "scaled_a", "scaled_v", "turned", "mixed", "kept",
                               "floored", "inverted", "clamped", "crossed"))
        out_of_bank = {"act": f.sem("copied_a"), "dve": f.sem("copied_v")}

        def rows_of(e):
            return slice(e * HD, (e + 1) * HD)

        def scaled_apart(u):
            return u + 1 - 2 * cmp_before[u // 2]

        def copy_piece(eng, n):
            s, i, who, _ = pieces[n]
            bank, to = ps[:, turn_bank + n % 2, :], w_T
            eng.wait_ge(turned, n + 1)
            if s:
                eng.wait_ge(mixed, s)
            if steps[s][0] == "cmp":
                bank, to = bank[0:32], w_T[0:32, i, 0:T]
            elif i == 2:
                bank, to = bank.rearrange("p (e c) -> p e c", e=2), to[:, :, w_at[2]:w_at[2] + 2 * P]
            else:
                c = w_at[piece_parts[i][0][1]]
                to = to[:, piece_parts[i][0][0], c:c + T]
            made = eng.copy(to, bank) if who == "act" else eng.tensor_copy(to, bank)
            made.then_inc(out_of_bank[who], 1)

        with nc.Block() as block:

            @block.tensor
            def _(pe):
                def scores(s):
                    kind, i = steps[s]
                    if s:
                        pe.wait_ge(lowered, 2 * TT * s)
                    q, keys = {"fox": (a.fq, a.fk[:, i, :]), "slc": (a.nq, a.ks[:, i // 2, :]),
                               "win": (a.nq, a.kw[:, i // 2, :]), "cmp": (a.nq, a.kc[:, i // 2, :])}[kind]

                    def tile(e, t):
                        q_t, keys_e = q[:, 2 * i + e, t * P:(t + 1) * P], keys
                        if kind == "cmp":
                            return pe.matmul(ps[:, 3 * e, t * 32:(t + 1) * 32], q_t, keys_e, start=True, stop=True)
                        bank, c = s_at[e][t]
                        n = (t + 1) * P
                        return pe.matmul(ps[:, bank, c:c + n], q_t, keys_e[:, 0:n], start=True, stop=kind != "fox")

                    def hide(e, t):
                        bank, c = s_at[e][t]
                        return pe.matmul(ps[:, bank, c + t * P:c + (t + 1) * P], k.ident[:], a.future[:], start=False, stop=True)

                    for group in ([(0, 1)], [(1, 3), (0, 3)], [(1, 2), (0, 2)], [(1, 0), (0, 0)], [(1, 1)]):
                        if group == [(1, 1)]:
                            pe.wait_ge(crossed, s + 1)
                        for e, t in group:
                            last = tile(e, t)
                        if kind == "fox":
                            for e, t in group:
                                last = hide(e, t)
                        if group == [(0, 1)]:
                            last.then_inc(crossed, 1)
                    last.then_inc(scored, 1)

                def turn(n):
                    s, i, _, _ = pieces[n]
                    cmp = steps[s][0] == "cmp"
                    for u in sorted({2 * s + i} if cmp else {2 * s + part[0] for part in piece_parts[i]}):
                        pe.wait_ge(scaled, u + 1)
                        if not cmp:
                            pe.wait_ge(scaled_a, scaled_apart(u))
                            pe.wait_ge(scaled_v, scaled_apart(u))
                    if n >= 2:
                        _, _, who, shows = pieces[n - 2]
                        pe.wait_ge(out_of_bank[who], shows)
                    bank = turn_bank + n % 2
                    if cmp:
                        u = (2 * s + i) % slots
                        for t in range(TT):
                            last = pe.transpose(ps[0:32, bank, t * P:(t + 1) * P], z[:, u, t * 32:(t + 1) * 32], k.ident[:])
                    else:
                        for e, j, c in piece_parts[i]:
                            for t in range(j, TT):
                                at = z_at[t] + j * P
                                last = pe.transpose(ps[:, bank, c + (t - j) * P:c + (t - j + 1) * P], z[:, (2 * s + e) % slots, at:at + P], k.ident[:])
                    last.then_inc(turned, 1)

                def mix(s, j):
                    kind, i = steps[s]
                    if kind == "cmp" and j:
                        return
                    if j == 0:
                        for n in pieces_of(s)[-2:]:
                            pe.wait_ge(out_of_bank[pieces[n][2]], pieces[n][3])
                        if first_of_head(s) and heads_before[s]:
                            pe.wait_ge(kept, heads_before[s])
                    first, final = first_of_head(s) and j == 0, last_of_head(s) and j in (0 if kind == "cmp" else TT - 1,)
                    for e in range(2):
                        out = ps[rows_of(e), out_bank, :]
                        if kind == "cmp":
                            last = pe.matmul(out, a.vc[:, i // 2, :], w_T[0:32, e, 0:T], start=first, stop=final)
                            continue
                        v = {"fox": a.fv[:, j, (2 * i + e) * HD:(2 * i + e + 1) * HD] if kind == "fox" else None,
                             "slc": a.vs[:, j, (i // 2) * HD:(i // 2 + 1) * HD], "win": a.vw[:, j, (i // 2) * HD:(i // 2 + 1) * HD]}[kind]
                        last = pe.matmul(out[:, j * P:T], v, w_T[:, e, w_at[j]:w_at[j] + T - j * P], start=first, stop=final)
                    if j == TT - 1 or kind == "cmp":
                        last.then_inc(mixed, 1)

                scores(0)
                scores(1)
                for s in range(n_steps):
                    for n in pieces_of(s):
                        turn(n)
                    if s + 2 < n_steps:
                        scores(s + 2)
                    for j in range(TT):
                        mix(s, j)

            @block.vector
            def _(dve):
                def lower(u):
                    s, e, at = u // 2, u % 2, u % slots
                    kind, h = steps[s][0], 2 * steps[s][1] + e
                    dve.wait_ge(scored, s + 1)
                    if s >= slots // 2:
                        dve.wait_ge(turned, first_piece[s - slots // 2 + 1])
                    if kind == "cmp":
                        zc, c = z[:, at, 0:TT * 32].rearrange("p (t n) -> p t n", t=TT), 2 * cmp_before[s] + e
                        dve.tensor_tensor(zc, a.cmp_dist[:], ps[:, 3 * e, 0:TT * 32].rearrange("p (t n) -> p t n", t=TT), ALU.add).then_inc(floored, 1)
                        dve.wait_ge(floored, 2 * c + 1)
                        dve.tensor_reduce(top[:, at, :], zc, AX.X, ALU.min).then_inc(floored, 1)
                        dve.wait_ge(floored, 2 * c + 2)
                        dve.tensor_scalar(top[:, at, :], top[:, at, :], 1e26, slope(h), ALU.min, ALU.mult).then_inc(lowered, TT)
                        return
                    for t in tiles:
                        bank, c = s_at[e][t]
                        n = (t + 1) * P
                        bias, by = (a.forget[:, h, 0:n], 1.0) if kind == "fox" else (a.dist[:, T - n:T], slope(h))
                        dve.tensor_tensor_reduce(z[:, at, z_at[t]:z_at[t] + n], ps[:, bank, c:c + n], bias, by, 3e38,
                                                 ALU.add, ALU.min, top[:, at, t:t + 1]).then_inc(lowered, 1)

                def weigh(u):
                    s, at = u // 2, u % slots
                    kind, h = steps[s][0], 2 * steps[s][1] + u % 2
                    dve.wait_ge(exped, u + 1)
                    if u >= slots:
                        dve.wait_ge(scaled, u - slots + 1)
                    if kind == "cmp":
                        dve.tensor_scalar(total[:, at, :], total[:, at, :], 1e-30, None, ALU.max).then_inc(clamped, 1)
                        dve.wait_ge(clamped, 2 * cmp_before[s] + u % 2 + 1)
                    if kind == "fox":
                        dve.reciprocal(weight[:, at, :], total[:, at, :]).then_inc(weighted, 1)
                    else:
                        dve.reciprocal(weight[:, at, :], total[:, at, :]).then_inc(inverted, 1)
                        dve.wait_ge(inverted, u + 1 - (FOX_H if s >= steps.index(("slc", 0)) else 0))
                        gate = a.gates[:, :, 3 * h + ("cmp", "slc", "win").index(kind)]
                        dve.tensor_tensor(weight[:, at, :], weight[:, at, :], gate, ALU.mult).then_inc(weighted, 1)
                    if kind != "cmp":
                        part = z[:, at, z_at[2]:z_at[2] + 3 * P]
                        dve.wait_ge(weighted, u + 1)
                        dve.tensor_scalar(part, part, weight[:, at, 2:3], None, ALU.mult).then_inc(scaled_v, 1)

                def add(s):
                    if steps[s][0] == "win":
                        block = heads[:, block_of(s), :]
                        dve.wait_ge(mixed, s + 1)
                        dve.wait_ge(kept, steps[s][1] + 1)
                        dve.tensor_tensor(block, ps[:, out_bank, :], block, ALU.add).then_inc(kept, 1)

                for u in range(2):
                    lower(u)
                for u in range(2):
                    weigh(u)
                for s in range(n_steps):
                    ahead = (2 * s + 2, 2 * s + 3) if s + 1 < n_steps else ()
                    for u in ahead:
                        lower(u)
                    if s:
                        add(s - 1)
                    for n in pieces_of(s):
                        if pieces[n][2] == "dve":
                            copy_piece(dve, n)
                    for u in ahead:
                        weigh(u)
                add(n_steps - 1)

            @block.scalar
            def _(act):
                def exps(u):
                    s, at = u // 2, u % slots
                    if u >= slots:
                        act.wait_ge(weighted, u - slots + 1)
                    for i, t in enumerate(tiles):
                        act.wait_ge(lowered, TT * u + i + 1)
                        c, n = (t * 32, 32) if steps[s][0] == "cmp" else (z_at[t], (t + 1) * P)
                        last = act.activation(z[:, at, c:c + n], z[:, at, c:c + n], ACT.Exp, bias=top[:, at, t:t + 1],
                                              scale=-slope(2 * steps[s][1] + u % 2) if steps[s][0] == "cmp" else -1.0, accum_out=total[:, at, t:t + 1])
                    last.then_inc(exped, 1)

                def scale(u):
                    if steps[u // 2][0] == "cmp":
                        return
                    at, c = u % slots, z_at[TT - 1]
                    act.wait_ge(weighted, u + 1)
                    act.mul(z[:, at, c:c + T], z[:, at, c:c + T], weight[:, at, TT - 1:TT]).then_inc(scaled_a, 1)

                def keep(s):
                    if steps[s][0] in ("cmp", "fox"):
                        act.wait_ge(mixed, s + 1)
                        act.copy(heads[:, block_of(s), :], ps[:, out_bank, :]).then_inc(kept, 1)

                for u in range(2):
                    exps(u)
                for u in range(2):
                    scale(u)
                for s in range(n_steps):
                    ahead = s + 1 < n_steps
                    if ahead:
                        exps(2 * s + 2)
                    for n in pieces_of(s):
                        if pieces[n][2] == "act":
                            copy_piece(act, n)
                    if s:
                        keep(s - 1)
                    if ahead:
                        exps(2 * s + 3)
                        scale(2 * s + 2)
                        scale(2 * s + 3)
                keep(n_steps - 1)

            @block.gpsimd
            def _(pool):
                for u in range(2 * n_steps):
                    pool.wait_ge(weighted, u + 1)
                    cmp = steps[u // 2][0] == "cmp"
                    for t in range(TT if cmp else 2):
                        c, n = (t * 32, 32) if cmp else (z_at[t], (t + 1) * P)
                        last = pool.tensor_scalar(z[:, u % slots, c:c + n], z[:, u % slots, c:c + n], weight[:, u % slots, t:t + 1], None, ALU.mult)
                    last.then_inc(scaled, 1)



POOL_WINDOWS = (2, 4, 8, 16)


def pool_mixer(k, out, norm_gain):
    nc, ps, g0 = k.nc, k.ps, k.first_panel["pool"]
    gain, groups, banks = k.col_b[:, ROW_B["pool_scale_2"]:ROW_B["pool_scale_2"] + KT], len(POOL_WINDOWS), 6
    with Phase(k, "pool") as f:
        h, sums, pooled, diff = (f.sb(s, [P, KT, T]) for s in ("h", "sums", "pooled", "diff"))
        count, inv = f.sb("count", [P, 16]), f.sb("inv", [P, 16])
        one = k.ones[:, 0:1].broadcast_to([P, T])
        x, rows = Operand(k, f, pooled), Stats(k, f)
        counted, inverted, gained, normed, summed, apart, pooled_s, first, scaled = (f.sem(s) for s in (
            "counted", "inverted", "gained", "normed", "summed", "apart", "pooled", "first", "scaled"))
        with nc.Block() as block:

            @block.sync
            def _(sp):
                k.load_panels(sp, k.lookahead("pool"))

            @block.gpsimd
            def _(pool):
                pool.iota(count[:], [[1, 16]], base=1, channel_multiplier=0, allow_small_or_imprecise_dtypes=True).then_inc(counted, 1)
                for b in range(KT):
                    pool.wait_ge(gained, b + 1)
                    pool.tensor_tensor(h[:, b, :], h[:, b, :], k.rstd[:], ALU.mult).then_inc(normed, 1)

            @block.vector
            def _(dve):
                dve.wait_ge(counted, 1)
                dve.reciprocal(inv[:], count[:]).then_inc(inverted, 1)
                dve.wait_ge(inverted, 1)
                for b in range(KT):
                    w = POOL_WINDOWS[b // 2]
                    dve.wait_ge(normed, b + 1)
                    dve.tensor_tensor_scan(sums[:, b, :], one, h[:, b, :], 0.0, ALU.mult, ALU.add).then_inc(summed, 1)
                    dve.wait_ge(summed, b + 1)
                    dve.tensor_tensor(diff[:, b, w:T], sums[:, b, w:T], sums[:, b, 0:T - w], ALU.subtract)
                    dve.tensor_tensor(diff[:, b, 0:w], sums[:, b, 0:w], inv[:, 0:w], ALU.mult).then_inc(apart, 1)
                    dve.wait_ge(apart, b + 1)
                    dve.tensor_tensor(pooled[:, b, 0:w], diff[:, b, 0:w], h[:, b, 0:w], ALU.subtract)
                    dve.scalar_tensor_tensor(pooled[:, b, w:T], diff[:, b, w:T], 1.0 / w, h[:, b, w:T], ALU.mult, ALU.subtract)\
                        .then_inc(pooled_s, 1)
                    if b:
                        x.low_of(dve, b - 1)
                x.low_of(dve, KT - 1)
                for g in range(groups):
                    k.split_low(dve, g0, 0, g + 2)

            @block.tensor
            def _(pe):
                for g in range(groups):
                    w_hi, w_lo = k.panel(pe, g0, 0, g, 2, PW)
                    for m in range(2):
                        b, at = 2 * g + m, slice(m * P, (m + 1) * P)
                        if b >= banks:
                            pe.wait_ge(scaled, b - banks + 1)
                        for kt in range(2):
                            x.ready(pe, 2 * g + kt)
                            last = product(pe, ps[:, b % banks, :], (w_hi[:, kt, at], w_lo[:, kt, at]), x.halves(2 * g + kt), kt == 0, kt == 1)
                        last.then_inc(k.panel_used if m else first, 1)
                    for b in (2 * g - 2, 2 * g - 1) if g else ():
                        rows.count(pe, b)
                for b in (KT - 2, KT - 1):
                    rows.count(pe, b)

            @block.scalar
            def _(act):
                for b in range(KT):
                    act.mul(h[:, b, :], k.xT[:, b, :], norm_gain[:, b:b + 1]).then_inc(gained, 1)
                for b in range(KT):
                    act.wait_ge(pooled_s, b + 1)
                    x.high_of(act, b)
                for b in range(KT):
                    if b % 2:
                        act.wait_ge(k.panel_used, g0 + b // 2 + 1)
                        k.split_high(act, g0, 0, b // 2 + 2)
                    else:
                        act.wait_ge(first, b // 2 + 1)
                    act.mul(out[:, b, :], ps[:, b % banks, :], gain[:, b:b + 1]).then_inc(scaled, 1)
                    act.wait_ge(scaled, b + 1)
                    rows.square(act, b, out[:, b, :])
                rows.root(act)


def second_block(k):
    def gain(layer, n):
        at = ROW_B["norm_g_2"] + (4 * layer + n) * KT
        return k.col_b[:, at:at + KT]

    for layer in range(2):
        with Phase(k, f"mixer{layer}") as f:
            mixed = f.sb("mixed", [P, KT, T])
            if layer == 0:
                with Phase(k, "attn_all") as g:
                    a = Attention(g)
                    a.add_tables(g)
                    with Phase(k, "compress") as c:
                        a.add_early(c)
                        w1, w2 = a.forget[:].rearrange("p h (i c) -> p (h i) c", c=HD).rearrange("p (v i) c -> p v i c", v=2), c.sb("w2", [P, 2, HD])
                        compress = w1, w2, c.sem("landed"), c.sem("doubled")
                        attn_project(k, a, gain(layer, 0), compress, mixed)
                        attn_prepare(k, a, mixed, compress)
                    attention(k, a, mixed)
                add_projection(k, "attn_out", mixed, (KT,), out=mixed, split=True)
            else:
                pool_mixer(k, mixed, gain(layer, 0))
            take_in(k, f"mixer{layer}_out", mixed, gain(layer, 1))
        with Phase(k, f"glu{layer}") as f:
            hidden = Hidden(f, HK)
            swiglu_in(k, layer, gain(layer, 2), hidden)
            mixed = f.sb("out", [P, KT, T])
            add_projection(k, f"down{layer}", hidden, DOWN_CHUNKS, out=mixed)
            take_in(k, f"glu{layer}_out", mixed, gain(layer, 3), stats=layer == 0)


def store(k):
    nc, ps = k.nc, k.ps
    with Phase(k, "store") as f:
        y = f.sb("y", [P, TT, D])
        turned, copied, stored = f.sem("turned"), f.sem("copied"), f.sem("stored")
        with nc.Block() as block:

            @block.tensor
            def _(pe):
                for t in range(TT):
                    for kt in range(KT):
                        last = pe.transpose(ps[:, 2 * t + kt // 4, (kt % 4) * P:(kt % 4 + 1) * P], k.xT[:, kt, t * P:(t + 1) * P], k.ident[:])
                    last.then_inc(turned, 1)

            @block.scalar
            def _(act):
                for t in range(TT):
                    act.wait_ge(turned, t + 1)
                    act.copy(y[:, t, 0:BANK], ps[:, 2 * t, :]).then_inc(copied, 1)

            @block.vector
            def _(dve):
                for t in range(TT):
                    dve.wait_ge(turned, t + 1)
                    dve.tensor_copy(y[:, t, BANK:D], ps[:, 2 * t + 1, :]).then_inc(stored, 1)

            @block.sync
            def _(sp):
                done = k.output_stored
                for t in range(TT):
                    sp.wait_ge(copied, t + 1)
                    sp.wait_ge(stored, t + 1)
                    sp.dma_start(k.out[0, t * P:(t + 1) * P, :], y[:, t, :]).then_inc(done, 16)
                sp.wait_ge(done, 16 * TT)


def build(nc, ins, out):
    with ExitStack() as ctx:
        k = Kernel(nc, ctx, ins, out)
        k.output_stored = ctx.enter_context(nc.semaphore("output_stored"))
        with Phase(k, "first_block") as first:
            k.add_first_block(first)
            with Phase(k, "memory") as f:
                mem_T = f.sb("mem_T", [P, KT, M])
                setup(k, mem_T)
                row_stats(k, "mem_stats", mem_T, M)
                memory_kv(k, mem_T, k.col_a[:, ROW_A["mem_norm_g"]:ROW_A["mem_norm_g"] + KT])
            row_stats(k, "x_stats", k.xT)
            rwkv_block(k)
        second_block(k)
        store(k)


_UNUSED = ("df_in", "df_q_norm_g", "df_k_norm_g", "df_lq1", "df_lk1", "df_lq2", "df_lk2", "df_subln_g")


def kernel(**inputs):
    import numpy as np
    import concourse.bacc as bacc
    from concourse.bass_utils import run_bass_kernel_spmd

    nc = bacc.Bacc("TRN2", target_bir_lowering=False, num_devices=1)
    arrays, ins = {}, {}
    for name, value in inputs.items():
        if name in _UNUSED:
            continue
        arrays[f"in_{name}"] = np.ascontiguousarray(value)
        ins[name] = nc.dram_tensor(f"in_{name}", arrays[f"in_{name}"].shape, F32, kind="ExternalInput").ap()
    out = nc.dram_tensor("out_x", (1, T, D), F32, kind="ExternalOutput").ap()
    build(nc, ins, out)
    result = run_bass_kernel_spmd(nc, [arrays], core_ids=[0])
    return result.results[0]["out_x"]
```
